# Optimizing a Trainium2 kernel written in Bass

```python
import jax, jax.numpy as jnp
from jax import lax
import numpy as np
import math
import jax
import jax.numpy as jnp

D_MODEL = 1024
BATCH = 1
SEQ = 256
DEPTH = 1

CTX_LEN = 256
GRID_W = 64
EXPAND = 2
D_INNER = EXPAND * D_MODEL
D_FOURIER = D_INNER // 4
FOURIER_GROUP = 64
N_FOURIER_GROUPS = D_FOURIER // FOURIER_GROUP
D_SSD = D_INNER - D_FOURIER
SSD_HEAD_DIM = 64
N_SSD_HEADS = D_SSD // SSD_HEAD_DIM
N_BC_GROUPS = 4
HEADS_PER_GROUP = N_SSD_HEADS // N_BC_GROUPS
D_STATE = 128
CONV_K = 3
CONV_CH = D_SSD + 2 * N_BC_GROUPS * D_STATE
CHUNK = 128
D_PROJ = 2 * D_FOURIER + D_SSD + CONV_CH + 2 * N_SSD_HEADS
PROJ_SPLITS = (D_FOURIER, 2 * D_FOURIER, 2 * D_FOURIER + D_SSD, 2 * D_FOURIER + D_SSD + CONV_CH)
EPS = 1e-6


def rmsnorm(x, w):
    xf = x.astype(jnp.float32)
    xf = xf * lax.rsqrt(jnp.mean(xf * xf, axis=-1, keepdims=True) + EPS)
    return xf.astype(x.dtype) * w

def segsum(a):
    cum = jnp.cumsum(a, axis=-1)
    diff = cum[..., :, None] - cum[..., None, :]
    t = a.shape[-1]
    mask = jnp.tril(jnp.ones((t, t), dtype=bool))
    return jnp.where(mask, diff, -jnp.inf)

def ssd_chunked(x, dt, A, B, C, h0):
    bsz, length, g, r, p = x.shape
    n = B.shape[-1]
    nc = length // CHUNK
    xc = (x * dt[..., None]).reshape(bsz, nc, CHUNK, g, r, p)
    bc = B.reshape(bsz, nc, CHUNK, g, n)
    cc = C.reshape(bsz, nc, CHUNK, g, n)
    a = (dt * A).reshape(bsz, nc, CHUNK, g, r).transpose(0, 3, 4, 1, 2)
    a_cum = jnp.cumsum(a, axis=-1)
    lmat = jnp.exp(segsum(a))
    cb = jnp.einsum('bclgn,bcsgn->bgcls', cc, bc)
    y_diag = jnp.einsum('bgcls,bgrcls,bcsgrp->bclgrp', cb, lmat, xc)
    decay_states = jnp.exp(a_cum[..., -1:] - a_cum)
    states = jnp.einsum('bcsgn,bgrcs,bcsgrp->bcgrpn', bc, decay_states, xc)
    states = jnp.concatenate([h0[:, None], states], axis=1)
    chunk_a = jnp.pad(a_cum[..., -1], ((0, 0), (0, 0), (0, 0), (1, 0)))
    decay_chunk = jnp.exp(segsum(chunk_a))
    new_states = jnp.einsum('bgrzc,bcgrpn->bzgrpn', decay_chunk, states)
    prev_states, h_final = new_states[:, :-1], new_states[:, -1]
    y_off = jnp.einsum('bclgn,bcgrpn,bgrcl->bclgrp', cc, prev_states, jnp.exp(a_cum))
    y = (y_diag + y_off).reshape(bsz, length, g, r, p)
    return y, h_final

def depthwise_conv_grid(u, w, bias, rows, cols):
    bsz, length, ch = u.shape
    img = u.reshape(bsz, rows, cols, ch)
    out = lax.conv_general_dilated(img, w[:, :, None, :], window_strides=(1, 1), padding='SAME',
                                   dimension_numbers=('NHWC', 'HWIO', 'NHWC'), feature_group_count=ch)
    return jax.nn.silu(out.reshape(bsz, length, ch) + bias)

def fourier_mixer(u, zf, w_f, b_f):
    bsz, length, _ = u.shape
    uf = u.astype(jnp.float32).reshape(bsz, length, N_FOURIER_GROUPS, FOURIER_GROUP)
    mixed = jnp.fft.fft2(uf, axes=(1, 3), norm='ortho').real.reshape(bsz, length, D_FOURIER)
    mixed = mixed.astype(u.dtype) @ w_f + b_f
    return mixed * jax.nn.silu(zf)

def ssd_mixer(xbc, dt_raw, zs, dt_bias, a_log, d_skip, norm_w, h0_f, h0_b):
    bsz, length, _ = xbc.shape
    f32 = jnp.float32
    g, r, p, n = N_BC_GROUPS, HEADS_PER_GROUP, SSD_HEAD_DIM, D_STATE
    xs, bm, cm = jnp.split(xbc.astype(f32), [D_SSD, D_SSD + g * n], axis=-1)
    xs = xs.reshape(bsz, length, g, r, p)
    bm = bm.reshape(bsz, length, g, n)
    cm = cm.reshape(bsz, length, g, n)
    dt = jax.nn.softplus(dt_raw.astype(f32).reshape(bsz, length, 2, N_SSD_HEADS) + dt_bias.astype(f32))
    A = -jnp.exp(a_log.astype(f32)).reshape(2, g, r)
    dt_f = dt[:, :, 0].reshape(bsz, length, g, r)
    dt_b = dt[:, :, 1].reshape(bsz, length, g, r)
    flip = lambda t: jnp.flip(t, axis=1)
    y_f, h_f = ssd_chunked(xs, dt_f, A[0], bm, cm, h0_f)
    y_b, h_b = ssd_chunked(flip(xs), flip(dt_b), A[1], flip(bm), flip(cm), h0_b)
    y = y_f + flip(y_b) + d_skip.astype(f32).reshape(g, r)[:, :, None] * xs
    gated = y.reshape(bsz, length, g, r * p) * jax.nn.silu(zs.astype(f32)).reshape(bsz, length, g, r * p)
    gated = gated * lax.rsqrt(jnp.mean(gated * gated, axis=-1, keepdims=True) + EPS)
    out = gated.reshape(bsz, length, D_SSD).astype(zs.dtype) * norm_w
    return out, h_f, h_b

def token_mixer(h, rows, cols, w_in, conv_w, conv_b, dt_bias, a_log, d_skip, ssd_norm_w,
                w_fourier, b_fourier, h0_f, h0_b):
    u, zf, zs, xbc, dt_raw = jnp.split(h @ w_in, PROJ_SPLITS, axis=-1)
    four = fourier_mixer(u, zf, w_fourier, b_fourier)
    xbc = depthwise_conv_grid(xbc, conv_w, conv_b, rows, cols)
    ssd, h_f, h_b = ssd_mixer(xbc, dt_raw, zs, dt_bias, a_log, d_skip, ssd_norm_w, h0_f, h0_b)
    return jnp.concatenate([four, ssd], axis=-1), h_f, h_b

def first_inputs(seed: int = 0) -> dict:
    key = jax.random.key(seed)
    ks = jax.random.split(key, 20)
    f32 = jnp.float32
    nrm = lambda k, shape, s: jax.random.normal(k, shape, f32) * s
    dt0 = jnp.exp(jax.random.uniform(ks[9], (DEPTH, 2, N_SSD_HEADS), f32,
                                     minval=np.log(1e-3), maxval=np.log(1e-1)))
    return {
        "x": nrm(ks[0], (BATCH, SEQ, D_MODEL), 1.0),
        "c": nrm(ks[1], (BATCH, D_MODEL), 1.0),
        "ctx": nrm(ks[2], (BATCH, CTX_LEN, D_MODEL), 1.0),
        "c_ctx": nrm(ks[3], (D_MODEL,), 1.0),
        "norm_w": 1.0 + nrm(ks[4], (DEPTH, D_MODEL), 0.05),
        "w_ada": nrm(ks[5], (DEPTH, D_MODEL, 3 * D_MODEL), 0.5 * D_MODEL ** -0.5),
        "b_ada": nrm(ks[6], (DEPTH, 3 * D_MODEL), 0.02),
        "w_in": nrm(ks[7], (DEPTH, D_MODEL, D_PROJ), D_MODEL ** -0.5),
        "conv_w": nrm(ks[8], (DEPTH, CONV_K, CONV_K, CONV_CH), 1.0 / CONV_K),
        "conv_b": nrm(ks[10], (DEPTH, CONV_CH), 0.02),
        "dt_bias": dt0 + jnp.log(-jnp.expm1(-dt0)),
        "a_log": jnp.log(jax.random.uniform(ks[11], (DEPTH, 2, N_SSD_HEADS), f32, minval=1.0, maxval=16.0)),
        "d_skip": 1.0 + nrm(ks[12], (DEPTH, N_SSD_HEADS), 0.1),
        "ssd_norm_w": 1.0 + nrm(ks[13], (DEPTH, D_SSD), 0.05),
        "w_fourier": nrm(ks[14], (DEPTH, D_FOURIER, D_FOURIER), D_FOURIER ** -0.5),
        "b_fourier": nrm(ks[15], (DEPTH, D_FOURIER), 0.02),
        "w_out": nrm(ks[16], (DEPTH, D_INNER, D_MODEL), D_INNER ** -0.5),
        "final_norm_w": 1.0 + nrm(ks[17], (D_MODEL,), 0.05),
    }

def first_block(x, c, ctx, c_ctx, norm_w, w_ada, b_ada, w_in, conv_w, conv_b, dt_bias, a_log, d_skip,
              ssd_norm_w, w_fourier, b_fourier, w_out, final_norm_w):
    bsz, seq_len, _ = x.shape
    ctx_len = ctx.shape[1]
    rows = seq_len // GRID_W
    zeros_state = jnp.zeros((bsz, N_BC_GROUPS, HEADS_PER_GROUP, SSD_HEAD_DIM, D_STATE), jnp.float32)
    silu_c = jax.nn.silu(c)
    silu_cc = jax.nn.silu(c_ctx)
    for i in range(DEPTH):
        mod = silu_c @ w_ada[i] + b_ada[i]
        shift, scale, gate = jnp.split(mod, 3, axis=-1)
        mod_c = silu_cc @ w_ada[i] + b_ada[i]
        shift_c, scale_c, gate_c = jnp.split(mod_c, 3, axis=-1)
        layer = (w_in[i], conv_w[i], conv_b[i], dt_bias[i], a_log[i], d_skip[i], ssd_norm_w[i],
                 w_fourier[i], b_fourier[i])
        hc = rmsnorm(ctx, norm_w[i]) * (1.0 + scale_c) + shift_c
        ctx_mix, h_f, h_b = token_mixer(hc, 1, ctx_len, *layer, zeros_state, zeros_state)
        hx = rmsnorm(x, norm_w[i]) * (1.0 + scale[:, None]) + shift[:, None]
        x_mix, _, _ = token_mixer(hx, rows, GRID_W, *layer, h_f, h_b)
        x = x + gate[:, None] * (x_mix @ w_out[i])
        if i < DEPTH - 1:
            ctx = ctx + gate_c * (ctx_mix @ w_out[i])
    return rmsnorm(x, final_norm_w)


DEPTH_2 = 2

ATTN_BLOCK = 128
ROPE_BASE = 10000.0
RMS_EPS = 1e-6

DIFF_HEADS = 4
DIFF_HEAD_DIM = 64
NA_HEADS = 8
NA_HEAD_DIM = 64
NA_WIN_ROWS_MAX = 8
NA_WIN_COLS = 16
MLA_HEADS = 8
MLA_Q_RANK = 256
MLA_KV_RANK = 128
MLA_NOPE_DIM = 64
MLA_ROPE_DIM = 32
MLA_V_DIM = 64
RET_HEADS = 4
RET_QK_DIM = 64
RET_V_DIM = 128
RET_CHUNK = 128
N_EXPERTS = 16
EC_CAPACITY_FACTOR = 2
EXPERT_FF = 1024

DIFF_WIDTH = DIFF_HEADS * 2 * DIFF_HEAD_DIM
NA_WIDTH = NA_HEADS * NA_HEAD_DIM
EVEN_IN = 3 * DIFF_WIDTH + 3 * NA_WIDTH
EVEN_OUT = DIFF_WIDTH + NA_WIDTH
MLA_QK_DIM = MLA_NOPE_DIM + MLA_ROPE_DIM
MLA_WIDTH = MLA_HEADS * MLA_V_DIM
RET_QK_WIDTH = RET_HEADS * RET_QK_DIM
RET_V_WIDTH = RET_HEADS * RET_V_DIM
ODD_IN = MLA_Q_RANK + MLA_KV_RANK + MLA_ROPE_DIM + 2 * RET_QK_WIDTH + 2 * RET_V_WIDTH
ODD_OUT = MLA_WIDTH + RET_V_WIDTH
N_EVEN = (DEPTH_2 + 1) // 2
N_ODD = DEPTH_2 // 2


def rms_norm(x, gain=None):
    xf = x.astype(jnp.float32)
    y = xf * lax.rsqrt(jnp.mean(xf * xf, axis=-1, keepdims=True) + RMS_EPS)
    if gain is not None:
        y = y * gain.astype(jnp.float32)
    return y.astype(x.dtype)

def split_cols(p, widths):
    idx, acc = [], 0
    for w in widths[:-1]:
        acc += w
        idx.append(acc)
    return jnp.split(p, idx, axis=-1)

def axial_angles(n_tokens, rot_dim):
    t = jnp.arange(n_tokens)
    rows = (t // GRID_W).astype(jnp.float32)
    cols = (t % GRID_W).astype(jnp.float32)
    m = rot_dim // 4
    freqs = ROPE_BASE ** (-jnp.arange(m, dtype=jnp.float32) / m)
    return rows[:, None] * freqs, cols[:, None] * freqs

def rope_half(x, ang):
    a, b = jnp.split(x, 2, axis=-1)
    cos = jnp.cos(ang).astype(x.dtype)
    sin = jnp.sin(ang).astype(x.dtype)
    return jnp.concatenate([a * cos - b * sin, b * cos + a * sin], axis=-1)

def apply_axial_rope(x, ang_r, ang_c):
    shape = ang_r.shape[:1] + (1,) * (x.ndim - 3) + ang_r.shape[1:]
    xr, xc = jnp.split(x, 2, axis=-1)
    return jnp.concatenate([rope_half(xr, ang_r.reshape(shape)), rope_half(xc, ang_c.reshape(shape))], axis=-1)

def sweep_query_blocks(fn, queries):
    B, L = queries[0].shape[:2]
    nb = L // ATTN_BLOCK
    blocks = tuple(jnp.moveaxis(q.reshape((B, nb, ATTN_BLOCK) + q.shape[2:]), 1, 0) for q in queries)
    out = jnp.moveaxis(lax.map(fn, blocks), 0, 1)
    return out.reshape((B, L) + out.shape[3:])

def softmax_attention(q, k, v, q_rope=None, k_rope=None):
    d = q.shape[-1] + (0 if q_rope is None else q_rope.shape[-1])
    scale = d ** -0.5

    def block(qs):
        s = jnp.einsum('bqhd,bkhd->bhqk', qs[0], k).astype(jnp.float32)
        if q_rope is not None:
            s = s + jnp.einsum('bqhr,bkr->bhqk', qs[1], k_rope).astype(jnp.float32)
        p = jax.nn.softmax(s * scale, axis=-1).astype(v.dtype)
        return jnp.einsum('bhqk,bkhe->bqhe', p, v)

    queries = (q,) if q_rope is None else (q, q_rope)
    return sweep_query_blocks(block, queries)

def diff_attention(q, k, v, lam):
    scale = DIFF_HEAD_DIM ** -0.5

    def block(qs):
        s = jnp.einsum('bqhcd,bkhcd->bhcqk', qs[0], k).astype(jnp.float32) * scale
        p = jax.nn.softmax(s, axis=-1)
        a = p[:, :, 0] - lam * p[:, :, 1]
        return jnp.einsum('bhqk,bkhe->bqhe', a.astype(v.dtype), v)

    return sweep_query_blocks(block, (q,))

def neighbourhood_attention(q, k, v, k_ctx, v_ctx, rpb):
    B, L, H, d = q.shape
    rows = L // GRID_W
    wr = min(NA_WIN_ROWS_MAX, rows)
    wc = NA_WIN_COLS
    scale = d ** -0.5
    qg = q.reshape(B, rows, GRID_W, H, d)
    kg = k.reshape(B, rows, GRID_W, H, d)
    vg = v.reshape(B, rows, GRID_W, H, d)
    cols = jnp.arange(GRID_W)
    col_start = jnp.clip(cols - wc // 2, 0, GRID_W - wc)
    col_idx = col_start[:, None] + jnp.arange(wc)[None, :]
    col_bias = rpb[:, :, col_idx - cols[:, None] + (NA_WIN_COLS - 1)]

    def row_block(r):
        rs = jnp.clip(r - wr // 2, 0, rows - wr)
        q_row = lax.dynamic_index_in_dim(qg, r, axis=1, keepdims=False)
        k_win = lax.dynamic_slice_in_dim(kg, rs, wr, axis=1)[:, :, col_idx]
        v_win = lax.dynamic_slice_in_dim(vg, rs, wr, axis=1)[:, :, col_idx]
        row_off = rs + jnp.arange(wr) - r + (NA_WIN_ROWS_MAX - 1)
        bias = jnp.transpose(jnp.take(col_bias, row_off, axis=1), (0, 2, 1, 3))
        s_loc = jnp.einsum('bqhd,brqwhd->bhqrw', q_row, k_win).astype(jnp.float32) * scale + bias[None].astype(jnp.float32)
        s_ctx = jnp.einsum('bqhd,bkhd->bhqk', q_row, k_ctx).astype(jnp.float32) * scale
        s = jnp.concatenate([s_loc.reshape(B, H, GRID_W, wr * wc), s_ctx], axis=-1)
        p = jax.nn.softmax(s, axis=-1).astype(v.dtype)
        p_loc = p[..., :wr * wc].reshape(B, H, GRID_W, wr, wc)
        p_ctx = p[..., wr * wc:]
        return jnp.einsum('bhqrw,brqwhd->bqhd', p_loc, v_win) + jnp.einsum('bhqk,bkhd->bqhd', p_ctx, v_ctx)

    out = lax.map(row_block, jnp.arange(rows))
    return jnp.moveaxis(out, 0, 1).reshape(B, L, H, d)

def retention_chunkwise(q, k, v, log_gamma, s0, include_diag):
    B, H, L, _ = q.shape
    dv = v.shape[-1]
    C = RET_CHUNK
    n = L // C
    pos = jnp.arange(C, dtype=jnp.float32)
    rel = pos[:, None] - pos[None, :]
    mask = (rel >= 0) if include_diag else (rel > 0)
    decay_in = jnp.where(mask, jnp.exp(log_gamma[:, None, None] * jnp.where(mask, rel, 0.0)), 0.0)
    decay_q = jnp.exp(log_gamma[:, None] * (pos + 1.0))[..., None]
    decay_k = jnp.exp(log_gamma[:, None] * (C - 1.0 - pos))[..., None]
    decay_chunk = jnp.exp(log_gamma * C)[:, None, None]

    def to_chunks(t):
        return jnp.moveaxis(t.reshape(B, H, n, C, t.shape[-1]), 2, 0)

    def step(state, blk):
        qb, kb, vb = blk
        inner = jnp.einsum('bhij,bhjv->bhiv', jnp.einsum('bhid,bhjd->bhij', qb, kb) * decay_in, vb)
        cross = jnp.einsum('bhid,bhdv->bhiv', qb * decay_q, state)
        new_state = decay_chunk * state + jnp.einsum('bhjd,bhjv->bhdv', kb * decay_k, vb)
        return new_state, inner + cross

    _, out = lax.scan(step, s0, (to_chunks(q), to_chunks(k), to_chunks(v)))
    return jnp.moveaxis(out, 0, 2).reshape(B, H, L, dv)

def retention_final_state(k, v, log_gamma):
    L = k.shape[2]
    w = jnp.exp(log_gamma[:, None] * (L - 1.0 - jnp.arange(L, dtype=jnp.float32)))
    return jnp.einsum('hl,bhld,bhlv->bhdv', w, k, v)

def retention_bidir(q, k, v, q_c, k_c, v_c, decay_logit, need_ctx):
    def to_bhld(t):
        return jnp.moveaxis(t, 2, 1).astype(jnp.float32)

    def flip(t):
        return jnp.flip(t, axis=2)

    kscale = RET_QK_DIM ** -0.5
    q, v, q_c, v_c = to_bhld(q), to_bhld(v), to_bhld(q_c), to_bhld(v_c)
    k, k_c = to_bhld(k) * kscale, to_bhld(k_c) * kscale
    log_g = jax.nn.log_sigmoid(decay_logit.astype(jnp.float32))
    lg_f, lg_b = log_g[0], log_g[1]
    s_f = retention_final_state(k_c, v_c, lg_f)
    s_b = retention_final_state(flip(k_c), flip(v_c), lg_b)
    out = retention_chunkwise(q, k, v, lg_f, s_f, True) + flip(retention_chunkwise(flip(q), flip(k), flip(v), lg_b, s_b, False))
    out = jnp.moveaxis(out, 1, 2)
    if not need_ctx:
        return out, None
    zero = jnp.zeros_like(s_f)
    out_c = retention_chunkwise(q_c, k_c, v_c, lg_f, zero, True) + flip(retention_chunkwise(flip(q_c), flip(k_c), flip(v_c), lg_b, zero, False))
    return out, jnp.moveaxis(out_c, 1, 2)

def even_layer(h, hc, w_in, w_out, lam_params, subln, rpb, layer_idx, need_ctx):
    B, L, _ = h.shape
    Lc = hc.shape[1]
    widths = (DIFF_WIDTH,) * 3 + (NA_WIDTH,) * 3
    aq, ak, av, nq, nk, nv = split_cols(h @ w_in, widths)
    aqc, akc, avc, nqc, nkc, nvc = split_cols(hc @ w_in, widths)

    def dh(t):
        return t.reshape(t.shape[:2] + (DIFF_HEADS, 2, DIFF_HEAD_DIM))

    def dvh(t):
        return t.reshape(t.shape[:2] + (DIFF_HEADS, 2 * DIFF_HEAD_DIM))

    def nh(t):
        return t.reshape(t.shape[:2] + (NA_HEADS, NA_HEAD_DIM))

    ang_r, ang_c = axial_angles(L, DIFF_HEAD_DIM)
    lam_init = 0.8 - 0.6 * math.exp(-0.3 * layer_idx)
    lq1, lk1, lq2, lk2 = lam_params
    lam = jnp.exp(jnp.sum(lq1 * lk1)) - jnp.exp(jnp.sum(lq2 * lk2)) + lam_init

    k_all = jnp.concatenate([apply_axial_rope(dh(ak), ang_r, ang_c), dh(akc)], axis=1)
    v_all = jnp.concatenate([dvh(av), dvh(avc)], axis=1)
    a = diff_attention(apply_axial_rope(dh(aq), ang_r, ang_c), k_all, v_all, lam)
    a = (rms_norm(a, subln) * (1.0 - lam_init)).reshape(B, L, DIFF_WIDTH)
    nb = neighbourhood_attention(nh(nq), nh(nk), nh(nv), nh(nkc), nh(nvc), rpb).reshape(B, L, NA_WIDTH)
    y = jnp.concatenate([a, nb], axis=-1) @ w_out
    if not need_ctx:
        return y, None
    ac = diff_attention(dh(aqc), dh(akc), dvh(avc), lam)
    ac = (rms_norm(ac, subln) * (1.0 - lam_init)).reshape(B, Lc, DIFF_WIDTH)
    nc = softmax_attention(nh(nqc), nh(nkc), nh(nvc)).reshape(B, Lc, NA_WIDTH)
    yc = jnp.concatenate([ac, nc], axis=-1) @ w_out
    return y, yc

def odd_layer(h, hc, w_in, w_out, q_norm, w_uq, kv_norm, w_ukv, decay_logit, need_ctx):
    B, L, _ = h.shape
    Lc = hc.shape[1]
    widths = (MLA_Q_RANK, MLA_KV_RANK, MLA_ROPE_DIM, RET_QK_WIDTH, RET_QK_WIDTH, RET_V_WIDTH, RET_V_WIDTH)
    cq, ckv, kr, rq, rk, rv, rg = split_cols(h @ w_in, widths)
    cqc, ckvc, krc, rqc, rkc, rvc, rgc = split_cols(hc @ w_in, widths)

    def mla_up(cq_, ckv_):
        n = cq_.shape[:2]
        qh = (rms_norm(cq_, q_norm) @ w_uq).reshape(n + (MLA_HEADS, MLA_QK_DIM))
        kvh = (rms_norm(ckv_, kv_norm) @ w_ukv).reshape(n + (MLA_HEADS, MLA_NOPE_DIM + MLA_V_DIM))
        return qh[..., :MLA_NOPE_DIM], qh[..., MLA_NOPE_DIM:], kvh[..., :MLA_NOPE_DIM], kvh[..., MLA_NOPE_DIM:]

    def rh(t, d):
        return t.reshape(t.shape[:2] + (RET_HEADS, d))

    qn, qr, kn, vm = mla_up(cq, ckv)
    qnc, qrc, knc, vmc = mla_up(cqc, ckvc)
    ang_r, ang_c = axial_angles(L, MLA_ROPE_DIM)
    k_rope_all = jnp.concatenate([apply_axial_rope(kr, ang_r, ang_c), krc], axis=1)
    m = softmax_attention(qn, jnp.concatenate([kn, knc], axis=1), jnp.concatenate([vm, vmc], axis=1),
                          apply_axial_rope(qr, ang_r, ang_c), k_rope_all).reshape(B, L, MLA_WIDTH)
    r, r_c = retention_bidir(rh(rq, RET_QK_DIM), rh(rk, RET_QK_DIM), rh(rv, RET_V_DIM),
                             rh(rqc, RET_QK_DIM), rh(rkc, RET_QK_DIM), rh(rvc, RET_V_DIM), decay_logit, need_ctx)
    r = rms_norm(r.astype(h.dtype)).reshape(B, L, RET_V_WIDTH) * jax.nn.silu(rg)
    y = jnp.concatenate([m, r], axis=-1) @ w_out
    if not need_ctx:
        return y, None
    mc = softmax_attention(qnc, knc, vmc, qrc, krc).reshape(B, Lc, MLA_WIDTH)
    rc = rms_norm(r_c.astype(hc.dtype)).reshape(B, Lc, RET_V_WIDTH) * jax.nn.silu(rgc)
    yc = jnp.concatenate([mc, rc], axis=-1) @ w_out
    return y, yc

def expert_choice_ffn(h, w_router, w1, w3, w2):
    B, T, _ = h.shape
    cap = (EC_CAPACITY_FACTOR * T) // N_EXPERTS
    aff = jax.nn.softmax((h @ w_router).astype(jnp.float32), axis=-1)
    gate, idx = lax.top_k(jnp.swapaxes(aff, 1, 2), cap)
    bidx = jnp.arange(B)[:, None, None]
    xe = h[bidx, idx]
    hid = jax.nn.silu(jnp.einsum('becd,edf->becf', xe, w1)) * jnp.einsum('becd,edf->becf', xe, w3)
    ye = jnp.einsum('becf,efd->becd', hid, w2) * gate[..., None].astype(h.dtype)
    return jnp.zeros_like(h).at[bidx, idx].add(ye)

def second_inputs(seed: int = 0) -> dict:
    key = jax.random.key(seed)
    ks = jax.random.split(key, 25)
    f32 = jnp.float32

    def nrm(k, shape, scale):
        return jax.random.normal(k, shape, f32) * scale

    def gain(k, shape):
        return 1.0 + 0.02 * jax.random.normal(k, shape, f32)

    decay_init = jnp.log(2.0 ** (5.0 + jnp.arange(RET_HEADS, dtype=f32)) - 1.0)
    return {
        'x': nrm(ks[0], (BATCH, SEQ, D_MODEL), 1.0),
        'c': nrm(ks[1], (BATCH, D_MODEL), 1.0),
        'ctx': nrm(ks[2], (BATCH, CTX_LEN, D_MODEL), 1.0),
        'c_ctx': nrm(ks[3], (D_MODEL,), 1.0),
        'ada_w': nrm(ks[4], (DEPTH_2, D_MODEL, 6 * D_MODEL), 0.5 * D_MODEL ** -0.5),
        'ada_b': nrm(ks[5], (DEPTH_2, 6 * D_MODEL), 0.01),
        'norm_mix': gain(ks[6], (DEPTH_2, D_MODEL)),
        'norm_ffn': gain(ks[7], (DEPTH_2, D_MODEL)),
        'final_norm': gain(ks[8], (D_MODEL,)),
        'even_w_in': nrm(ks[9], (N_EVEN, D_MODEL, EVEN_IN), D_MODEL ** -0.5),
        'even_w_out': nrm(ks[10], (N_EVEN, EVEN_OUT, D_MODEL), EVEN_OUT ** -0.5),
        'diff_lambda': nrm(ks[11], (N_EVEN, 4, DIFF_HEAD_DIM), 0.1),
        'diff_subln': gain(ks[12], (N_EVEN, 2 * DIFF_HEAD_DIM)),
        'na_rpb': nrm(ks[13], (N_EVEN, NA_HEADS, 2 * NA_WIN_ROWS_MAX - 1, 2 * NA_WIN_COLS - 1), 0.02),
        'odd_w_in': nrm(ks[14], (N_ODD, D_MODEL, ODD_IN), D_MODEL ** -0.5),
        'odd_w_out': nrm(ks[15], (N_ODD, ODD_OUT, D_MODEL), ODD_OUT ** -0.5),
        'mla_q_norm': gain(ks[16], (N_ODD, MLA_Q_RANK)),
        'mla_w_uq': nrm(ks[17], (N_ODD, MLA_Q_RANK, MLA_HEADS * MLA_QK_DIM), MLA_Q_RANK ** -0.5),
        'mla_kv_norm': gain(ks[18], (N_ODD, MLA_KV_RANK)),
        'mla_w_ukv': nrm(ks[19], (N_ODD, MLA_KV_RANK, MLA_HEADS * (MLA_NOPE_DIM + MLA_V_DIM)), MLA_KV_RANK ** -0.5),
        'ret_decay_logit': jnp.broadcast_to(decay_init, (N_ODD, 2, RET_HEADS)) + nrm(ks[20], (N_ODD, 2, RET_HEADS), 0.05),
        'moe_router': nrm(ks[21], (DEPTH_2, D_MODEL, N_EXPERTS), D_MODEL ** -0.5),
        'moe_w1': nrm(ks[22], (DEPTH_2, N_EXPERTS, D_MODEL, EXPERT_FF), D_MODEL ** -0.5),
        'moe_w3': nrm(ks[23], (DEPTH_2, N_EXPERTS, D_MODEL, EXPERT_FF), D_MODEL ** -0.5),
        'moe_w2': nrm(ks[24], (DEPTH_2, N_EXPERTS, EXPERT_FF, D_MODEL), EXPERT_FF ** -0.5),
    }

def second_block(x, c, ctx, c_ctx, ada_w, ada_b, norm_mix, norm_ffn, final_norm, even_w_in, even_w_out,
              diff_lambda, diff_subln, na_rpb, odd_w_in, odd_w_out, mla_q_norm, mla_w_uq, mla_kv_norm,
              mla_w_ukv, ret_decay_logit, moe_router, moe_w1, moe_w3, moe_w2):
    xc = ctx
    silu_c = jax.nn.silu(c)
    silu_cc = jax.nn.silu(c_ctx)
    for l in range(DEPTH_2):
        need_ctx = l < DEPTH_2 - 1
        mods = jnp.split(silu_c @ ada_w[l] + ada_b[l], 6, axis=-1)
        sh1, sc1, g1, sh2, sc2, g2 = [m[:, None, :] for m in mods]
        sh1c, sc1c, g1c, sh2c, sc2c, g2c = jnp.split(silu_cc @ ada_w[l] + ada_b[l], 6, axis=-1)
        h = rms_norm(x, norm_mix[l]) * (1.0 + sc1) + sh1
        hc = rms_norm(xc, norm_mix[l]) * (1.0 + sc1c) + sh1c
        i = l // 2
        if l % 2 == 0:
            y, yc = even_layer(h, hc, even_w_in[i], even_w_out[i], diff_lambda[i], diff_subln[i], na_rpb[i], l, need_ctx)
        else:
            y, yc = odd_layer(h, hc, odd_w_in[i], odd_w_out[i], mla_q_norm[i], mla_w_uq[i], mla_kv_norm[i],
                              mla_w_ukv[i], ret_decay_logit[i], need_ctx)
        x = x + g1 * y
        h2 = rms_norm(x, norm_ffn[l]) * (1.0 + sc2) + sh2
        x = x + g2 * expert_choice_ffn(h2, moe_router[l], moe_w1[l], moe_w3[l], moe_w2[l])
        if need_ctx:
            xc = xc + g1c * yc
            hc2 = rms_norm(xc, norm_ffn[l]) * (1.0 + sc2c) + sh2c
            xc = xc + g2c * expert_choice_ffn(hc2, moe_router[l], moe_w1[l], moe_w3[l], moe_w2[l])
    return rms_norm(x, final_norm)


def setup_inputs(seed=0):
    out = dict(first_inputs(seed))
    for name, value in second_inputs(seed + 1).items():
        if name != "x":
            out[name + "_2"] = value
    return out


def reference(
    x, c, ctx, c_ctx, norm_w, w_ada, b_ada, w_in, conv_w, conv_b, dt_bias, a_log, d_skip,
    ssd_norm_w, w_fourier, b_fourier, w_out, final_norm_w, c_2, ctx_2, c_ctx_2, ada_w_2,
    ada_b_2, norm_mix_2, norm_ffn_2, final_norm_2, even_w_in_2, even_w_out_2, diff_lambda_2,
    diff_subln_2, na_rpb_2, odd_w_in_2, odd_w_out_2, mla_q_norm_2, mla_w_uq_2, mla_kv_norm_2,
    mla_w_ukv_2, ret_decay_logit_2, moe_router_2, moe_w1_2, moe_w3_2, moe_w2_2,
):
    x = first_block(
        x, c, ctx, c_ctx, norm_w, w_ada, b_ada, w_in, conv_w, conv_b, dt_bias, a_log, d_skip,
        ssd_norm_w, w_fourier, b_fourier, w_out, final_norm_w,
    )
    return second_block(
        x, c_2, ctx_2, c_ctx_2, ada_w_2, ada_b_2, norm_mix_2, norm_ffn_2, final_norm_2,
        even_w_in_2, even_w_out_2, diff_lambda_2, diff_subln_2, na_rpb_2, odd_w_in_2,
        odd_w_out_2, mla_q_norm_2, mla_w_uq_2, mla_kv_norm_2, mla_w_ukv_2, ret_decay_logit_2,
        moe_router_2, moe_w1_2, moe_w3_2, moe_w2_2,
    )


_drawn_inputs = setup_inputs


def setup_inputs(seed=0):
    import zlib

    import numpy as np

    out = dict(_drawn_inputs(seed))
    spreads = {}
    factors = {'ctx': 7.348,
     'c_ctx': 8.0,
     'norm_w': 2.762,
     'conv_b': 5.532,
     'd_skip': 4.593,
     'ssd_norm_w': 3.82,
     'b_fourier': 8.0,
     'ada_b_2': 3.713,
     'norm_mix_2': 8.0,
     'norm_ffn_2': 7.07,
     'final_norm_2': 2.709,
     'diff_lambda_2': 4.645,
     'diff_subln_2': 8.0,
     'na_rpb_2': 8.0,
     'mla_q_norm_2': 8.0,
     'mla_kv_norm_2': 8.0}
    for name, (base, spread) in spreads.items():
        noise = np.random.default_rng([zlib.crc32(name.encode()), seed]).standard_normal(out[name].shape)
        drawn = base * np.exp(spread * noise) if base else spread * noise
        out[name] = jnp.asarray(drawn.astype(out[name].dtype))
    for name, factor in factors.items():
        out[name] = (out[name] * factor).astype(out[name].dtype)
    return out
```

```python
from contextlib import ExitStack

import numpy as np
import concourse.bass as bass
from concourse import mybir

F32 = mybir.dt.float32
ALU = mybir.AluOpType
ACT = mybir.ActivationFunctionType
AX = mybir.AxisListType.X

P = 128
D = 1024
KT = D // P
SEQ = 256
TOK = 2 * SEQ
GRID_W = 64
ROWS = SEQ // GRID_W
EPS = 1e-6
D_SSD, D_FOUR = 1536, 512
HEADS, GROUPS = 24, 4
HPG = HEADS // GROUPS
GW = D_SSD // GROUPS
CONV_TILES = 20
EXPERTS, CAP, FF = 16, 32, 1024
SLOT = 4096
LAM_INIT = 0.8 - 0.6 * float(np.exp(-0.3 * 0))
NA_SCALE = 64 ** -0.5
MLA_SCALE = 96 ** -0.5
MASKED = -1.0e30


def rope_tables(rot, n_pad):
    t = np.arange(SEQ)
    m = rot // 4
    freq = (10000.0 ** (-np.arange(m, dtype=np.float32) / m)).astype(np.float32)
    ang = [(t // GRID_W)[:, None].astype(np.float32) * freq, (t % GRID_W)[:, None].astype(np.float32) * freq]
    n = n_pad + rot
    cos, sin, swap = np.ones((n, SEQ), np.float32), np.zeros((n, SEQ), np.float32), np.zeros((n, n), np.float32)
    for half in range(2):
        for j in range(m):
            a = n_pad + half * 2 * m + j
            b = a + m
            cos[a] = cos[b] = np.cos(ang[half][:, j])
            sin[a] = sin[b] = np.sin(ang[half][:, j])
            swap[b, a] = -1.0
            swap[a, b] = 1.0
    return cos, sin, swap


def shape_constants():
    p = np.arange(P)
    c = {}
    c["ident"] = np.eye(P)
    tok = np.arange(SEQ)
    le = (tok[:, None] <= tok[None, :]).astype(np.float32)
    c["tri_f"] = le.reshape(2, P, SEQ).transpose(1, 0, 2)
    c["tri_b"] = le.T.reshape(2, P, SEQ).transpose(1, 0, 2)
    sel = np.zeros((P, 2))
    sel[p[p % 32 == 0], 0] = 1
    sel[p[p % 32 == 1], 1] = 1
    c["sum2"] = sel
    c["sel_x"] = np.repeat(sel[:, 0:1], P, 1)
    c["sel_c"] = np.repeat(sel[:, 1:2], P, 1)
    c["sel_xc"] = np.concatenate([c["sel_x"][:, :32], c["sel_c"][:, :32]], 1)
    pick = np.zeros((P, 30, 2))
    pick[np.arange(30), np.arange(30), :] = 1
    c["ada_pick"] = pick
    c["iota"] = np.repeat(1.0 + np.arange(CAP)[None, :], P, 0)
    cc = np.arange(GRID_W)
    cs = np.clip(cc - 8, 0, GRID_W - 16)
    inside = (cc[None, :] >= cs[:, None]) & (cc[None, :] < cs[:, None] + 16)
    c["na_mask"] = np.tile(np.where(inside, 0.0, MASKED), (2, 1))
    pos = 128.0 * np.arange(2)[None, :] + p[:, None]
    c["ret_age"] = np.concatenate([255.0 - pos, pos], 1)
    c["block1"] = None
    g = np.arange(64)
    ang = 2 * np.pi * np.outer(g, g) / 64
    bd = lambda m: np.kron(np.eye(2), m)
    k = {}
    k["dft_ch"] = np.concatenate([bd(np.cos(ang)), bd(np.sin(ang))], 1)
    angt = 2 * np.pi * (np.outer(tok, tok) % SEQ) / SEQ
    k["dft_cos"] = (np.cos(angt) / 128.0).reshape(2, P, SEQ).transpose(1, 0, 2)
    k["dft_nsin"] = (-np.sin(angt) / 128.0).reshape(2, P, SEQ).transpose(1, 0, 2)
    del c["block1"]
    cos, sin, swap = rope_tables(64, 0)
    e = {"rope_cos": np.tile(cos, (2, 1)), "rope_sin": np.tile(sin, (2, 1)), "rope_swap": np.kron(np.eye(2), swap)}
    cos, sin, swap = rope_tables(32, 64)
    pad = lambda a, n: np.concatenate([a, np.zeros((P - a.shape[0], a.shape[1]))], 0)
    o = {"mla_cos": pad(cos, P), "mla_sin": pad(sin, P), "mla_swap": pad(swap, P)}
    o["ret_fwd"] = np.maximum(tok[None, :] - tok[:, None], 0).reshape(2, P, SEQ).transpose(1, 0, 2)
    o["ret_bwd"] = np.maximum(tok[:, None] - tok[None, :], 0).reshape(2, P, SEQ).transpose(1, 0, 2)
    o["ret_q"] = np.repeat(np.stack([tok + 1.0, 256.0 - tok])[None], P, 0)
    flat = lambda d: {n: np.ascontiguousarray(a, np.float32).reshape(P, -1) for n, a in d.items()}
    return flat(c), flat(k), flat(e), flat(o)


def packed(d):
    at, off = {}, 0
    for n, a in d.items():
        at[n] = (off, a.shape[1])
        off += a.shape[1]
    return np.ascontiguousarray(np.concatenate(list(d.values()), 1), np.float32), at


CONSTS = tuple(packed(d) for d in shape_constants())

PAR = {}
_n = 0
for _name, _w in (("cvec1", 16), ("cvec2", 16), ("norm_w", 8), ("conv_w", 180), ("conv_b", 20), ("ssd_norm", 12),
                  ("b_four", 4), ("norm_mix", 16), ("norm_ffn", 16), ("subln", 1), ("q_norm", 2), ("kv_norm", 1)):
    PAR[_name] = (_n, _w)
    _n += _w
N_PAR = _n
ROWP = {}
_n = 0
for _name, _w in (("dt_bias", 48), ("a_log", 48), ("d_skip", 24), ("diff_lambda", 256), ("ret_decay", 8)):
    ROWP[_name] = (_n, _w)
    _n += _w
N_ROWP = _n


def build(nc, A, out):
    ctx = ExitStack()
    with ctx:
        WORDS = 53200
        mem = ctx.enter_context(nc.sbuf_tensor("mem", [P, WORDS], F32))
        bank = [ctx.enter_context(nc.psum_tensor(f"bank{i}", [P, 512], F32)) for i in range(8)]

        def sem(name):
            return ctx.enter_context(nc.semaphore(name))

        class Region:

            def __init__(self, at, words):
                self.at, self.end = at, at + words

            def take(self, *dims):
                n = int(np.prod(dims))
                assert self.at + n <= self.end, (self.at, n, self.end)
                v = mem[:, self.at:self.at + n]
                self.at += n
                if len(dims) == 2:
                    v = v.rearrange("p (a b) -> p a b", b=dims[1])
                elif len(dims) == 3:
                    v = v.rearrange("p (a b c) -> p a b c", b=dims[1], c=dims[2])
                return v

        RING0 = 0
        ARENA2 = 3 * SLOT
        XRES = 6 * SLOT
        XN = XRES + 4096
        HT = XN + 4096
        FIXED = HT + 4096
        fixed = Region(FIXED, WORDS - FIXED)
        xres = Region(XRES, 4096).take(4, D)
        xn = Region(XN, 4096).take(4, D)
        hT = Region(HT, 4096).take(KT, TOK)

        consts, const_at = CONSTS[0]
        cbuf = fixed.take(consts.shape[1])
        C = lambda n: cbuf[:, const_at[n][0]:const_at[n][0] + const_at[n][1]]
        ident = C("ident")
        tri_f = C("tri_f").rearrange("p (a b) -> p a b", b=SEQ)
        tri_b = C("tri_b").rearrange("p (a b) -> p a b", b=SEQ)
        par = fixed.take(N_PAR)
        rowp = fixed.take(N_ROWP)
        G = lambda n: par[:, PAR[n][0]:PAR[n][0] + PAR[n][1]]
        R = lambda n: rowp[:, ROWP[n][0]:ROWP[n][0] + ROWP[n][1]]
        ADA_WORK = fixed.at
        ada_bias = fixed.take(512)
        silu_c = [fixed.take(KT, 32) for _ in range(2)]
        ada_row = [fixed.take(512) for _ in range(2)]
        ADA_WORK_WORDS = fixed.at - ADA_WORK
        ada_col = [fixed.take(2, 16), fixed.take(4, 16), fixed.take(4, 16)]
        norm_a = fixed.take(5, 16)
        gate_1 = fixed.take(D)
        gate_mix = [fixed.take(2, D), fixed.take(1, D)]
        gate_ffn = [fixed.take(512), fixed.take(256)]
        ssq = fixed.take(4)
        meansq = fixed.take(4)
        rstd = fixed.take(4)
        neg_half = fixed.take(32)
        small = fixed.take(112)
        fixed_extra = fixed.take(8)
        ARENA1 = fixed.at
        ARENA1_WORDS = WORDS - ARENA1

        chunks = []

        def cols(w, a, n):
            return w[:, a:a + n].rearrange("(k p) f -> p k f", p=P)

        def rows(w, a, n):
            return w[a:a + n, :].rearrange("(k p) f -> p k f", p=P)

        def chunk(name, src):
            chunks.append((name, src))

        w_in = A["w_in"]
        for i in range(4):
            chunk(f"ada0.{i}", cols(A["w_ada"], 512 * i, 512))
        chunk("dt", cols(w_in, 5120, 48))
        chunk("u", cols(w_in, 0, 512))
        chunk("zf", cols(w_in, 512, 512))
        chunk("w_four", rows(A["w_fourier"], 0, 512))
        for i in range(4, 6):
            chunk(f"ada0.{i}", cols(A["w_ada"], 512 * i, 512))
        for i in range(5):
            chunk(f"conv{i}", cols(w_in, 2560 + 512 * i, 512))
        for i in range(3):
            chunk(f"zs{i}", cols(w_in, 1024 + 512 * i, 512))
        for i in range(20):
            chunk(f"ada{i // 12 + 1}.{i % 12}", cols(A["ada_w"][i // 12], 512 * (i % 12), 512))
        for i in range(4):
            chunk(f"w_out{i}", rows(A["w_out"], 512 * i, 512))
        for i in range(20, 24):
            chunk(f"ada{i // 12 + 1}.{i % 12}", cols(A["ada_w"][i // 12], 512 * (i % 12), 512))
        for i in range(6):
            chunk(f"even{i}", cols(A["even_w_in"][0], 512 * i, 512))
        for i in range(2):
            chunk(f"even_out{i}", rows(A["even_w_out"][0], 512 * i, 512))
        N_PRE0 = len(chunks)
        odd = A["odd_w_in"][0]
        odd_chunks = []
        odd_chunks.append(("odd_cq", cols(odd, 0, 416)))
        odd_chunks.append(("odd_rqk", cols(odd, 416, 512)))
        odd_chunks.append(("odd_rv", cols(odd, 928, 512)))
        odd_chunks.append(("odd_rg", cols(odd, 1440, 512)))
        odd_chunks.append(("w_ukv", rows(A["mla_w_ukv"][0], 0, 128)))
        odd_chunks.append(("w_uq", rows(A["mla_w_uq"][0], 0, 256)))
        for i in range(2):
            odd_chunks.append((f"odd_out{i}", rows(A["odd_w_out"][0], 512 * i, 512)))
        chunks += odd_chunks
        place, fill_no = {}, {}
        filled = [sem(f"slot{i}_filled") for i in range(6)]
        fills = [0] * 6
        turn = 0
        for n, (name, _) in enumerate(chunks[:N_PRE0]):
            s = turn % 3
            turn += 1
            fills[s] += 1
            place[name], fill_no[name] = s, fills[s]
        moe_slot = [[0] * 6, [0] * 6]
        moe_fill = [[0] * 6, [0] * 6]

        def moe_places(l):
            first = turn % 3
            for j in range(6):
                s = (first + j) % 3 + (3 if j >= 3 else 0)
                moe_slot[l][j] = s
                moe_fill[l][j] = fills[s]
            for s in range(6):
                fills[s] += EXPERTS

        moe_places(0)
        for name, _ in chunks[N_PRE0:]:
            s = turn % 3
            turn += 1
            fills[s] += 1
            place[name], fill_no[name] = s, fills[s]
        moe_places(1)

        def slot(s, k, n):
            return mem[:, RING0 + s * SLOT:RING0 + s * SLOT + k * n].rearrange("p (k f) -> p k f", f=n)

        def chunk_view(name):
            src = dict(chunks)[name]
            return slot(place[name], src.shape[1], src.shape[2])

        mm_done = sem("mm_done")
        took_sem = {"dve": sem("dve_took"), "act": sem("act_took")}
        consts_in = sem("consts_in")
        x_in, ctx_in, bias_in = sem("x_in"), sem("ctx_in"), sem("bias_in")
        ctx2_in = sem("ctx2_in")
        arena_in = {n: sem(f"{n}_in") for n in ("dft", "rope", "na_bias", "odd_tables", "router0", "router1", "gain1", "gain2")}
        silu_pad = sem("silu_pad")
        silu_done = sem("silu_done")
        sums_done = sem("sums_done")
        ms_done = sem("ms_done")
        rstd_done = sem("rstd_done")
        xn_done = sem("xn_done")
        pool_zero = sem("pool_zero")
        dt_abs, dt_log, a_ready, a_exp = sem("dt_abs"), sem("dt_log"), sem("a_ready"), sem("a_exp")
        ctx_arg, ctx_exp, ctx_w = sem("ctx_arg"), sem("ctx_exp"), sem("ctx_w")
        x_ecum, xw_done = sem("x_ecum"), sem("xw_done")
        y_skip, ssd_z, ssd_sq = sem("y_skip"), sem("ssd_z"), sem("ssd_sq")
        conv_done, act_conv = sem("conv_done"), sem("act_conv")
        decay_out, m_ready, gated_done = sem("decay_out"), sem("m_ready"), sem("gated_done")
        out_stored, out_ready = sem("out_stored"), sem("out_ready")
        neg_max, comb_done = sem("neg_max"), sem("comb_done")
        na_neg, na_p = sem("na_neg"), sem("na_p")
        m_neg = sem("m_neg")
        lam_sum, lam_exp = sem("lam_sum"), sem("lam_exp")
        q_ready, att_done = sem("q_ready"), sem("att_done")
        rt_neg, rt_exp = sem("rt_neg"), sem("rt_exp")
        aff_done, topk_done, d_done = sem("aff_done"), sem("topk_done"), sem("d_done")
        lg_abs, lg_ln, lg_done = sem("lg_abs"), sem("lg_ln"), sem("lg_done")
        ret_arg, ret_tab, ret_qdec, rkw_done, rq_done = (sem(n) for n in ("ret_arg", "ret_tab", "ret_qdec", "rkw_done", "rq_done"))
        moe_bufs_zero = sem("moe_bufs_zero")
        pair = lambda n: [sem(n + "0"), sem(n + "1")]
        dstage, xe_staged, moe_used, silu_ready = pair("dstage"), pair("xe_staged"), pair("moe_used"), pair("silu_ready")
        hid_ready, hidT_mm, hidT_ready, y_ready = pair("hid_ready"), pair("hidT_mm"), pair("hidT_ready"), pair("y_ready")
        dT_mm, dgT_ready, scat_mm, acc_done = pair("dT_mm"), pair("dgT_ready"), pair("scat_mm"), pair("acc_done")

        N_CONST_DMAS = 3
        tiles = {}

        class Tile:
            pass

        class Banks:

            def __init__(self, pe):
                self.pe, self.count, self.next = pe, 0, 0
                self.ordinal = {"dve": 0, "act": 0}
                self.last = [None] * 8
                self.open_banks = set()

            def open(self, name, by):
                while self.next % 8 in self.open_banks:
                    self.next += 1
                b = self.next % 8
                self.next += 1
                prev = self.last[b]
                if prev is not None:
                    self.pe.wait_ge(took_sem[prev.by], prev.ordinal)
                t = Tile()
                t.name, t.by, t.b, t.ps = name, by, b, bank[b]
                self.open_banks.add(b)
                return t

            def close(self, t, ins):
                ins.then_inc(mm_done, 1)
                self.count += 1
                self.ordinal[t.by] += 1
                t.no, t.ordinal = self.count, self.ordinal[t.by]
                self.last[t.b] = t
                self.open_banks.discard(t.b)
                assert t.name not in tiles
                tiles[t.name] = t

        taken = {"dve": 0, "act": 0}

        def arrive(eng, name):
            eng.wait_ge(mm_done, tiles[name].no)
            return tiles[name].ps

        def took(name, ins):
            t = tiles[name]
            taken[t.by] += 1
            assert taken[t.by] == t.ordinal, (name, taken[t.by], t.ordinal)
            ins.then_inc(took_sem[t.by], 1)

        def wait_took(eng, name):
            eng.wait_ge(took_sem[tiles[name].by], tiles[name].ordinal)

        chunk_freed = {}

        NORM_TILES = [4, 2, 4, 4, 4, 2, 2]
        NORM_SUM = [sum(NORM_TILES[:i + 1]) for i in range(7)]
        ADA = [(0, i) for i in range(6)] + [(l + 1, i) for l in range(2) for i in range(12)]

        ADA_AT_HEAD = {}
        for h in range(HEADS):
            if h % 4 != 3:
                ADA_AT_HEAD[h] = 6 + len(ADA_AT_HEAD)
        ADA_LEFT = 6 + len(ADA_AT_HEAD)

        def ada_kind(k):
            s, i = ADA[k]
            v, half = i // 2, i % 2
            if s == 0:
                return ("col", v, half) if v < 2 else ("gate1", 0, half)
            return {0: ("col", 0, half), 1: ("col", 1, half), 2: ("mix", 0, half),
                    3: ("col", 2, half), 4: ("col", 3, half), 5: ("ffn", 0, half)}[v]

        a1 = Region(ARENA1, ARENA1_WORDS)
        mixT = a1.take(16, SEQ)
        uT, zfT, mixedT = mixT[:, 4:8, :], mixT[:, 8:12, :], mixT[:, 12:16, :]
        cumT = a1.take(2, SEQ)
        dt_z, dt_a, dt_v, a_dt = (a1.take(4, 48) for _ in range(4))
        cum_col = a1.take(4, 48)
        x_dec = a1.take(2, 48)
        w_ctx = a1.take(2, 48)
        exp_alog = a1.take(48)
        y_t = [a1.take(GW) for _ in range(2)]
        r = Region(XRES + 2048, 2048)
        y_acc = [r.take(GW) for _ in range(2)]
        off_t = [y_t, [r.take(GW) for _ in range(2)]]
        sq_junk = r.take(GW)
        gain_1 = Region(ARENA2 + 4096, D).take(D)
        a2 = Region(ARENA2, 3 * SLOT)
        xs_tok = a2.take(4, D_SSD)
        conv0 = a2.at
        xpad = [a2.take(6, 66) for _ in range(2)]
        cpad = [a2.take(258) for _ in range(2)]
        conv_acc = [a2.take(512) for _ in range(2)]
        conv_out = [a2.take(512) for _ in range(2)]
        dft_a = a2.take(2, 4, 256)
        a2b = Region(conv0, 6144)
        cb = a2b.take(GROUPS, 2, 384)
        h_init = a2b.take(2, D_SSD)
        dft_tab, dft_at = CONSTS[1]
        dft = Region(ARENA2, 1280).take(dft_tab.shape[1])
        DFT = lambda n: dft[:, dft_at[n][0]:dft_at[n][0] + dft_at[n][1]]
        dft_cos = DFT("dft_cos").rearrange("p (a b) -> p a b", b=SEQ)
        dft_nsin = DFT("dft_nsin").rearrange("p (a b) -> p a b", b=SEQ)
        r = Region(XN, 4096)
        zs = r.take(2, D_SSD)
        c_fm = r.take(GROUPS, SEQ)
        r = Region(XRES + 2048, 2048)
        b_tok = r.take(2, 512)
        b_fm = r.take(GROUPS, SEQ)
        xw = [mixT[:, 4:16, :].rearrange("p a b -> p (a b)").rearrange("p (q c) -> p q c", c=D_SSD),
              Region(HT, 4096).take(2, D_SSD)]
        r = Region(HT, 4096)
        dec_arg = [r.take(2, 384) for _ in range(2)]
        dec_exp = [r.take(2, 384) for _ in range(2)]
        m_mat = [r.take(2, SEQ) for _ in range(2)]
        res_t = [Region(ARENA1 + 512 * i, 512).take(512) for i in range(4)]
        r = Region(ARENA2, 3 * SLOT)
        qz = [r.take(4, TOK) for _ in range(2)]
        k_fm = r.take(4, TOK)
        v_tok = r.take(4, 512)
        nqz = [r.take(4, TOK) for _ in range(2)]
        r = Region(ARENA1, ARENA1_WORDS)
        nk_fm = r.take(4, TOK)
        nv_tok = r.take(4, 512)
        keep = r.at
        rope_tab, rope_at = CONSTS[2]
        rope = r.take(rope_tab.shape[1])
        ROPE = lambda n: rope[:, rope_at[n][0]:rope_at[n][0] + rope_at[n][1]]
        rope_raw = [r.take(TOK) for _ in range(2)]
        rope_t = [r.take(SEQ) for _ in range(2)]
        r = Region(keep, ARENA1 + ARENA1_WORDS - keep)
        probs = [[r.take(512) for _ in range(2)] for _ in range(2)]
        na_p_buf = [*probs[0], *probs[1]]
        probs.append(ada_row)
        sq_t = r.take(512)
        r = Region(HT, 4096)
        na_bias = r.take(8, 384)
        att_T2 = [r.take(4, P) for _ in range(2)]
        att = xn
        attT = hT
        d_sel = [Region(moe_slot[l][5] * SLOT, SLOT).take(4, 512) for l in range(2)]
        r = Region(ARENA1, ARENA1_WORDS)
        xe_hi = r.take(4, 1024)
        d_gate = r.take(4, 512)
        hid = r.take(512)
        xe_lo = Region(HT, 4096).take(4, 1024)
        r = Region(XN, 4096)
        y_sb = r.take(D)
        silu_h = r.take(512)
        hidT = r.take(512)
        dgT = r.take(512)
        dstg = r.take(4, P)
        xe_stg = r.take(1024)
        r = Region(ADA_WORK, ADA_WORK_WORDS)
        router_sb = r.take(KT, EXPERTS)
        aff = r.take(4, EXPERTS)
        aff_work = r.take(SEQ)
        sel_e = r.take(SEQ)
        top8 = [r.take(8) for _ in range(4)]
        sel_t = r.take(4, EXPERTS)
        slot_t = r.take(4, EXPERTS)
        rt_mx = r.take(4, 1)
        rt_t = r.take(4, EXPERTS)
        rt_sum = r.take(4, 1)
        r = Region(ARENA2, 3 * SLOT)
        mk = r.take(8, TOK)
        mq = r.take(8, SEQ)
        mv_tok = r.take(4, 512)
        rv_tok = r.take(4, 512)
        rg_tok = r.take(2, 512)
        ret_state = r.take(4, SEQ)
        r = Region(ARENA1, ARENA1_WORDS)
        ret_d = r.take(4, 512)
        odd_tab, odd_at = CONSTS[3]
        odd_c = r.take(odd_tab.shape[1])
        ODD = lambda n: odd_c[:, odd_at[n][0]:odd_at[n][0] + odd_at[n][1]]
        rk_tok = r.take(2, SEQ)
        probs1 = [r.take(512) for _ in range(2)]
        probs1.append(ada_row[0])
        r = Region(XRES + 2048, 2048)
        rqz = r.take(4, SEQ)
        rk_fm = r.take(2, SEQ)
        ret_s2 = [r.take(2, SEQ)]
        r = Region(XN, 4096)
        c_lat = r.take(4, 384)
        cqT = r.take(2, SEQ)
        ckvT = r.take(TOK)
        kr_raw = r.take(TOK)
        q_raw = [r.take(512), probs1[1]]
        q_rot = [probs1[0], probs1[2]]
        ret_s2.append(r.take(2, SEQ))
        r = Region(XN, 4096)
        att1 = r.take(2, D)
        r.take(512)
        att_T21 = [r.take(4, P) for _ in range(2)]
        r = Region(HT, 4096)
        rqf = r.take(4, SEQ)
        rqb = r.take(4, SEQ)
        rvw_all = r.take(4, 2, SEQ)
        attT1 = Region(HT, 4096).take(KT, SEQ)
        kr_copied = sem("kr_copied")
        res_done = sem("res_done")
        gain0_done, na_masked = sem("gain0_done"), sem("na_masked")
        part_used = sem("part_used")
        lam_b = fixed_extra[:, 0:4]

        POW = ["norm0", "norm1", "norm2", "diff", "norm3", "norm4", "lat", "ret", "norm5", "norm6"]
        NORM_A = {0: 0, 2: 1, 3: 2, 4: 3, 5: 4}
        NORM_B = {0: (0, 0), 2: (1, 0), 3: (1, 2), 4: (2, 0), 5: (2, 2)}
        ssq8, ms8, rstd8 = small[:, 0:8], small[:, 8:16], small[:, 16:24]
        a_neg, a_mx, a_sum, a_rec = small[:, 0:6], small[:, 6:12], small[:, 12:18], small[:, 18:24]
        n_neg, n_mx, n_sum, n_rec = small[:, 24:28], small[:, 28:32], small[:, 32:48], small[:, 48:64]
        d_ss, d_ms = small[:, 64:80], small[:, 80:96]
        m_ng, m_mx, m_sum, m_rec = small[:, 8:11], small[:, 11:14], small[:, 40:56], small[:, 96:112]

        def xe_rows(l, kt, s):
            S = 64 if l == 0 else 32
            rows = (xe_lo if kt < 4 else xe_hi)[:, kt % 4, 0:EXPERTS * S].rearrange("p (e s) -> p e s", s=S)
            return rows[:, :, CAP * s:CAP * s + CAP]

        def bc(ap, dims):
            return ap.to_broadcast(dims)

        block = ctx.enter_context(nc.Block())

        @block.tensor
        def _(pe):
            B = Banks(pe)

            def use(name):
                pe.wait_ge(filled[place[name]], 16 * fill_no[name])
                return chunk_view(name)

            def done_with(name):
                chunk_freed[name] = (mm_done, B.count)

            def mm(o, lhsT, rhs, start, stop):
                return nc.tensor.matmul(o, lhsT, rhs, start=start, stop=stop, skip_group_check=True)

            def tr(o, i):
                return nc.tensor.transpose(o, i, ident)

            def ada_rows(k):
                s, i = ADA[k]
                w = use(f"ada{s}.{i}")
                t = B.open(f"row{k}", "dve")
                for kt in range(KT):
                    g = kt % 4
                    mm(t.ps[32 * g:32 * g + 32, :], silu_c[min(s, 1)][:, kt, :], w[:, kt, :], kt < 4, kt >= 4 and g > 0)
                pick = C("ada_pick").rearrange("p (a b) -> p a b", b=2)
                B.close(t, mm(t.ps[0:2, :], pick[:, k, :], ada_bias, False, True))
                done_with(f"ada{s}.{i}")

            def ada_outs(k):
                kind, v, half = ada_kind(k)
                wait_took(pe, f"row{k}")
                row = ada_row[k % 2]
                l = ADA[k][0] - 1
                if kind == "col":
                    t = B.open(f"col{k}", "dve")
                    for j in range(4):
                        last = mm(t.ps[:, 2 * j:2 * j + 2], row[:, P * j:P * j + P], C("sum2"), True, True)
                    B.close(t, last)
                elif kind == "ffn":
                    t = B.open(f"col{k}", "dve")
                    if l == 0:
                        last = mm(t.ps[64 * half:64 * half + 64, :], C("sel_xc"), row, True, True)
                    else:
                        for q in range(2):
                            g = 2 * half + q
                            last = mm(t.ps[32 * g:32 * g + 32, 0:256], C("sel_x")[:, 0:32], row[:, 256 * q:256 * q + 256], True, True)
                    B.close(t, last)
                else:
                    for j, sel in enumerate(("sel_x", "sel_c")[:2 if (kind == "mix" and l == 0) else 1]):
                        t = B.open(f"col{k}" + "c" * j, "dve")
                        B.close(t, mm(t.ps[:, :], C(sel), row, True, True))

            def norm_T(n):
                T = NORM_TILES[n]
                pe.wait_ge(xn_done, NORM_SUM[n])
                for kt in range(KT):
                    t = B.open(f"nT{n}.{kt}", "act" if kt % 2 else "dve")
                    for j in range(T):
                        last = tr(t.ps[:, P * j:P * j + P], xn[:, j, P * kt:P * kt + P])
                    B.close(t, last)
                wait_took(pe, f"nT{n}.6")
                wait_took(pe, f"nT{n}.7")

            def feature_major(t, w, c0, mw, n0, n1, o=None, p0=0):
                o = t.ps[p0:p0 + mw, 0:n1 - n0] if o is None else o
                for kt in range(KT):
                    last = mm(o, w[:, kt, c0:c0 + mw], hT[:, kt, n0:n1], kt == 0, kt == KT - 1)
                return last

            def token_major(o, w, j, c0, nw):
                for kt in range(KT):
                    last = mm(o, hT[:, kt, P * j:P * j + P], w[:, kt, c0:c0 + nw], kt == 0, kt == KT - 1)
                return last

            pe.wait_ge(consts_in, 16 * N_CONST_DMAS)
            pe.wait_ge(bias_in, 16)
            pe.wait_ge(silu_done, 2)
            for k in range(4):
                ada_rows(k)
                if k:
                    ada_outs(k - 1)
            ada_outs(3)
            norm_T(0)
            w = use("dt")
            t = B.open("dt", "dve")
            for j in range(4):
                last = token_major(t.ps[:, 48 * j:48 * j + 48], w, j, 0, 48)
            B.close(t, last)
            done_with("dt")
            for name in ("u", "zf"):
                w = use(name)
                for m in range(4):
                    t = B.open(f"{name}{m}", "act")
                    B.close(t, feature_major(t, w, P * m, P, 0, SEQ))
                done_with(name)
            pe.wait_ge(arena_in["dft"], 16)
            wait_took(pe, "u3")
            for j in range(2):
                for h in range(2):
                    t = B.open(f"fa{j}{h}", "dve")
                    for q in range(2):
                        last = mm(t.ps[:, 256 * q:256 * q + 256], uT[:, 2 * h + q, P * j:P * j + P], DFT("dft_ch"), True, True)
                    B.close(t, last)
            wait_took(pe, "fa11")
            for h in range(2):
                t = B.open(f"fm{h}", "dve")
                for q in range(2):
                    n = 0
                    for j in range(2):
                        for part, tab in ((0, dft_cos), (1, dft_nsin)):
                            last = mm(t.ps[:, 256 * q:256 * q + 256], dft_a[:, j, 2 * h + q, P * part:P * part + P], tab[:, j, :], n == 0, n == 3)
                            n += 1
                B.close(t, last)
            w = use("w_four")
            wait_took(pe, "fm1")
            wait_took(pe, "zf3")
            for m in range(4):
                t = B.open(f"four{m}", "dve")
                for kt in range(4):
                    last = mm(t.ps[:, 0:SEQ], w[:, kt, P * m:P * m + P], mixedT[:, kt, :], kt == 0, kt == 3)
                B.close(t, last)
            done_with("w_four")

            ada_rows(4)
            ada_rows(5)
            ada_outs(4)
            ada_outs(5)

            def conv_proj(j):
                w = use(f"conv{j // 4}")
                t = B.open(f"conv{j}", "act")
                B.close(t, feature_major(t, w, P * (j % 4), P, 0, TOK if j < 16 else SEQ))
                if j % 4 == 3:
                    done_with(f"conv{j // 4}")

            def conv_T(j):
                if j >= 16:
                    return
                pe.wait_ge(act_conv, j + 1)
                t = B.open(f"ct{j}", "act")
                src = conv_out[j % 2]
                for q in (range(4) if j < 12 else range(2, 4)):
                    last = tr(t.ps[:, P * q:P * q + P], src[:, P * q:P * q + P])
                B.close(t, last)

            pe.wait_ge(a_ready, 1)
            t = B.open("cumT", "dve")
            for d, tab in enumerate((tri_f, tri_b)):
                for q in range(2):
                    last = mm(t.ps[0:24, SEQ * d:SEQ * d + SEQ], a_dt[:, q, 24 * d:24 * d + 24], tab[:, q, :], q == 0, q == 1)
            B.close(t, last)
            t = B.open("cum_col", "dve")
            for j in range(4):
                for d in range(2):
                    up = (d == 0) == (j < 2)
                    tab = tri_f if up else tri_b
                    lt = j % 2
                    qs = [q for q in range(2) if (q <= lt if up else q >= lt)]
                    for q in qs:
                        last = mm(t.ps[:, 48 * j + 24 * d:48 * j + 24 * d + 24], tab[:, q, P * lt:P * lt + P],
                                  a_dt[:, 2 * (j // 2) + q, 24 * d:24 * d + 24], q == qs[0], q == qs[-1])
            B.close(t, last)
            conv_proj(0)
            conv_proj(1)
            for j in range(CONV_TILES):
                if j + 2 < CONV_TILES:
                    conv_proj(j + 2)
                conv_T(j)
            for i in range(3):
                w = use(f"zs{i}")
                for j in range(2):
                    t = B.open(f"zs{i}{j}", "act")
                    B.close(t, token_major(t.ps[:, :], w, j, 0, 512))
                done_with(f"zs{i}")

            pe.wait_ge(act_conv, CONV_TILES)
            for g in range(GROUPS):
                t = B.open(f"cb{g}", "dve")
                for q in range(2):
                    last = mm(t.ps[:, SEQ * q:SEQ * q + SEQ], b_fm[:, g, P * q:P * q + P], c_fm[:, g, :], True, True)
                B.close(t, last)
            wait_took(pe, "ct15")
            for d in range(2):
                pe.wait_ge(xw_done, 2 * (d + 1))
                for g in range(GROUPS):
                    t = B.open(f"hs{d}{g}", "act")
                    for q in range(2):
                        last = mm(t.ps[:, 0:GW], b_tok[:, q, P * g:P * g + P], xw[d][:, q, GW * g:GW * g + GW], q == 0, q == 1)
                    B.close(t, last)
            wait_took(pe, "hs13")
            wait_took(pe, "cumT")

            def head_rows(h):
                t = B.open(f"bc{h}", "dve")
                B.close(t, mm(t.ps[:, :], ident[:, h:h + 1].to_broadcast([P, P]), cumT.rearrange("p a b -> p (a b)"), True, True))

            y_open = {}

            def head_y(h):
                g, c = h // HPG, 64 * (h % HPG)
                if h % HPG == 0:
                    for l in range(2):
                        y_open[l] = B.open(f"y{g}{l}", "dve")
                pe.wait_ge(m_ready, h + 1)
                for l in range(2):
                    for q in range(2):
                        last = mm(y_open[l].ps[:, c:c + 64], m_mat[h % 2][:, q, P * l:P * l + P], xs_tok[:, q, 64 * h:64 * h + 64], q == 0, q == 1)
                    if h % HPG == HPG - 1:
                        B.close(y_open[l], last)
                if h % HPG == HPG - 1:
                    for l in range(2):
                        for d in range(2):
                            t = B.open(f"off{g}{l}{d}", "dve")
                            B.close(t, mm(t.ps[:, 0:GW], c_fm[:, g, P * l:P * l + P], h_init[:, d, GW * g:GW * g + GW], True, True))

            head_rows(0)
            head_rows(1)
            for h in range(HEADS):
                if h + 2 < HEADS:
                    head_rows(h + 2)
                if h in ADA_AT_HEAD:
                    ada_rows(ADA_AT_HEAD[h])
                    if h:
                        ada_outs(ADA_AT_HEAD[h] - 1)
                head_y(h)
            for k in range(ADA_LEFT, 26):
                ada_rows(k)
                ada_outs(k - 1)

            def gated_T(m):
                t = B.open(f"gT{m}", "act" if m % 2 else "dve")
                for l in range(2):
                    last = tr(t.ps[:, P * l:P * l + P], zs[:, l, P * m:P * m + P])
                B.close(t, last)

            for m in range(9):
                pe.wait_ge(gated_done, 2 * (m // 3 + 1))
                gated_T(m)
            wait_took(pe, "four3")

            def project_out(names, src, T, kts, tag):
                o = {(j, n): B.open(f"{tag}{j}{n}", "dve") for j in range(T) for n in range(2)}
                per = 4
                for i, name in enumerate(names):
                    if tag == "o1_" and i == 2:
                        pe.wait_ge(gated_done, 8)
                        for m in range(9, 12):
                            gated_T(m)
                    w = use(name)
                    for q in range(per):
                        kt = per * i + q
                        if tag == "o1_" and kt >= 4:
                            wait_took(pe, f"gT{kt - 4}")
                        for j in range(T):
                            for n in range(2):
                                last = mm(o[j, n].ps[:, :], src[:, kt, P * j:P * j + P], w[:, q, 512 * n:512 * n + 512], kt == 0, kt == kts - 1)
                                if kt == kts - 1:
                                    B.close(o[j, n], last)
                    if i == len(names) - 1:
                        done_with(name)
                    else:
                        parts.append(name)
                        last.then_inc(part_used, 1)
                        chunk_freed[name] = (part_used, len(parts))

            parts = []
            project_out([f"w_out{i}" for i in range(4)], mixT, 2, 16, "o1_")

            for k in range(26, 30):
                ada_rows(k)
                ada_outs(k - 1)
            ada_outs(29)

            norm_T(2)
            for i, name in enumerate(("q", "k")):
                w = use(f"even{i}")
                if i == 0:
                    pe.wait_ge(arena_in["rope"], 16)
                for m in range(4):
                    t = B.open(f"{name}{m}", "act")
                    B.close(t, feature_major(t, w, P * m, P, 0, TOK))
                    if m == 3:
                        done_with(f"even{i}")
                    wait_took(pe, f"{name}{m}")
                    t = B.open(f"{name}r{m}", "dve")
                    B.close(t, mm(t.ps[:, 0:SEQ], ROPE("rope_swap"), rope_raw[m % 2][:, 0:SEQ], True, True))
            w = use("even2")
            for j in range(4):
                t = B.open(f"v{j}", "act")
                B.close(t, token_major(t.ps[:, :], w, j, 0, 512))
            done_with("even2")
            for i, name in ((3, "nq"), (4, "nk")):
                w = use(f"even{i}")
                for m in range(4):
                    t = B.open(f"{name}{m}", "act")
                    B.close(t, feature_major(t, w, P * m, P, 0, TOK))
                done_with(f"even{i}")
            w = use("even5")
            for j in range(4):
                t = B.open(f"nv{j}", "act")
                B.close(t, token_major(t.ps[:, :], w, j, 0, 512))
            done_with("even5")
            wait_took(pe, "nv3")
            wait_took(pe, "kr3")

            def d_scores(u):
                j, h = u // 4, u % 4
                n0 = 0 if j < 2 else SEQ
                for c in range(2):
                    t = B.open(f"ds{u}{'ab'[c]}", "act")
                    B.close(t, mm(t.ps[:, n0:TOK], qz[c][:, h, P * j:P * j + P], k_fm[:, h, n0:TOK], True, True))

            def probs_T(tag, u, src, j):
                t = B.open(f"{tag}T{u}", "act")
                for b in range(0 if j < 2 else 2, 4):
                    last = tr(t.ps[:, P * b:P * b + P], src[:, P * b:P * b + P])
                B.close(t, last)

            av_open = {}

            def attend(tag, u, per, width, v, j, h, T2):
                if h == 0:
                    av_open[tag] = B.open(f"{tag}o{j}", "dve")
                t = av_open[tag]
                wait_took(pe, f"{tag}T{u}")
                b0 = 0 if j < 2 else 2
                for b in range(b0, 4):
                    last = mm(t.ps[:, width * h:width * h + width], T2[u % 2][:, b, :], v[:, b, width * h:width * h + width], b == b0, b == 3)
                if h == per - 1:
                    B.close(t, last)

            d_scores(0)
            d_scores(1)
            for u in range(16):
                if u + 2 < 16:
                    d_scores(u + 2)
                pe.wait_ge(comb_done, u + 1)
                probs_T("d", u, probs[u % 3][0], u // 4)
                if u:
                    attend("d", u - 1, 4, P, v_tok, (u - 1) // 4, (u - 1) % 4, att_T2)
            attend("d", 15, 4, P, v_tok, 3, 3, att_T2)

            def n_scores(u):
                j, h = u // 8, u % 8
                n0 = 0 if j < 2 else SEQ
                t = B.open(f"ns{u}", "dve" if j < 2 else "act")
                B.close(t, mm(t.ps[:, n0:TOK], nqz[h % 2][:, h // 2, P * j:P * j + P], nk_fm[:, h // 2, n0:TOK], True, True))

            n_scores(0)
            n_scores(1)
            for u in range(32):
                if u + 2 < 32:
                    n_scores(u + 2)
                if u < 16:
                    pe.wait_ge(na_p, u + 1)
                else:
                    wait_took(pe, f"ns{u}")
                probs_T("n", u, na_p_buf[u % 4], u // 8)
                if u:
                    attend("n", u - 1, 8, 64, nv_tok, (u - 1) // 8, (u - 1) % 8, att_T2)
            attend("n", 31, 8, 64, nv_tok, 3, 7, att_T2)
            pe.wait_ge(att_done, 4)
            wait_took(pe, "no3")
            for kt in range(KT):
                t = B.open(f"aT{kt}", "dve" if kt < 4 else "act")
                for j in range(4):
                    last = tr(t.ps[:, P * j:P * j + P], att[:, j, P * kt:P * kt + P])
                B.close(t, last)
            wait_took(pe, "aT3")
            wait_took(pe, "aT7")
            project_out(["even_out0", "even_out1"], attT, 4, 8, "o2_")

            def route(l):
                T = 4 if l == 0 else 2
                norm_T(3 if l == 0 else 5)
                pe.wait_ge(arena_in[f"router{l}"], 16)
                t = B.open(f"rl{l}", "dve")
                for j in range(T):
                    last = token_major(t.ps[:, EXPERTS * j:EXPERTS * j + EXPERTS], router_sb, j, 0, EXPERTS)
                B.close(t, last)
                pe.wait_ge(aff_done, l + 1)
                t = B.open(f"affT{l}", "dve")
                for j in range(T):
                    r0 = 32 * (j // 2)
                    last = mm(t.ps[r0:r0 + EXPERTS, P * (j % 2):P * (j % 2) + P], aff[:, j, :], ident, True, True)
                B.close(t, last)
                pe.wait_ge(topk_done, l + 1)
                t = B.open(f"selT{l}", "dve")
                for j in range(T):
                    r0 = 32 * (j // 2)
                    n_rows = 16 * T - 16
                    last = mm(t.ps[:, EXPERTS * j:EXPERTS * j + EXPERTS], sel_e[0:n_rows, P * (j % 2):P * (j % 2) + P],
                              ident[0:n_rows, r0:r0 + EXPERTS], True, True)
                B.close(t, last)
                wait_took(pe, f"selT{l}")
                t = B.open(f"pos{l}", "dve")
                for j in range(T):
                    for q in range(j % 2 + 1):
                        last = mm(t.ps[:, EXPERTS * j:EXPERTS * j + EXPERTS], tri_f[:, q, P * (j % 2):P * (j % 2) + P],
                                  sel_t[:, 2 * (j // 2) + q, :], q == 0, q == j % 2)
                B.close(t, last)
                pe.wait_ge(d_done, l + 1)
                for kt in range(KT):
                    for s in range(T // 2):
                        t = B.open(f"ga{l}.{kt}{s}", "act" if (kt + s) % 2 else "dve")
                        for q in range(2):
                            last = mm(t.ps[:, :], xn[:, 2 * s + q, P * kt:P * kt + P], d_sel[l][:, 2 * s + q, :], q == 0, q == 1)
                        B.close(t, last)
                chunk_freed[f"gather{l}"] = B.count

            def experts(l):
                n_grp = 2 if l == 0 else 4
                S = P // n_grp
                W = FF // n_grp
                J = W // P
                T = 4 if l == 0 else 2
                used, xe = moe_used[l], xe_stg.rearrange("p (g k s) -> p g k s", g=n_grp, k=KT)
                h1, h3, tps, yps, dps = bank[0], bank[1], bank[2], bank[3], bank[4]
                pe.wait_ge(took_sem["dve"], B.ordinal["dve"])
                pe.wait_ge(took_sem["act"], B.ordinal["act"])
                pieces = [slot(moe_slot[l][j], 4, 1024) for j in range(6)]
                hT4 = hidT[:, 0:P * J].rearrange("p (j g s) -> p j g s", j=J, g=n_grp)
                with nc.tensor.Fori(0, EXPERTS // n_grp) as it:
                    for e in range(n_grp):
                        def landed(j):
                            pe.wait_ge(filled[moe_slot[l][j]], it * (16 * n_grp) + 16 * (moe_fill[l][j] + e + 1))
                        pe.wait_ge(xe_staged[l], it * n_grp + (e + 1))
                        for m, ps in ((0, h1), (1, h3)):
                            for half in range(2):
                                landed(2 * m + half)
                                w = pieces[2 * m + half]
                                for q in range(4):
                                    kt = 4 * half + q
                                    for g in range(n_grp):
                                        last = mm(ps[S * g:S * g + S, 0:W], xe[:, e, kt, :], w[:, q, W * g:W * g + W], kt == 0, kt == KT - 1)
                                last.then_inc(used, 1)
                        pe.wait_ge(hid_ready[l], it * n_grp + (e + 1))
                        for j in range(J):
                            last = tr(tps[:, P * j:P * j + P], hid[:, P * j:P * j + P])
                        last.then_inc(hidT_mm[l], 1)
                        pe.wait_ge(hidT_ready[l], it * n_grp + (e + 1))
                        if e:
                            pe.wait_ge(y_ready[l], it * n_grp + e)
                        for half in range(2):
                            landed(4 + half)
                            w = pieces[4 + half]
                            for q in range(4):
                                ft = 4 * half + q
                                for g in range(n_grp):
                                    last = mm(yps[S * g:S * g + S, 0:W], hT4[:, ft % J, ft // J, :], w[:, q, W * g:W * g + W], ft == 0, ft == 7)
                            last.then_inc(used, 1)
                        if e == 0:
                            pe.wait_ge(dstage[l], it + 1)
                            for j in range(T):
                                last = tr(dps[:, P * j:P * j + P], dstg[:, j, :])
                            last.then_inc(dT_mm[l], 1)
                    pe.wait_ge(dgT_ready[l], it + 1)
                    pe.wait_ge(y_ready[l], it * n_grp + n_grp)
                    for i in range(2 * T):
                        if i >= 3:
                            pe.wait_ge(acc_done[l], it * (2 * T) + (i - 2))
                        mm(bank[5 + i % 3][:, :], dgT[:, P * (i // 2):P * (i // 2) + P], y_sb[:, 512 * (i % 2):512 * (i % 2) + 512],
                           True, True).then_inc(scat_mm[l], 1)
                pe.wait_ge(acc_done[l], 2 * T * (EXPERTS // n_grp))

            route(0)
            experts(0)

            norm_T(4)
            w = use("odd_cq")
            for j in range(4):
                t = B.open(f"lat{j}", "dve")
                B.close(t, token_major(t.ps[:, 0:384], w, j, 0, 384) if j < 2 else token_major(t.ps[:, 256:384], w, j, 256, 128))
            t = B.open("krope", "act")
            B.close(t, feature_major(t, w, 384, 32, 0, TOK, p0=64))
            done_with("odd_cq")
            pe.wait_ge(arena_in["odd_tables"], 16)
            w = use("odd_rqk")
            for m in range(2):
                t = B.open(f"rq{m}", "act")
                B.close(t, feature_major(t, w, P * m, P, 0, SEQ))
            for m in range(2):
                t = B.open(f"rk{m}", "act")
                B.close(t, feature_major(t, w, 256 + P * m, P, 0, SEQ))
            for j in range(2):
                t = B.open(f"rkt{j}", "act")
                B.close(t, token_major(t.ps[:, 0:SEQ], w, 2 + j, 256, SEQ))
            done_with("odd_rqk")
            w = use("odd_rv")
            for j in range(4):
                t = B.open(f"rv{j}", "act")
                B.close(t, token_major(t.ps[:, :], w, j, 0, 512))
            done_with("odd_rv")
            w = use("odd_rg")
            for j in range(2):
                t = B.open(f"rg{j}", "act")
                B.close(t, token_major(t.ps[:, :], w, j, 0, 512))
            done_with("odd_rg")
            wait_took(pe, "krope")
            t = B.open("krot", "dve")
            B.close(t, mm(t.ps[64:96, 0:SEQ], ODD("mla_swap")[64:96, 64:96], kr_raw[64:96, 0:SEQ], True, True))
            pe.wait_ge(q_ready, 1)
            for m in range(2):
                t = B.open(f"cqT{m}", "dve")
                for j in range(2):
                    last = tr(t.ps[:, P * j:P * j + P], c_lat[:, j, P * m:P * m + P])
                B.close(t, last)
            t = B.open("ckvT", "dve")
            for j in range(4):
                last = tr(t.ps[:, P * j:P * j + P], c_lat[:, j, 256:384])
            B.close(t, last)
            w = use("w_ukv")
            wait_took(pe, "ckvT")
            for h in range(8):
                t = B.open(f"kn{h}", "act")
                B.close(t, mm(t.ps[0:64, :], w[:, 0, P * h:P * h + 64], ckvT, True, True))
            wv = w[:, 0, :].rearrange("p (h c) -> p h c", c=P)[:, :, 64:128]
            for j in range(4):
                t = B.open(f"mv{j}", "act")
                B.close(t, mm(t.ps[:, :], ckvT[:, P * j:P * j + P], wv, True, True))
            done_with("w_ukv")
            w = use("w_uq")

            def queries(h):
                t = B.open(f"mq{h}", "act")
                for i in range(2):
                    for kt in range(2):
                        last = mm(t.ps[0:96, SEQ * i:SEQ * i + SEQ], w[:, kt, 96 * (h + i):96 * (h + i) + 96], cqT[:, kt, :], kt == 0, kt == 1)
                B.close(t, last)

            queries(0)
            for h in range(0, 8, 2):
                if h < 6:
                    queries(h + 2)
                if h == 4:
                    done_with("w_uq")
                wait_took(pe, f"mq{h}")
                t = B.open(f"mqr{h}", "dve")
                B.close(t, mm(t.ps[0:96, :], ODD("mla_swap")[0:96, 0:96], q_raw[h // 2 % 2][0:96, :], True, True))
            wait_took(pe, "mv3")
            pe.wait_ge(kr_copied, 1)

            def m_scores(u):
                j, h = u // 8, u % 8
                if u < 8 and u % 2 == 0:
                    wait_took(pe, f"mqr{u}")
                t = B.open(f"ms{u}", "act")
                B.close(t, mm(t.ps[:, :], mq[0:96, h, P * j:P * j + P], mk[0:96, h, :], True, True))

            m_scores(0)
            m_scores(1)
            for u in range(16):
                if u + 2 < 16:
                    m_scores(u + 2)
                wait_took(pe, f"ms{u}")
                probs_T("m", u, probs1[u % 3], 0)
                if u:
                    attend("m", u - 1, 8, 64, mv_tok, (u - 1) // 8, (u - 1) % 8, att_T21)
            attend("m", 15, 8, 64, mv_tok, 1, 7, att_T21)
            for hp in range(2):
                t = B.open(f"rs{hp}", "act")
                for i in range(2):
                    h = 2 * hp + i
                    for q in range(2):
                        pe.wait_ge(rkw_done, 2 * h + q + 1)
                        last = mm(t.ps[:, SEQ * i:SEQ * i + SEQ], rk_tok[:, q, P * hp:P * hp + P], rvw_all[:, h, q, :], q == 0, q == 1)
                B.close(t, last)
            pe.wait_ge(rq_done, 1)
            wait_took(pe, "rs1")
            ro = [B.open(f"ro{j}", "dve") for j in range(2)]

            def r_scores(h):
                t = B.open(f"rsc{h}", "dve")
                for q in range(2):
                    last = mm(t.ps[:, SEQ * q:SEQ * q + SEQ], rk_fm[:, h // 2, P * q:P * q + P], rqz[:, h, :], True, True)
                B.close(t, last)

            r_scores(0)
            for h in range(4):
                if h + 1 < 4:
                    r_scores(h + 1)
                wait_took(pe, f"rsc{h}")
                for j in range(2):
                    o = ro[j].ps[:, P * h:P * h + P]
                    s3 = ret_s2[h % 2]
                    for q in range(2):
                        mm(o, s3[:, q, P * j:P * j + P], rv_tok[:, q, P * h:P * h + P], q == 0, False)
                    mm(o, rqf[:, h, P * j:P * j + P], ret_state[:, h, 0:P], False, False)
                    last = mm(o, rqb[:, h, P * j:P * j + P], ret_state[:, h, P:2 * P], False, True)
                    if h == 3:
                        B.close(ro[j], last)
            pe.wait_ge(att_done, 6)
            for kt in range(KT):
                t = B.open(f"bT{kt}", "dve" if kt % 2 else "act")
                for j in range(2):
                    last = tr(t.ps[:, P * j:P * j + P], att1[:, j, P * kt:P * kt + P])
                B.close(t, last)
            wait_took(pe, "bT7")
            wait_took(pe, "bT6")
            project_out(["odd_out0", "odd_out1"], attT1, 2, 8, "o3_")
            route(1)
            experts(1)
        @block.vector
        def _(dve):
            V = nc.vector

            def settle():
                dve.drain()

            def scaled(o, i, s1, s2, op0, op1):
                return V.tensor_scalar(o, i, s1, s2, op0, op1)

            def pow_wait(name):
                dve.wait_ge(rstd_done, POW.index(name) + 1)

            def ada_rows(k):
                ps = arrive(dve, f"row{k}")
                took(f"row{k}", V.tensor_copy(ada_row[k % 2], ps[:, :]))

            def ada_outs(k):
                kind, v, half = ada_kind(k)
                s = ADA[k][0]
                l = s - 1
                ps = arrive(dve, f"col{k}")
                if kind == "col":
                    took(f"col{k}", V.tensor_copy(ada_col[s][:, v, 8 * half:8 * half + 8], ps[:, 0:8]))
                elif kind == "ffn":
                    w = 512 if l == 0 else 256
                    took(f"col{k}", V.tensor_copy(gate_ffn[l][64 * half:64 * half + 64, :], ps[64 * half:64 * half + 64, 0:w]))
                else:
                    dst = gate_1 if s == 0 else gate_mix[l][:, 0, :]
                    took(f"col{k}", V.tensor_copy(dst[:, 512 * half:512 * half + 512], ps[:, :]))
                    if kind == "mix" and l == 0:
                        ps = arrive(dve, f"col{k}c")
                        took(f"col{k}c", V.tensor_copy(gate_mix[l][:, 1, 512 * half:512 * half + 512], ps[:, :]))

            def gains(n):
                s, v = NORM_B[n]
                gain = {0: G("norm_w"), 2: G("norm_mix")[:, 0:8], 3: G("norm_ffn")[:, 0:8], 4: G("norm_mix")[:, 8:16], 5: G("norm_ffn")[:, 8:16]}[n]
                sc = ada_col[s][:, v + 1, :].rearrange("p (k i) -> p k i", i=2)
                o = norm_a[:, NORM_A[n], :].rearrange("p (k i) -> p k i", i=2)
                return V.scalar_tensor_tensor(out=o, in0=sc, scalar=1.0, in1=gain.unsqueeze(2).to_broadcast([P, KT, 2]), op0=ALU.add, op1=ALU.mult)

            def mean_squares(n):
                T = NORM_TILES[n]
                dve.wait_ge(sums_done, NORM_SUM[n])
                scaled(meansq[:, 0:T], ssq[:, 0:T], 1.0 / D, EPS, ALU.mult, ALU.add).then_inc(ms_done, 1)
                pow_wait(f"norm{n}")

            def norm_rows(n):
                mean_squares(n)
                for j in range(NORM_TILES[n]):
                    V.tensor_scalar(xn[:, j, :], xres[:, j, :], rstd[:, j:j + 1], None, ALU.mult).then_inc(xn_done, 1)

            def modulate(n, name, kt, o, T=None):
                ps = arrive(dve, name)
                s, v = NORM_B[n]
                for i in range((NORM_TILES[n] if T is None else T) // 2):
                    last = scaled(o[:, kt, SEQ * i:SEQ * i + SEQ], ps[:, SEQ * i:SEQ * i + SEQ], norm_a[:, NORM_A[n], 2 * kt + i:2 * kt + i + 1],
                                  ada_col[s][:, v, 2 * kt + i:2 * kt + i + 1], ALU.mult, ALU.add)
                took(name, last)

            def norm_T(n):
                for kt in range(0, KT, 2):
                    modulate(n, f"nT{n}.{kt}", kt, hT)

            dve.wait_ge(consts_in, 16 * N_CONST_DMAS)
            lam_p = R("diff_lambda")
            for i in range(2):
                V.tensor_tensor_reduce(y_t[i][:, 0:64], lam_p[:, 128 * i:128 * i + 64], lam_p[:, 128 * i + 64:128 * i + 128], 1.0, 0.0,
                                       ALU.mult, ALU.add, lam_b[:, i:i + 1]).then_inc(lam_sum, 1)
            for k in range(4):
                ada_rows(k)
                if k:
                    ada_outs(k - 1)
                if k == 2:
                    norm_rows(0)
            ada_outs(3)
            settle()
            gains(0).then_inc(gain0_done, 1)
            dve.wait_ge(lam_exp, 1)
            V.tensor_tensor(lam_b[:, 0:1], lam_b[:, 3:4], lam_b[:, 2:3], ALU.subtract)
            settle()
            V.tensor_scalar(lam_b[:, 0:1], lam_b[:, 0:1], -LAM_INIT, None, ALU.add)
            norm_T(0)
            ps = arrive(dve, "dt")
            took("dt", V.tensor_tensor(dt_z, ps[:, 0:192].rearrange("p (a b) -> p a b", b=48), R("dt_bias").unsqueeze(1).to_broadcast([P, 4, 48]), ALU.add))
            settle()
            V.scalar_tensor_tensor(out=dt_a, in0=dt_z, scalar=-1.0, in1=dt_z, op0=ALU.mult, op1=ALU.max).then_inc(dt_abs, 1)
            dve.wait_ge(dt_log, 1)
            V.scalar_tensor_tensor(out=dt_v, in0=dt_z, scalar=0.0, in1=dt_a, op0=ALU.max, op1=ALU.add)
            settle()
            dve.wait_ge(a_exp, 1)
            V.scalar_tensor_tensor(out=a_dt, in0=dt_v, scalar=-1.0, in1=exp_alog.unsqueeze(1).to_broadcast([P, 4, 48]), op0=ALU.mult, op1=ALU.mult).then_inc(a_ready, 1)
            for j in range(2):
                for h in range(2):
                    ps = arrive(dve, f"fa{j}{h}")
                    took(f"fa{j}{h}", V.tensor_copy(dft_a[:, j, 2 * h:2 * h + 2, :], ps.rearrange("p (a b) -> p a b", b=256)))
            for h in range(2):
                ps = arrive(dve, f"fm{h}")
                took(f"fm{h}", V.tensor_copy(mixedT[:, 2 * h:2 * h + 2, :], ps.rearrange("p (a b) -> p a b", b=SEQ)))
            for m in range(4):
                ps = arrive(dve, f"four{m}")
                took(f"four{m}", V.scalar_tensor_tensor(out=mixT[:, m, :], in0=ps[:, 0:SEQ], scalar=G("b_four")[:, m:m + 1], in1=zfT[:, m, :],
                                                        op0=ALU.add, op1=ALU.mult))
            ada_rows(4)
            ada_rows(5)
            ada_outs(4)
            ada_outs(5)
            ps = arrive(dve, "cumT")
            dve.wait_ge(pool_zero, 3)
            took("cumT", V.tensor_copy(cumT[0:24], ps[0:24, :].rearrange("p (a b) -> p a b", b=SEQ)))
            ps = arrive(dve, "cum_col")
            took("cum_col", V.tensor_copy(cum_col, ps[:, 0:192].rearrange("p (a b) -> p a b", b=48)))
            settle()
            V.tensor_tensor(dt_z[:, 0:2, :], cum_col[:, 2:4, :], a_dt[:, 2:4, :], ALU.subtract).then_inc(ctx_arg, 1)
            dve.wait_ge(ctx_exp, 1)
            V.tensor_tensor(w_ctx, dt_z[:, 0:2, :], dt_v[:, 2:4, :], ALU.mult).then_inc(ctx_w, 1)
            for j in range(CONV_TILES):
                wait_took(dve, f"conv{j}")
                if j >= 2:
                    dve.wait_ge(act_conv, j - 1)
                w = G("conv_w")[:, 9 * j:9 * j + 9]
                acc = conv_acc[j % 2]
                xa, ca = acc[:, 0:SEQ].rearrange("p (r c) -> p r c", c=GRID_W), acc[:, SEQ:TOK]
                xp, cp = xpad[j % 2], cpad[j % 2]
                for tap in range(9):
                    dr, dc = tap // 3, tap % 3
                    src = xp[:, dr:dr + ROWS, dc:dc + GRID_W]
                    ctx_tap = 3 + tap if tap < 3 and j < 16 else None
                    if tap == 0:
                        last = V.tensor_scalar(xa, src, w[:, 0:1], None, ALU.mult)
                        if ctx_tap is not None:
                            V.tensor_scalar(ca, cp[:, 0:SEQ], w[:, 3:4], None, ALU.mult)
                    else:
                        settle()
                        if ctx_tap is not None:
                            V.scalar_tensor_tensor(out=ca, in0=cp[:, tap:tap + SEQ], scalar=w[:, 3 + tap:4 + tap], in1=ca, op0=ALU.mult, op1=ALU.add)
                        last = V.scalar_tensor_tensor(out=xa, in0=src, scalar=w[:, tap:tap + 1], in1=xa, op0=ALU.mult, op1=ALU.add)
                last.then_inc(conv_done, 1)
            for g in range(GROUPS):
                ps = arrive(dve, f"cb{g}")
                for q in range(2):
                    lo, hi = (0, SEQ) if q == 0 else (P, SEQ)
                    V.tensor_tensor(cb[:, g, q, 0:hi - lo], ps[:, SEQ * q + lo:SEQ * q + hi], tri_f[:, q, lo:hi], ALU.mult)
                    at = hi - lo
                    lo, hi = (0, P) if q == 0 else (0, SEQ)
                    last = V.tensor_tensor(cb[:, g, q, at:384], ps[:, SEQ * q + lo:SEQ * q + hi], tri_b[:, q, lo:hi], ALU.mult)
                took(f"cb{g}", last)

            def decay_args(h):
                ps = arrive(dve, f"bc{h}")
                d = dec_arg[h % 2]
                f0, f1 = cum_col[:, 0, h:h + 1], cum_col[:, 1, h:h + 1]
                b0, b1 = cum_col[:, 0, 24 + h:25 + h], cum_col[:, 1, 24 + h:25 + h]
                scaled(d[:, 0, 0:256], ps[:, 0:256], f0, 0.0, ALU.subtract, ALU.min)
                scaled(d[:, 0, 256:384], ps[:, 256:384], b0, 0.0, ALU.subtract, ALU.min)
                scaled(d[:, 1, 0:128], ps[:, 128:256], f1, 0.0, ALU.subtract, ALU.min)
                took(f"bc{h}", scaled(d[:, 1, 128:384], ps[:, 256:512], b1, 0.0, ALU.subtract, ALU.min))

            def mixing(h):
                dve.wait_ge(decay_out, h + 1)
                e, m, g = dec_exp[h % 2], m_mat[h % 2], h // HPG
                stt = lambda o, i, s, c: V.scalar_tensor_tensor(out=o, in0=i, scalar=s, in1=c, op0=ALU.mult, op1=ALU.mult)
                stt(m[:, 0, :], e[:, 0, 0:256], dt_v[:, 0, h:h + 1], cb[:, g, 0, 0:256])
                stt(m[:, 1, :], e[:, 1, 128:384], dt_v[:, 1, 24 + h:25 + h], cb[:, g, 1, 128:384])
                stt(e[:, 0, 256:384], e[:, 0, 256:384], dt_v[:, 0, 24 + h:25 + h], cb[:, g, 0, 256:384])
                stt(e[:, 1, 0:128], e[:, 1, 0:128], dt_v[:, 1, h:h + 1], cb[:, g, 1, 0:128])
                settle()
                V.tensor_tensor(m[:, 0, 0:128], m[:, 0, 0:128], e[:, 0, 256:384], ALU.add)
                V.tensor_tensor(m[:, 1, 128:256], m[:, 1, 128:256], e[:, 1, 0:128], ALU.add).then_inc(m_ready, 1)

            by_head = lambda a: a.rearrange("p (h c) -> p h c", c=64)

            def group_out(g):
                if g == 0:
                    dve.wait_ge(x_ecum, 1)
                dve.wait_ge(y_skip, g + 1)
                for l in range(2):
                    ps = arrive(dve, f"y{g}{l}")
                    took(f"y{g}{l}", V.tensor_tensor(y_acc[l], ps[:, 0:GW], y_acc[l], ALU.add))
                for l in range(2):
                    for d in range(2):
                        ps = arrive(dve, f"off{g}{l}{d}")
                        took(f"off{g}{l}{d}", V.tensor_tensor(by_head(off_t[l][d]), by_head(ps[:, 0:GW]),
                             x_dec[:, l, 24 * d + HPG * g:24 * d + HPG * g + HPG].unsqueeze(2).to_broadcast([P, HPG, 64]), ALU.mult))

            decay_args(0)
            decay_args(1)
            for h in range(HEADS):
                mixing(h)
                if h + 2 < HEADS:
                    decay_args(h + 2)
                if h in ADA_AT_HEAD:
                    ada_rows(ADA_AT_HEAD[h])
                    if h:
                        ada_outs(ADA_AT_HEAD[h] - 1)
                if h % HPG == HPG - 1:
                    group_out(h // HPG)
            for k in range(ADA_LEFT, 26):
                ada_rows(k)
                ada_outs(k - 1)
            settle()
            for n in (2, 3, 4):
                gains(n)
            for m in range(0, 12, 2):
                ps = arrive(dve, f"gT{m}")
                took(f"gT{m}", V.tensor_scalar(mixT[:, 4 + m, :], ps[:, 0:SEQ], G("ssd_norm")[:, m:m + 1], None, ALU.mult))

            def residual(tag, T, gate):
                for i in range(2 * T):
                    j, n = i // 2, i % 2
                    ps = arrive(dve, f"{tag}{j}{n}")
                    took(f"{tag}{j}{n}", V.tensor_tensor(res_t[i % 4], ps[:, :], gate(j)[:, 512 * n:512 * n + 512], ALU.mult))
                    settle()
                    x = xres[:, j, 512 * n:512 * n + 512]
                    V.tensor_tensor(x, x, res_t[i % 4], ALU.add).then_inc(res_done, 1)

            residual("o1_", 2, lambda j: gate_1)
            ada_rows(26)
            ada_outs(25)
            mean_squares(1)
            dve.wait_ge(arena_in["gain1"], 16)
            for j in range(2):
                V.scalar_tensor_tensor(out=xres[:, j, :], in0=xres[:, j, :], scalar=rstd[:, j:j + 1], in1=gain_1, op0=ALU.mult, op1=ALU.mult).then_inc(xn_done, 1)
            for k in range(27, 30):
                ada_rows(k)
                ada_outs(k - 1)
            ada_outs(29)
            settle()
            gains(5)

            norm_rows(2)
            norm_T(2)
            dve.wait_ge(arena_in["rope"], 16)
            dve.wait_ge(pool_zero, 4)
            for i in range(8):
                name, m = "qk"[i // 4], i % 4
                ps = arrive(dve, f"{name}r{m}")
                raw, t = rope_raw[m % 2][:, 0:SEQ], rope_t[m % 2]
                V.tensor_tensor(t, ps[:, 0:SEQ], ROPE("rope_sin"), ALU.mult)
                V.tensor_tensor(raw, raw, ROPE("rope_cos"), ALU.mult)
                settle()
                if name == "q":
                    V.tensor_tensor(qz[0][0:64, m, 0:SEQ], raw[0:64], t[0:64], ALU.add)
                    last = V.tensor_tensor(qz[1][64:128, m, 0:SEQ], raw[64:128], t[64:128], ALU.add)
                else:
                    last = V.tensor_tensor(k_fm[:, m, 0:SEQ], raw, t, ALU.add)
                took(f"{name}r{m}", last)
                settle()

            def d_max(u):
                n0 = 0 if u < 8 else SEQ
                for c in range(2):
                    i = 2 * (u % 3) + c
                    ps = arrive(dve, f"ds{u}{'ab'[c]}")
                    V.tensor_reduce(a_mx[:, i:i + 1], ps[:, n0:TOK], AX, ALU.max)
                    settle()
                    V.tensor_scalar(a_neg[:, i:i + 1], a_mx[:, i:i + 1], -NA_SCALE, None, ALU.mult).then_inc(neg_max, 1)

            def combine(u):
                n0 = 0 if u < 8 else SEQ
                wait_took(dve, f"ds{u}b")
                i = 2 * (u % 3)
                p0, p1 = probs[u % 3][0][:, n0:TOK], probs[u % 3][1][:, n0:TOK]
                V.reciprocal(a_rec[:, i:i + 2], a_sum[:, i:i + 2])
                settle()
                scaled(p1, p1, a_rec[:, i + 1:i + 2], lam_b[:, 0:1], ALU.mult, ALU.mult)
                settle()
                V.scalar_tensor_tensor(out=p0, in0=p0, scalar=a_rec[:, i:i + 1], in1=p1, op0=ALU.mult, op1=ALU.add).then_inc(comb_done, 1)

            def head_square(o, j, width, first, n):
                V.tensor_tensor(sq_t[:, 0:n * width], o, o, ALU.mult)
                settle()
                V.tensor_reduce(d_ss[:, first:first + n], sq_t[:, 0:n * width].rearrange("p (h c) -> p h c", c=width), AX, ALU.add)

            def d_out(j):
                ps = arrive(dve, f"do{j}")
                took(f"do{j}", V.tensor_copy(att[:, j, 0:512], ps[:, :]))
                settle()
                head_square(att[:, j, 0:512], j, P, 4 * j, 4)
                settle()

            wait_took(dve, "nv3")
            d_max(0)
            d_max(1)
            for u in range(16):
                combine(u)
                if u % 4 == 1 and u > 4:
                    d_out(u // 4 - 1)
                if u + 2 < 16:
                    d_max(u + 2)
            d_out(3)
            scaled(d_ms, d_ss, 1.0 / P, EPS, ALU.mult, ALU.add).then_inc(ms_done, 1)
            dve.wait_ge(na_masked, 1)

            def n_max(u):
                j, h = u // 8, u % 8
                ps = arrive(dve, f"ns{u}")
                i = u % 4
                if j < 2:
                    s = na_p_buf[i]
                    V.scalar_tensor_tensor(out=s[:, 0:SEQ], in0=ps[:, 0:SEQ], scalar=NA_SCALE, in1=na_bias[:, h, P - P * j:P - P * j + SEQ], op0=ALU.mult, op1=ALU.add)
                    took(f"ns{u}", V.tensor_scalar(s[:, SEQ:TOK], ps[:, SEQ:TOK], NA_SCALE, None, ALU.mult))
                    settle()
                    V.tensor_reduce(n_mx[:, i:i + 1], s, AX, ALU.max)
                else:
                    V.tensor_reduce(n_mx[:, i:i + 1], ps[:, SEQ:TOK], AX, ALU.max)
                settle()
                V.tensor_scalar(n_neg[:, i:i + 1], n_mx[:, i:i + 1], -1.0 if j < 2 else -NA_SCALE, None, ALU.mult).then_inc(na_neg, 1)

            def head_norm(name, j, o):
                ps = arrive(dve, name)
                i = 8 * (j % 2)
                V.reciprocal(n_rec[:, i:i + 8], n_sum[:, i:i + 8])
                settle()
                took(name, V.tensor_tensor(by_head(o), by_head(ps[:, :]), n_rec[:, i:i + 8].unsqueeze(2).to_broadcast([P, 8, 64]), ALU.mult))

            n_max(0)
            n_max(1)
            pow_wait("diff")
            for u in range(32):
                if u % 8 == 1 and u > 8:
                    head_norm(f"no{u // 8 - 1}", u // 8 - 1, att[:, u // 8 - 1, 512:1024])
                if u + 2 < 32:
                    if u >= 2:
                        dve.wait_ge(mm_done, tiles[f"nT{u - 2}"].no)
                    n_max(u + 2)
                if u in (18, 20, 22, 24):
                    j = (u - 18) // 2
                    o = att[:, j, 0:512].rearrange("p (h c) -> p h c", c=P)
                    V.tensor_tensor(o, o, d_ss[:, 4 * j:4 * j + 4].unsqueeze(2).to_broadcast([P, 4, P]), ALU.mult).then_inc(att_done, 1)
            head_norm("no3", 3, att[:, 3, 512:1024])
            for kt in range(4):
                ps = arrive(dve, f"aT{kt}")
                took(f"aT{kt}", scaled(attT[:, kt, :], ps[:, :], G("subln")[:, 0:1], 1.0 - LAM_INIT, ALU.mult, ALU.mult))
            residual("o2_", 4, lambda j: gate_mix[0][:, j // 2, :])

            def route(l):
                n, T = (3, 4) if l == 0 else (5, 2)
                settle()
                norm_rows(n)
                norm_T(n)
                three = lambda a: a[:, 0:T, :]
                ps = arrive(dve, f"rl{l}")
                lg = ps[:, 0:EXPERTS * T].rearrange("p (a b) -> p a b", b=EXPERTS)
                V.tensor_reduce(rt_mx[:, 0:T, 0], lg, AX, ALU.max)
                settle()
                took(f"rl{l}", V.tensor_tensor(three(rt_t), lg, rt_mx[:, 0:T, :].to_broadcast([P, T, EXPERTS]), ALU.subtract))
                dve.wait_ge(rt_exp, l + 1)
                V.tensor_reduce(rt_sum[:, 0:T, 0], three(aff), AX, ALU.add)
                settle()
                V.reciprocal(rt_mx[:, 0:T, :], rt_sum[:, 0:T, :])
                settle()
                V.tensor_tensor(three(aff), three(aff), rt_mx[:, 0:T, :].to_broadcast([P, T, EXPERTS]), ALU.mult).then_inc(aff_done, 1)
                ps = arrive(dve, f"affT{l}")
                n_rows = 16 * T - 16
                if l == 0:
                    for r0 in (0, 32):
                        last = V.tensor_copy(aff_work[r0:r0 + EXPERTS, :], ps[r0:r0 + EXPERTS, 0:SEQ])
                else:
                    last = V.tensor_copy(aff_work[0:EXPERTS, :], ps[0:EXPERTS, 0:SEQ])
                took(f"affT{l}", last)
                wk = aff_work[0:n_rows, :]
                for i in range(CAP // 8):
                    settle()
                    V.max(top8[i][0:n_rows, :], wk)
                    settle()
                    V.match_replace(wk, top8[i][0:n_rows, :], wk, -1.0)
                settle()
                V.tensor_scalar(sel_e[0:n_rows, :], wk, 0.0, None, ALU.is_lt).then_inc(topk_done, 1)
                ps = arrive(dve, f"selT{l}")
                took(f"selT{l}", V.tensor_copy(three(sel_t), ps[:, 0:EXPERTS * T].rearrange("p (a b) -> p a b", b=EXPERTS)))
                settle()
                ps = arrive(dve, f"pos{l}")
                took(f"pos{l}", V.tensor_tensor(three(slot_t), ps[:, 0:EXPERTS * T].rearrange("p (a b) -> p a b", b=EXPERTS), three(sel_t), ALU.mult))
                settle()
                grid = [P, EXPERTS, CAP]
                cube = lambda a: a.rearrange("p (e s) -> p e s", s=CAP)
                for j in range(T):
                    last = V.tensor_tensor(cube(d_sel[l][:, j, :]), C("iota").unsqueeze(1).to_broadcast(grid), slot_t[:, j, :].unsqueeze(2).to_broadcast(grid), ALU.is_equal)
                last.then_inc(d_done, 1)
                settle()
                for j in range(T):
                    V.tensor_tensor(cube(d_gate[:, j, :]), cube(d_sel[l][:, j, :]), aff[:, j, :].unsqueeze(2).to_broadcast(grid), ALU.mult)
                for kt in range(KT):
                    for s in range(T // 2):
                        if (kt + s) % 2 == 0:
                            name = f"ga{l}.{kt}{s}"
                            ps = arrive(dve, name)
                            took(name, gathered(V, l, kt, s, ps))

            def gathered(V, l, kt, s, ps):
                n = 3 if l == 0 else 5
                sh, v = NORM_B[n]
                return scaled(xe_rows(l, kt, s), ps.rearrange("p (e s) -> p e s", s=CAP), norm_a[:, NORM_A[n], 2 * kt + s:2 * kt + s + 1],
                              ada_col[sh][:, v, 2 * kt + s:2 * kt + s + 1], ALU.mult, ALU.add)

            def experts(l):
                n_grp = 2 if l == 0 else 4
                S, W, T = P // n_grp, FF // n_grp, 4 if l == 0 else 2
                with nc.vector.Fori(0, EXPERTS // n_grp) as it:
                    for e in range(n_grp):
                        dve.wait_ge(silu_ready[l], it * n_grp + (e + 1))
                        dve.wait_ge(moe_used[l], it * (6 * n_grp) + (6 * e + 4))
                        V.tensor_tensor(hid[:, 0:W], silu_h[:, 0:W], bank[1][:, 0:W], ALU.mult).then_inc(hid_ready[l], 1)
                        dve.wait_ge(moe_used[l], it * (6 * n_grp) + (6 * e + 6))
                        for g in range(n_grp):
                            last = V.tensor_tensor(y_sb[S * e:S * e + S, W * g:W * g + W], bank[3][S * g:S * g + S, 0:W],
                                                   gate_ffn[l][S * g:S * g + S, :], ALU.mult)
                        last.then_inc(y_ready[l], 1)
                    for i in range(2 * T):
                        dve.wait_ge(scat_mm[l], it * (2 * T) + (i + 1))
                        x = xres[:, i // 2, 512 * (i % 2):512 * (i % 2) + 512]
                        V.tensor_tensor(x, x, bank[5 + i % 3][:, :], ALU.add).then_inc(acc_done[l], 1)

            route(0)
            experts(0)

            lg, lgt = small[:, 0:8], small[:, 8:16]
            V.scalar_tensor_tensor(out=lgt, in0=R("ret_decay"), scalar=-1.0, in1=R("ret_decay"), op0=ALU.mult, op1=ALU.max).then_inc(lg_abs, 1)
            dve.wait_ge(lg_ln, 1)
            V.scalar_tensor_tensor(out=lg, in0=R("ret_decay"), scalar=0.0, in1=lgt, op0=ALU.min, op1=ALU.subtract).then_inc(lg_done, 1)
            settle()
            norm_rows(4)
            norm_T(4)
            lat_ss, lat_ms = small[:, 64:72], small[:, 80:88]
            for j in range(4):
                ps = arrive(dve, f"lat{j}")
                c0 = 0 if j < 2 else 256
                took(f"lat{j}", V.tensor_copy(c_lat[:, j, c0:384], ps[:, c0:384]))
                settle()
                if j < 2:
                    V.tensor_tensor_reduce(probs1[0][:, 0:256], c_lat[:, j, 0:256], c_lat[:, j, 0:256], 1.0, 0.0, ALU.mult, ALU.add, lat_ss[:, j:j + 1])
                V.tensor_tensor_reduce(probs1[1][:, 0:128], c_lat[:, j, 256:384], c_lat[:, j, 256:384], 1.0, 0.0, ALU.mult, ALU.add, lat_ss[:, 2 + j:3 + j])
                settle()
            scaled(lat_ms[:, 0:2], lat_ss[:, 0:2], 1.0 / 256, EPS, ALU.mult, ALU.add)
            scaled(lat_ms[:, 2:6], lat_ss[:, 2:6], 1.0 / 128, EPS, ALU.mult, ALU.add).then_inc(ms_done, 1)
            pow_wait("lat")
            for j in range(2):
                V.tensor_scalar(c_lat[:, j, 0:256], c_lat[:, j, 0:256], lat_ss[:, j:j + 1], None, ALU.mult)
            for j in range(4):
                last = V.tensor_scalar(c_lat[:, j, 256:384], c_lat[:, j, 256:384], lat_ss[:, 2 + j:3 + j], None, ALU.mult)
            last.then_inc(q_ready, 1)
            dve.wait_ge(arena_in["odd_tables"], 16)
            for h in range(4):
                V.tensor_scalar(ret_d[:, h, :], ODD("ret_bwd"), lg[:, 4 + h:5 + h], None, ALU.mult)
                settle()
                V.scalar_tensor_tensor(out=ret_d[:, h, :], in0=ODD("ret_fwd"), scalar=lg[:, h:h + 1], in1=ret_d[:, h, :], op0=ALU.mult, op1=ALU.add).then_inc(ret_arg, 1)
            ps = arrive(dve, "krot")
            t = probs1[0][64:96, 0:SEQ]
            kx = kr_raw[64:96, 0:SEQ]
            V.tensor_tensor(t, ps[64:96, 0:SEQ], ODD("mla_sin")[64:96], ALU.mult)
            V.tensor_tensor(kx, kx, ODD("mla_cos")[64:96], ALU.mult)
            settle()
            took("krot", V.tensor_tensor(kx, kx, t, ALU.add))
            for m in range(2):
                ps = arrive(dve, f"cqT{m}")
                took(f"cqT{m}", V.tensor_scalar(cqT[:, m, :], ps[:, 0:SEQ], G("q_norm")[:, m:m + 1], None, ALU.mult))
            ps = arrive(dve, "ckvT")
            took("ckvT", V.tensor_scalar(ckvT, ps[:, :], G("kv_norm")[:, 0:1], None, ALU.mult))
            two = lambda a: a.rearrange("p (h c) -> p h c", c=SEQ)
            for h in range(0, 8, 2):
                ps = arrive(dve, f"mqr{h}")
                tab = lambda n: ODD(n)[0:96].unsqueeze(1).to_broadcast([96, 2, SEQ])
                t, raw = q_rot[h // 2 % 2][0:96], q_raw[h // 2 % 2][0:96]
                V.tensor_tensor(two(t), two(ps[0:96, :]), tab("mla_sin"), ALU.mult)
                V.tensor_tensor(two(raw), two(raw), tab("mla_cos"), ALU.mult)
                settle()
                took(f"mqr{h}", V.tensor_tensor(mq[0:96, h:h + 2, :], two(raw), two(t), ALU.add))
            def m_max(u):
                i = u % 3
                ps = arrive(dve, f"ms{u}")
                V.tensor_reduce(m_mx[:, i:i + 1], ps[:, :], AX, ALU.max)
                settle()
                V.tensor_scalar(m_ng[:, i:i + 1], m_mx[:, i:i + 1], -MLA_SCALE, None, ALU.mult).then_inc(m_neg, 1)

            def m_norm(name, j):
                ps = arrive(dve, name)
                V.reciprocal(m_rec[:, 8 * j:8 * j + 8], m_sum[:, 8 * j:8 * j + 8])
                settle()
                took(name, V.tensor_tensor(by_head(att1[:, j, 0:512]), by_head(ps[:, :]), m_rec[:, 8 * j:8 * j + 8].unsqueeze(2).to_broadcast([P, 8, 64]), ALU.mult))

            def retention_inputs():
                dve.wait_ge(ret_qdec, 8)
                ages = small[:, 24:40].rearrange("p (h d q) -> p h d q", d=2, q=2)
                wait_took(dve, "rv3")
                dve.wait_ge(mm_done, tiles["rg1"].no)
                for h in range(4):
                    for q in range(2):
                        for d in range(2):
                            last = scaled(rvw_all[:, h, q, P * d:P * d + P], rv_tok[:, 2 + q, P * h:P * h + P], ages[:, h, d, q:q + 1], 0.125, ALU.mult, ALU.mult)
                        last.then_inc(rkw_done, 1)
                for h in range(4):
                    V.tensor_tensor(rqf[:, h, :], rqf[:, h, :], rqz[:, h, :], ALU.mult)
                    last = V.tensor_tensor(rqb[:, h, :], rqb[:, h, :], rqz[:, h, :], ALU.mult)
                last.then_inc(rq_done, 1)

            m_max(0)
            m_max(1)
            for u in range(16):
                if u == 10:
                    retention_inputs()
                if u + 2 < 16:
                    if u >= 1:
                        wait_took(dve, f"ms{u - 1}")
                    if u == 9:
                        m_norm("mo0", 0)
                    m_max(u + 2)
            m_norm("mo1", 1)
            dve.wait_ge(ret_tab, 4)
            for h in range(4):
                ps = arrive(dve, f"rsc{h}")
                took(f"rsc{h}", V.scalar_tensor_tensor(out=ret_s2[h % 2].rearrange("p a b -> p (a b)"), in0=ps[:, :], scalar=0.125, in1=ret_d[:, h, :], op0=ALU.mult, op1=ALU.mult))
            for j in range(2):
                ps = arrive(dve, f"ro{j}")
                took(f"ro{j}", V.tensor_copy(att1[:, j, 512:1024], ps[:, :]))
            settle()
            for j in range(2):
                V.tensor_tensor(probs1[j], att1[:, j, 512:1024], att1[:, j, 512:1024], ALU.mult)
            settle()
            for j in range(2):
                V.tensor_reduce(lat_ss[:, 4 * j:4 * j + 4], probs1[j].rearrange("p (h c) -> p h c", c=P), AX, ALU.add)
            settle()
            scaled(lat_ms, lat_ss, 1.0 / P, EPS, ALU.mult, ALU.add).then_inc(ms_done, 1)
            pow_wait("ret")
            wait_took(dve, "rg1")
            for j in range(2):
                o = att1[:, j, 512:1024].rearrange("p (h c) -> p h c", c=P)
                V.tensor_tensor(o, o, lat_ss[:, 4 * j:4 * j + 4].unsqueeze(2).to_broadcast([P, 4, P]), ALU.mult)
            settle()
            for j in range(2):
                o = att1[:, j, 512:1024]
                V.tensor_tensor(o, o, rg_tok[:, j, :], ALU.mult).then_inc(att_done, 1)
            for kt in range(1, KT, 2):
                ps = arrive(dve, f"bT{kt}")
                took(f"bT{kt}", V.tensor_copy(attT1[:, kt, :], ps[:, 0:SEQ]))
            residual("o3_", 2, lambda j: gate_mix[1][:, 0, :])
            route(1)
            experts(1)
            settle()
            mean_squares(6)
            dve.wait_ge(arena_in["gain2"], 16)
            for j in range(2):
                V.scalar_tensor_tensor(out=xres[:, j, :], in0=xres[:, j, :], scalar=rstd[:, j:j + 1], in1=gate_1, op0=ALU.mult, op1=ALU.mult).then_inc(out_ready, 1)

        @block.scalar
        def _(act):
            S = nc.scalar

            def copy(o, i):
                return S.activation(o, i, ACT.Copy)

            def settle():
                act.drain()

            act.wait_ge(consts_in, 16 * N_CONST_DMAS)
            act.wait_ge(silu_pad, 2)
            for s, name in enumerate(("cvec1", "cvec2")):
                S.activation(silu_c[s][:, :, 0:2], G(name).rearrange("p (k i) -> p k i", i=2), ACT.Silu).then_inc(silu_done, 1)
            S.activation(exp_alog, R("a_log"), ACT.Exp).then_inc(a_exp, 1)
            act.wait_ge(lam_sum, 2)
            S.activation(lam_b[:, 2:4], lam_b[:, 0:2], ACT.Exp).then_inc(lam_exp, 1)

            def squares(n):
                for j in range(NORM_TILES[n]):
                    S.activation(xn[:, j, :], xres[:, j, :], ACT.Square, accum_out=ssq[:, j:j + 1]).then_inc(sums_done, 1)

            def norm_T(n):
                sh, v = NORM_B[n]
                for kt in range(1, KT, 2):
                    ps = arrive(act, f"nT{n}.{kt}")
                    for i in range(NORM_TILES[n] // 2):
                        last = S.activation(hT[:, kt, SEQ * i:SEQ * i + SEQ], ps[:, SEQ * i:SEQ * i + SEQ], ACT.Identity,
                                            scale=norm_a[:, NORM_A[n], 2 * kt + i:2 * kt + i + 1], bias=ada_col[sh][:, v, 2 * kt + i:2 * kt + i + 1])
                    took(f"nT{n}.{kt}", last)

            def take(name, o, i, func=ACT.Copy):
                took(name, S.activation(o, i, func))

            act.wait_ge(x_in, 16)
            act.wait_ge(ctx_in, 16)
            squares(0)
            act.wait_ge(gain0_done, 1)
            norm_T(0)
            act.wait_ge(dt_abs, 1)
            S.activation(dt_a, dt_a, ACT.Exp, scale=-1.0)
            settle()
            S.activation(dt_a, dt_a, ACT.Ln, bias=1.0).then_inc(dt_log, 1)
            for m in range(4):
                take(f"u{m}", uT[:, m, :], arrive(act, f"u{m}")[:, 0:SEQ])
            for m in range(4):
                take(f"zf{m}", zfT[:, m, :], arrive(act, f"zf{m}")[:, 0:SEQ], ACT.Silu)

            wait_took(act, "cum_col")
            S.activation(x_dec, cum_col[:, 0:2, :], ACT.Exp).then_inc(x_ecum, 1)
            act.wait_ge(ctx_arg, 1)
            S.activation(dt_z[:, 0:2, :], dt_z[:, 0:2, :], ACT.Exp).then_inc(ctx_exp, 1)
            act.wait_ge(pool_zero, 2)

            def pad(j):
                ps = arrive(act, f"conv{j}")
                if j >= 2:
                    act.wait_ge(conv_done, j - 1)
                last = copy(xpad[j % 2][:, 1:1 + ROWS, 1:1 + GRID_W], ps[:, 0:SEQ].rearrange("p (r c) -> p r c", c=GRID_W))
                if j < 16:
                    last = copy(cpad[j % 2][:, 1:1 + SEQ], ps[:, SEQ:TOK])
                took(f"conv{j}", last)

            pad(0)
            pad(1)
            for j in range(CONV_TILES):
                act.wait_ge(conv_done, j + 1)
                acc, b = conv_acc[j % 2], G("conv_b")[:, j:j + 1]
                if 2 <= j < 18:
                    act.wait_ge(mm_done, tiles[f"ct{j - 2}"].no)
                if j < 12:
                    S.activation(conv_out[j % 2], acc, ACT.Silu, bias=b).then_inc(act_conv, 1)
                elif j < 16:
                    S.activation(b_fm[:, j - 12, :], acc[:, 0:SEQ], ACT.Silu, bias=b)
                    S.activation(conv_out[j % 2][:, SEQ:TOK], acc[:, SEQ:TOK], ACT.Silu, bias=b).then_inc(act_conv, 1)
                else:
                    S.activation(c_fm[:, j - 16, :], acc[:, 0:SEQ], ACT.Silu, bias=b).then_inc(act_conv, 1)
                if j + 2 < CONV_TILES:
                    pad(j + 2)
                if j < 16:
                    ps = arrive(act, f"ct{j}").rearrange("p (t c) -> p t c", c=P)
                    if j < 12:
                        take(f"ct{j}", xs_tok[:, :, P * j:P * j + P], ps)
                    else:
                        take(f"ct{j}", b_tok[:, :, P * (j - 12):P * (j - 12) + P], ps[:, 2:4, :])
            for i in range(3):
                for j in range(2):
                    take(f"zs{i}{j}", zs[:, j, 512 * i:512 * i + 512], arrive(act, f"zs{i}{j}")[:, :], ACT.Silu)
            for d in range(2):
                for g in range(GROUPS):
                    take(f"hs{d}{g}", h_init[:, d, GW * g:GW * g + GW], arrive(act, f"hs{d}{g}")[:, 0:GW])

            def gated_squares(g):
                act.wait_ge(ssd_z, g + 1)
                for l in range(2):
                    settle()
                    S.activation(sq_junk, zs[:, l, GW * g:GW * g + GW], ACT.Square, accum_out=ssq8[:, 4 * l + g:4 * l + g + 1]).then_inc(ssd_sq, 1)

            for h in range(HEADS):
                wait_took(act, f"bc{h}")
                S.activation(dec_exp[h % 2], dec_arg[h % 2], ACT.Exp).then_inc(decay_out, 1)
                if h >= HPG and h % HPG == 2:
                    gated_squares(h // HPG - 1)
            gated_squares(GROUPS - 1)
            for m in range(1, 12, 2):
                ps = arrive(act, f"gT{m}")
                took(f"gT{m}", S.activation(mixT[:, 4 + m, :], ps[:, 0:SEQ], ACT.Copy, scale=G("ssd_norm")[:, m:m + 1]))
            act.wait_ge(res_done, 4)
            squares(1)

            act.wait_ge(xn_done, NORM_SUM[1])
            act.wait_ge(ctx2_in, 16)
            squares(2)
            norm_T(2)
            act.wait_ge(pool_zero, 4)
            for i in range(8):
                name, m = "qk"[i // 4], i % 4
                ps = arrive(act, f"{name}{m}")
                if i >= 2:
                    prev = "qk"[(i - 2) // 4] + f"r{(i - 2) % 4}"
                    wait_took(act, prev)
                if name == "q":
                    copy(qz[0][0:64, m, SEQ:TOK], ps[0:64, SEQ:TOK])
                    copy(qz[1][64:128, m, SEQ:TOK], ps[64:128, SEQ:TOK])
                else:
                    copy(k_fm[:, m, SEQ:TOK], ps[:, SEQ:TOK])
                take(f"{name}{m}", rope_raw[m % 2][:, 0:SEQ], ps[:, 0:SEQ])
            for j in range(4):
                take(f"v{j}", v_tok[:, j, :], arrive(act, f"v{j}")[:, :])
            for m in range(4):
                ps = arrive(act, f"nq{m}")
                copy(nqz[0][0:64, m, :], ps[0:64, :])
                take(f"nq{m}", nqz[1][64:128, m, :], ps[64:128, :])
            for m in range(4):
                take(f"nk{m}", nk_fm[:, m, :], arrive(act, f"nk{m}")[:, :])
            for j in range(4):
                take(f"nv{j}", nv_tok[:, j, :], arrive(act, f"nv{j}")[:, :])
            wait_took(act, "kr3")

            def d_exp(u):
                n0 = 0 if u < 8 else SEQ
                for c in range(2):
                    i = 2 * (u % 3) + c
                    name = f"ds{u}{'ab'[c]}"
                    act.wait_ge(neg_max, 2 * u + c + 1)
                    ps = tiles[name].ps
                    took(name, S.activation(probs[u % 3][c][:, n0:TOK], ps[:, n0:TOK], ACT.Exp, bias=a_neg[:, i:i + 1], scale=NA_SCALE, accum_out=a_sum[:, i:i + 1]))

            def probs_T(tag, u, T2, x):
                ps = arrive(act, f"{tag}T{u}").rearrange("p (b q) -> p b q", q=P)
                b0 = 0 if x else 2
                take(f"{tag}T{u}", T2[u % 2][:, b0:4, :], ps[:, b0:4, :])

            d_exp(0)
            d_exp(1)
            for u in range(16):
                if u + 2 < 16:
                    d_exp(u + 2)
                probs_T("d", u, att_T2, u < 8)

            def n_exp(u):
                j, h, i = u // 8, u % 8, u % 4
                act.wait_ge(na_neg, u + 1)
                s, total = na_p_buf[i], n_sum[:, 8 * (j % 2) + h:8 * (j % 2) + h + 1]
                if j < 2:
                    S.activation(s, s, ACT.Exp, bias=n_neg[:, i:i + 1], accum_out=total).then_inc(na_p, 1)
                else:
                    ps = tiles[f"ns{u}"].ps
                    took(f"ns{u}", S.activation(s[:, SEQ:TOK], ps[:, SEQ:TOK], ACT.Exp, bias=n_neg[:, i:i + 1], scale=NA_SCALE, accum_out=total))

            n_exp(0)
            n_exp(1)
            for u in range(32):
                if u + 2 < 32:
                    n_exp(u + 2)
                probs_T("n", u, att_T2, u < 16)
            for kt in range(4, 8):
                take(f"aT{kt}", attT[:, kt, :], arrive(act, f"aT{kt}")[:, :])

            def route(l):
                n, T = (3, 4) if l == 0 else (5, 2)
                act.wait_ge(res_done, 12 if l == 0 else 16)
                squares(n)
                norm_T(n)
                wait_took(act, f"rl{l}")
                S.activation(aff[:, 0:T, :], rt_t[:, 0:T, :], ACT.Exp).then_inc(rt_exp, 1)
                sh, v = NORM_B[n]
                for kt in range(KT):
                    for s in range(T // 2):
                        if (kt + s) % 2:
                            name = f"ga{l}.{kt}{s}"
                            ps = arrive(act, name)
                            took(name, S.activation(xe_rows(l, kt, s), ps.rearrange("p (e s) -> p e s", s=CAP), ACT.Identity,
                                                    scale=norm_a[:, NORM_A[n], 2 * kt + s:2 * kt + s + 1], bias=ada_col[sh][:, v, 2 * kt + s:2 * kt + s + 1]))

            def experts(l):
                n_grp = 2 if l == 0 else 4
                W, T = FF // n_grp, 4 if l == 0 else 2
                with nc.scalar.Fori(0, EXPERTS // n_grp) as it:
                    for e in range(n_grp):
                        act.wait_ge(moe_used[l], it * (6 * n_grp) + (6 * e + 2))
                        S.activation(silu_h[:, 0:W], bank[0][:, 0:W], ACT.Silu).then_inc(silu_ready[l], 1)
                        act.wait_ge(hidT_mm[l], it * n_grp + (e + 1))
                        copy(hidT[:, 0:W], bank[2][:, 0:W]).then_inc(hidT_ready[l], 1)
                        if e == 0:
                            act.wait_ge(dT_mm[l], it + 1)
                            copy(dgT[:, 0:P * T], bank[4][:, 0:P * T]).then_inc(dgT_ready[l], 1)

            route(0)
            experts(0)

            act.wait_ge(lg_abs, 1)
            lg, lgt = small[:, 0:8], small[:, 8:16]
            S.activation(lgt, lgt, ACT.Exp, scale=-1.0)
            settle()
            S.activation(lgt, lgt, ACT.Ln, bias=1.0).then_inc(lg_ln, 1)
            act.wait_ge(acc_done[0], 2 * 4 * (EXPERTS // 2))
            squares(4)
            norm_T(4)
            take("krope", kr_raw[64:96, :], arrive(act, "krope")[64:96, :])
            act.wait_ge(pool_zero, 5)
            for m in range(2):
                ps = arrive(act, f"rq{m}")
                copy(rqz[0:64, 2 * m, :], ps[0:64, 0:SEQ])
                take(f"rq{m}", rqz[64:128, 2 * m + 1, :], ps[64:128, 0:SEQ])
            for m in range(2):
                take(f"rk{m}", rk_fm[:, m, :], arrive(act, f"rk{m}")[:, 0:SEQ])
            for j in range(2):
                take(f"rkt{j}", rk_tok[:, j, :], arrive(act, f"rkt{j}")[:, 0:SEQ])
            for j in range(4):
                take(f"rv{j}", rv_tok[:, j, :], arrive(act, f"rv{j}")[:, :])
            for j in range(2):
                take(f"rg{j}", rg_tok[:, j, :], arrive(act, f"rg{j}")[:, :], ACT.Silu)
            act.wait_ge(lg_done, 1)
            act.wait_ge(arena_in["odd_tables"], 16)
            ret_q = ODD("ret_q").rearrange("p (d i) -> p d i", i=SEQ)
            age = C("ret_age").rearrange("p (d q) -> p d q", q=2)
            ages = small[:, 24:40].rearrange("p (h d q) -> p h d q", d=2, q=2)
            for h in range(4):
                for d, o in ((0, rqf), (1, rqb)):
                    rate = lg[:, 4 * d + h:4 * d + h + 1]
                    S.activation(ages[:, h, d, :], age[:, d, :], ACT.Exp, scale=rate)
                    S.activation(o[:, h, :], ret_q[:, d, :], ACT.Exp, scale=rate).then_inc(ret_qdec, 1)
            for h in range(4):
                act.wait_ge(ret_arg, h + 1)
                S.activation(ret_d[:, h, :], ret_d[:, h, :], ACT.Exp).then_inc(ret_tab, 1)
            for h in range(8):
                take(f"kn{h}", mk[0:64, h, :], arrive(act, f"kn{h}")[0:64, :])
            for j in range(4):
                take(f"mv{j}", mv_tok[:, j, :], arrive(act, f"mv{j}")[:, :])
            for h in range(0, 8, 2):
                ps = arrive(act, f"mq{h}")
                if h >= 4:
                    wait_took(act, f"mqr{h - 4}")
                take(f"mq{h}", q_raw[h // 2 % 2][0:96, :], ps[0:96, :])

            def m_exp(u):
                j, h, i = u // 8, u % 8, u % 3
                act.wait_ge(m_neg, u + 1)
                ps = tiles[f"ms{u}"].ps
                if u < 3:
                    wait_took(act, "mqr6")
                took(f"ms{u}", S.activation(probs1[i], ps[:, :], ACT.Exp, bias=m_ng[:, i:i + 1], scale=MLA_SCALE, accum_out=m_sum[:, u:u + 1]))

            m_exp(0)
            m_exp(1)
            for u in range(16):
                if u + 2 < 16:
                    m_exp(u + 2)
                probs_T("m", u, att_T21, True)
            for hp in range(2):
                take(f"rs{hp}", ret_state[:, 2 * hp:2 * hp + 2, :], arrive(act, f"rs{hp}").rearrange("p (h c) -> p h c", c=SEQ))
            for kt in range(0, KT, 2):
                take(f"bT{kt}", attT1[:, kt, :], arrive(act, f"bT{kt}")[:, 0:SEQ])
            route(1)
            experts(1)
            act.wait_ge(acc_done[1], 2 * 2 * (EXPERTS // 4))
            squares(6)

        @block.gpsimd
        def _(pool):
            Q = nc.gpsimd

            def roots(name, o, i):
                pool.wait_ge(ms_done, POW.index(name) + 1)
                n = i.shape[1]
                Q.tensor_tensor(o, i, neg_half[:, 0:n], ALU.pow).then_inc(rstd_done, 1)

            def norm_roots(n):
                roots(f"norm{n}", rstd[:, 0:NORM_TILES[n]], meansq[:, 0:NORM_TILES[n]])

            Q.memset(neg_half, -0.5)
            Q.memset(ada_bias, 0.0).then_inc(pool_zero, 1)
            for s in range(2):
                Q.memset(silu_c[s], 0.0).then_inc(silu_pad, 1)
            Q.memset(mem[:, conv0:conv0 + 2 * (396 + 258)], 0.0).then_inc(pool_zero, 1)
            Q.memset(cumT, 0.0).then_inc(pool_zero, 1)
            pool.dma_start(dft, A["dft_tab"]).then_inc(arena_in["dft"], 16)
            norm_roots(0)
            pool.wait_ge(ctx_w, 1)
            wait_took(pool, "ct15")
            wait_took(pool, "four3")
            for d in range(2):
                if d:
                    pool.wait_ge(mm_done, tiles["zs21"].no)
                for q in range(2):
                    Q.tensor_tensor(xw[d][:, q, :].rearrange("p (h c) -> p h c", c=64), xs_tok[:, 2 + q, :].rearrange("p (h c) -> p h c", c=64),
                                    w_ctx[:, q, 24 * d:24 * d + 24].unsqueeze(2).to_broadcast([P, HEADS, 64]), ALU.mult).then_inc(xw_done, 1)
            pool.wait_ge(mm_done, tiles["hs13"].no)
            pool.wait_ge(consts_in, 16 * N_CONST_DMAS)
            for g in range(GROUPS):
                z = [zs[:, l, GW * g:GW * g + GW] for l in range(2)]
                for l in range(2):
                    last = Q.tensor_tensor(y_acc[l].rearrange("p (h c) -> p h c", c=64), xs_tok[:, l, GW * g:GW * g + GW].rearrange("p (h c) -> p h c", c=64),
                                           R("d_skip")[:, HPG * g:HPG * g + HPG].unsqueeze(2).to_broadcast([P, HPG, 64]), ALU.mult)
                last.then_inc(y_skip, 1)
                wait_took(pool, f"off{g}11")
                for d in range(2):
                    for l in range(2):
                        Q.tensor_tensor(y_acc[l], y_acc[l], off_t[l][d], ALU.add)
                    pool.drain()
                for l in range(2):
                    last = Q.tensor_tensor(z[l], y_acc[l], z[l], ALU.mult)
                last.then_inc(ssd_z, 1)
                pool.wait_ge(ssd_sq, 2 * g + 2)
                by_tile = lambda a: a.rearrange("p (l g) -> p l g", g=GROUPS)[:, :, g]
                Q.tensor_scalar(by_tile(ms8), by_tile(ssq8), 1.0 / GW, EPS, ALU.mult, ALU.add)
                pool.drain()
                Q.tensor_tensor(by_tile(rstd8), by_tile(ms8), neg_half[:, 0:2], ALU.pow)
                pool.drain()
                for l in range(2):
                    Q.tensor_scalar(z[l], z[l], rstd8[:, 4 * l + g:4 * l + g + 1], None, ALU.mult).then_inc(gated_done, 1)
            pool.dma_start(gain_1, A["final_norm_w"].unsqueeze(0).to_broadcast([P, D])).then_inc(arena_in["gain1"], 16)
            pool.dma_start(xres[:, 2:4, :], A["ctx_2"][0].rearrange("(t p) d -> p t d", p=P)).then_inc(ctx2_in, 16)
            pool.dma_start(rope, A["rope_tab"]).then_inc(arena_in["rope"], 16)
            for b in (*qz, *nqz):
                last = Q.memset(b, 0.0)
            last.then_inc(pool_zero, 1)
            norm_roots(1)
            pool.wait_ge(res_done, 4)
            pool.dma_start(gate_1, A["final_norm_2"].unsqueeze(0).to_broadcast([P, D])).then_inc(arena_in["gain2"], 16)
            def load_router(l):
                pool.dma_start(router_sb, A["moe_router"][l].rearrange("(k p) e -> p k e", p=P)).then_inc(arena_in[f"router{l}"], 16)

            norm_roots(2)
            pool.wait_ge(mm_done, tiles["row29"].no)
            load_router(0)
            pool.wait_ge(mm_done, tiles["nv3"].no)
            pool.dma_start(na_bias.rearrange("p h n -> p (h n)"), A["na_bias"]).then_inc(arena_in["na_bias"], 16)
            pool.wait_ge(arena_in["na_bias"], 16)
            nb = na_bias.rearrange("p h (m c) -> p (h m) c", c=GRID_W)
            Q.tensor_tensor(nb, nb, C("na_mask").unsqueeze(1).to_broadcast([P, 48, GRID_W]), ALU.add).then_inc(na_masked, 1)
            roots("diff", d_ss, d_ms)

            def experts(l):
                T, n_grp = (4, 2) if l == 0 else (2, 4)
                S = P // n_grp
                steps = EXPERTS // n_grp
                xe = xe_stg.rearrange("p (g k s) -> p g k s", g=n_grp, k=KT)
                last_gather = [f"ga{l}.7{s}" for s in range(T // 2)] + [f"ga{l}.6{s}" for s in range(T // 2)]
                for name in last_gather:
                    wait_took(pool, name)
                if l == 0:
                    Q.memset(dstg, 0.0).then_inc(moe_bufs_zero, 1)
                    pool.wait_ge(moe_bufs_zero, 1)

                def stage_rows(e, at):
                    for half, src in ((0, xe_lo), (1, xe_hi)):
                        last = Q.tensor_copy(xe[:, e, 4 * half:4 * half + 4, :], src[:, :, at])
                    last.then_inc(xe_staged[l], 1)

                def stage_gates(at):
                    if l == 0:
                        d4 = dstg.rearrange("p t (g s) -> p t g s", g=n_grp)
                        for s in range(2):
                            last = Q.tensor_copy(d4[:, 2 * s:2 * s + 2, :, CAP * s:CAP * s + CAP],
                                                 d_gate[:, 2 * s:2 * s + 2, at].rearrange("p t (g s) -> p t g s", s=CAP))
                    else:
                        last = Q.tensor_copy(dstg[:, 0:2, :], d_gate[:, 0:2, at])
                    last.then_inc(dstage[l], 1)

                stage_gates(slice(0, n_grp * CAP))
                for e in range(n_grp):
                    stage_rows(e, slice(S * e, S * e + S))
                with nc.gpsimd.Fori(0, steps - 1) as it:
                    for e in range(n_grp):
                        pool.wait_ge(moe_used[l], it * (6 * n_grp) + (6 * e + 4))
                        stage_rows(e, bass.ds(it * P + (P + S * e), S))
                        if e == 0:
                            pool.wait_ge(dT_mm[l], it + 1)
                            stage_gates(bass.ds(it * (n_grp * CAP) + n_grp * CAP, n_grp * CAP))

            norm_roots(3)
            pool.wait_ge(mm_done, tiles["rl0"].no)
            load_router(1)
            experts(0)
            pool.wait_ge(acc_done[0], 2 * 4 * (EXPERTS // 2))
            pool.dma_start(odd_c, A["odd_tab"]).then_inc(arena_in["odd_tables"], 16)
            norm_roots(4)
            pool.wait_ge(xn_done, NORM_SUM[4])
            Q.memset(rqz, 0.0).then_inc(pool_zero, 1)
            roots("lat", small[:, 64:70], small[:, 80:86])
            wait_took(pool, "krot")
            Q.tensor_copy(mk[64:96, :, :], kr_raw[64:96, :].unsqueeze(1).to_broadcast([32, 8, TOK])).then_inc(kr_copied, 1)
            roots("ret", small[:, 64:72], small[:, 80:88])
            norm_roots(5)
            experts(1)
            norm_roots(6)

        @block.sync
        def _(sp):
            def load_x(name, t0, s):
                sp.dma_start(xres[:, t0:t0 + 2, :], A[name][0].rearrange("(t p) d -> p t d", p=P)).then_inc(s, 16)

            sp.dma_start(cbuf, A["const_tab"]).then_inc(consts_in, 16)
            sp.dma_start(par, A["par"]).then_inc(consts_in, 16)
            sp.dma_start(rowp, A["rowp"].unsqueeze(0).to_broadcast([P, N_ROWP])).then_inc(consts_in, 16)
            sp.wait_ge(pool_zero, 1)
            sp.dma_start(ada_bias[0:30, :], A["ada_bias"]).then_inc(bias_in, 16)
            order = [n for n, _ in chunks]
            last_in_slot = [None] * 6

            def load(name):
                s = place[name]
                prev = last_in_slot[s]
                if prev is not None:
                    sem_, v = prev
                    sp.wait_ge(sem_, v)
                src = dict(chunks)[name]
                sp.dma_start(slot(s, src.shape[1], src.shape[2]), src).then_inc(filled[s], 16)
                last_in_slot[s] = chunk_freed[name]

            def load_experts(l):
                w = (A["moe_w1"][l], A["moe_w3"][l], A["moe_w2"][l])

                def piece(j, e):
                    s = moe_slot[l][j]
                    src = w[j // 2][e, 512 * (j % 2):512 * (j % 2) + 512, :].rearrange("(k p) f -> p k f", p=P) if isinstance(e, int) else \
                        w[j // 2][bass.ds(e, 1), 512 * (j % 2):512 * (j % 2) + 512, :].rearrange("o (k p) f -> p (o k) f", p=P)
                    sp.dma_start(slot(s, 4, 1024), src).then_inc(filled[s], 16)

                for j in (0, 3, 4, 1, 2, 5):
                    s = moe_slot[l][j]
                    if j < 3:
                        sem_, v = last_in_slot[s]
                        sp.wait_ge(sem_, v)
                    elif j < 5:
                        sp.wait_ge(mm_done, tiles["aT0" if l == 0 else "bT0"].no)
                    else:
                        sp.wait_ge(mm_done, chunk_freed[f"gather{l}"])
                        wait_took(sp, "ga0.71" if l == 0 else "ga1.60")
                    piece(j, 0)
                with nc.sync.Fori(1, EXPERTS) as e:
                    for j in range(6):
                        sp.wait_ge(moe_used[l], e * 6 + (j - 5))
                        piece(j, e)
                for j in range(6):
                    last_in_slot[moe_slot[l][j]] = (moe_used[l], 6 * (EXPERTS - 1) + j + 1)

            for name in order[:2]:
                load(name)
            load_x("x", 0, x_in)
            load_x("ctx", 2, ctx_in)
            for name in order[2:N_PRE0]:
                load(name)
            load_experts(0)
            for name in order[N_PRE0:]:
                load(name)
            load_experts(1)
            for j in range(2):
                sp.wait_ge(out_ready, j + 1)
                sp.dma_start(out[0, P * j:P * j + P, :], xres[:, j, :]).then_inc(out_stored, 16)
            sp.wait_ge(out_stored, 32)


WEIGHTS = ["x", "ctx", "ctx_2", "w_ada", "w_in", "w_fourier", "w_out", "ada_w", "even_w_in", "even_w_out", "moe_w1", "moe_w3", "moe_w2",
           "moe_router", "odd_w_in", "odd_w_out", "mla_w_uq", "mla_w_ukv", "final_norm_w", "final_norm_2"]


def laid_out(i):
    f = {k: np.asarray(v) for k, v in i.items()}
    col = lambda a: np.ascontiguousarray(a.reshape(-1, P).T)
    pair = lambda a, b: np.stack([col(a), col(b)], 2).reshape(P, 16)
    parts = {
        "cvec1": pair(f["c"][0], f["c_ctx"]), "cvec2": pair(f["c_2"][0], f["c_ctx_2"]), "norm_w": col(f["norm_w"][0]),
        "conv_w": f["conv_w"][0].reshape(9, CONV_TILES, P).transpose(2, 1, 0).reshape(P, 180), "conv_b": col(f["conv_b"][0]),
        "ssd_norm": col(f["ssd_norm_w"][0]), "b_four": col(f["b_fourier"][0]), "norm_mix": col(f["norm_mix_2"].reshape(-1)),
        "norm_ffn": col(f["norm_ffn_2"].reshape(-1)), "subln": col(f["diff_subln_2"][0]), "q_norm": col(f["mla_q_norm_2"][0]),
        "kv_norm": col(f["mla_kv_norm_2"][0]),
    }
    o = {"par": np.concatenate([parts[n] for n in PAR], 1)}
    rows_ = {"dt_bias": f["dt_bias"], "a_log": f["a_log"], "d_skip": f["d_skip"], "diff_lambda": f["diff_lambda_2"], "ret_decay": f["ret_decay_logit_2"]}
    o["rowp"] = np.concatenate([rows_[n].reshape(-1) for n in ROWP])
    o["ada_bias"] = np.concatenate([f["b_ada"].reshape(6, 512), f["ada_b_2"].reshape(24, 512)], 0)
    par_, c, m, k = np.meshgrid(np.arange(2), np.arange(GRID_W), np.arange(6), np.arange(GRID_W), indexing="ij")
    dr, dc = m + 5 - par_, k - c + 15
    ok = (dc >= 0) & (dc < 31)
    padded = np.pad(f["na_rpb_2"][0], ((0, 0), (0, 0), (0, 1)))
    o["na_bias"] = np.ascontiguousarray(padded[:, dr, np.where(ok, dc, 31)].transpose(1, 2, 0, 3, 4).reshape(P, 8 * 384))
    names = {"ada_w": "ada_w_2", "even_w_in": "even_w_in_2", "even_w_out": "even_w_out_2", "moe_w1": "moe_w1_2", "moe_w3": "moe_w3_2",
             "moe_w2": "moe_w2_2", "moe_router": "moe_router_2", "odd_w_in": "odd_w_in_2", "odd_w_out": "odd_w_out_2",
             "mla_w_uq": "mla_w_uq_2", "mla_w_ukv": "mla_w_ukv_2"}
    for n in WEIGHTS:
        a = f[names.get(n, n)]
        o[n] = np.ascontiguousarray(a[0] if n in ("w_ada", "w_in", "w_fourier", "w_out") else a)
    for n, (tab, _) in zip(("const_tab", "dft_tab", "rope_tab", "odd_tab"), CONSTS):
        o[n] = tab
    return o


def kernel(**inputs):
    import concourse.bacc as bacc
    from concourse.bass_utils import run_bass_kernel_spmd

    arrays = {f"in_{n}": a for n, a in laid_out(inputs).items()}
    nc = bacc.Bacc("TRN2", target_bir_lowering=False, num_devices=1)
    A = {n[3:]: nc.dram_tensor(n, a.shape, mybir.dt.from_np(a.dtype), kind="ExternalInput").ap() for n, a in arrays.items()}
    out = nc.dram_tensor("out", (1, SEQ, D), F32, kind="ExternalOutput").ap()
    build(nc, A, out)
    return run_bass_kernel_spmd(nc, [arrays], core_ids=[0]).results[0]["out"]
```

```python
from contextlib import ExitStack

import numpy as np
import concourse.bass as bass
from concourse import mybir

F32 = mybir.dt.float32
ALU = mybir.AluOpType
ACT = mybir.ActivationFunctionType
AX = mybir.AxisListType.X

P = 128
D = 1024
KT = D // P
SEQ = 256
TOK = 2 * SEQ
GRID_W = 64
ROWS = SEQ // GRID_W
EPS = 1e-6
D_SSD = 1536
HEADS, GROUPS = 24, 4
HPG = HEADS // GROUPS
GW = D_SSD // GROUPS
CONV_TILES = 20
EXPERTS, CAP, FF = 16, 32, 1024
SLOT = 4096
LAM_INIT = 0.8 - 0.6 * float(np.exp(-0.3 * 0))
NA_SCALE = 64 ** -0.5
MLA_SCALE = 96 ** -0.5
MASKED = -1.0e30

ADA = [(0, i) for i in range(6)] + [(l + 1, i) for l in range(2) for i in range(12)]
ROW_STEPS = [k for k, (s, i) in enumerate(ADA) if i // 2 in ((2,) if s == 0 else (2, 5))]
COL_STEPS = [k for k in range(len(ADA)) if k not in ROW_STEPS]


def rope_tables(rot, n_pad):
    t = np.arange(SEQ)
    m = rot // 4
    freq = (10000.0 ** (-np.arange(m, dtype=np.float32) / m)).astype(np.float32)
    ang = [(t // GRID_W)[:, None].astype(np.float32) * freq, (t % GRID_W)[:, None].astype(np.float32) * freq]
    n = n_pad + rot
    cos, sin, swap = np.ones((n, SEQ), np.float32), np.zeros((n, SEQ), np.float32), np.zeros((n, n), np.float32)
    for half in range(2):
        for j in range(m):
            a = n_pad + half * 2 * m + j
            b = a + m
            cos[a] = cos[b] = np.cos(ang[half][:, j])
            sin[a] = sin[b] = np.sin(ang[half][:, j])
            swap[b, a] = -1.0
            swap[a, b] = 1.0
    return cos, sin, swap


def shape_constants():
    p = np.arange(P)
    c = {}
    c["ident"] = np.eye(P)
    tok = np.arange(SEQ)
    le = (tok[:, None] <= tok[None, :]).astype(np.float32)
    c["tri_f"] = le.reshape(2, P, SEQ).transpose(1, 0, 2)
    c["tri_b"] = le.T.reshape(2, P, SEQ).transpose(1, 0, 2)
    sel = np.zeros((P, 2))
    sel[p[p % 32 == 0], 0] = 1
    sel[p[p % 32 == 1], 1] = 1
    c["sum2"] = sel
    c["sel_x"] = np.repeat(sel[:, 0:1], P, 1)
    c["sel_c"] = np.repeat(sel[:, 1:2], P, 1)
    c["sel_xc"] = np.concatenate([c["sel_x"][:, :32], c["sel_c"][:, :32]], 1)
    c["sum_e"] = (p[:, None] % 32 == np.arange(EXPERTS)[None, :]).astype(np.float32)
    n_rows = len(ROW_STEPS)
    pick = np.zeros((P, n_rows, 2))
    pick[np.arange(n_rows), np.arange(n_rows), :] = 1
    c["ada_pick"] = pick
    c["iota"] = np.repeat(1.0 + np.arange(CAP)[None, :], P, 0)
    cc = np.arange(GRID_W)
    cs = np.clip(cc - 8, 0, GRID_W - 16)
    inside = (cc[None, :] >= cs[:, None]) & (cc[None, :] < cs[:, None] + 16)
    c["na_mask"] = np.tile(np.where(inside, 0.0, MASKED), (2, 1))
    pos = 128.0 * np.arange(2)[None, :] + p[:, None]
    c["ret_age"] = np.concatenate([255.0 - pos, pos], 1)
    c["block1"] = None
    g = np.arange(64)
    ang = 2 * np.pi * np.outer(g, g) / 64
    bd = lambda m: np.kron(np.eye(2), m)
    k = {}
    k["dft_ch"] = np.concatenate([bd(np.cos(ang)), bd(np.sin(ang))], 1)
    angt = 2 * np.pi * (np.outer(tok, tok) % SEQ) / SEQ
    k["dft_cos"] = (np.cos(angt) / 128.0).reshape(2, P, SEQ).transpose(1, 0, 2)
    k["dft_nsin"] = (-np.sin(angt) / 128.0).reshape(2, P, SEQ).transpose(1, 0, 2)
    del c["block1"]
    cos, sin, swap = rope_tables(64, 0)
    e = {"rope_cos": np.tile(cos, (2, 1)), "rope_sin": np.tile(sin, (2, 1)), "rope_swap": np.kron(np.eye(2), swap)}
    cos, sin, swap = rope_tables(32, 64)
    pad = lambda a, n: np.concatenate([a, np.zeros((P - a.shape[0], a.shape[1]))], 0)
    o = {"mla_cos": pad(cos, P), "mla_sin": pad(sin, P), "mla_swap": pad(swap, P)}
    o["ret_fwd"] = np.maximum(tok[None, :] - tok[:, None], 0).reshape(2, P, SEQ).transpose(1, 0, 2)
    o["ret_bwd"] = np.maximum(tok[:, None] - tok[None, :], 0).reshape(2, P, SEQ).transpose(1, 0, 2)
    o["ret_q"] = np.repeat(np.stack([tok + 1.0, 256.0 - tok])[None], P, 0)
    flat = lambda d: {n: np.ascontiguousarray(a, np.float32).reshape(P, -1) for n, a in d.items()}
    return flat(c), flat(k), flat(e), flat(o)


def packed(d):
    at, off = {}, 0
    for n, a in d.items():
        at[n] = (off, a.shape[1])
        off += a.shape[1]
    return np.ascontiguousarray(np.concatenate(list(d.values()), 1), np.float32), at


CONSTS = tuple(packed(d) for d in shape_constants())

PAR = {}
_n = 0
for _name, _w in (("cvec1", 16), ("cvec2", 16), ("norm_w", 8), ("conv_w", 180), ("conv_b", 20), ("ssd_norm", 12),
                  ("b_four", 4), ("norm_mix", 16), ("norm_ffn", 16), ("subln", 1), ("q_norm", 2), ("kv_norm", 1), ("ada_bias", 4 * len(COL_STEPS))):
    PAR[_name] = (_n, _w)
    _n += _w
N_PAR = _n
ROWP = {}
_n = 0
for _name, _w in (("dt_bias", 48), ("a_log", 48), ("d_skip", 24), ("diff_lambda", 256), ("ret_decay", 8)):
    ROWP[_name] = (_n, _w)
    _n += _w
N_ROWP = _n


def build(nc, A, out):
    ctx = ExitStack()
    with ctx:
        WORDS = 53200
        mem = ctx.enter_context(nc.sbuf_tensor("mem", [P, WORDS], F32))
        bank = [ctx.enter_context(nc.psum_tensor(f"bank{i}", [P, 512], F32)) for i in range(8)]

        def sem(name):
            return ctx.enter_context(nc.semaphore(name))

        class Region:

            def __init__(self, at, words):
                self.at, self.end = at, at + words

            def take(self, *dims):
                n = int(np.prod(dims))
                assert self.at + n <= self.end, (self.at, n, self.end)
                v = mem[:, self.at:self.at + n]
                self.at += n
                if len(dims) == 2:
                    v = v.rearrange("p (a b) -> p a b", b=dims[1])
                elif len(dims) == 3:
                    v = v.rearrange("p (a b c) -> p a b c", b=dims[1], c=dims[2])
                return v

        RING0 = 0
        ARENA2 = 3 * SLOT
        XRES = 6 * SLOT
        XN = XRES + 4096
        HT = XN + 4096
        FIXED = HT + 4096
        fixed = Region(FIXED, WORDS - FIXED)
        xres = Region(XRES, 4096).take(4, D)
        xn = Region(XN, 4096).take(4, D)
        hT = Region(HT, 4096).take(KT, TOK)

        consts, const_at = CONSTS[0]
        cbuf = fixed.take(consts.shape[1])
        C = lambda n: cbuf[:, const_at[n][0]:const_at[n][0] + const_at[n][1]]
        ident = C("ident")
        tri_f = C("tri_f").rearrange("p (a b) -> p a b", b=SEQ)
        tri_b = C("tri_b").rearrange("p (a b) -> p a b", b=SEQ)
        par = fixed.take(N_PAR)
        rowp = fixed.take(N_ROWP)
        G = lambda n: par[:, PAR[n][0]:PAR[n][0] + PAR[n][1]]
        R = lambda n: rowp[:, ROWP[n][0]:ROWP[n][0] + ROWP[n][1]]
        ADA_WORK = fixed.at
        ada_bias = fixed.take(512)
        silu_c = [fixed.take(KT, 32) for _ in range(2)]
        ada_row = [fixed.take(512) for _ in range(2)]
        ADA_WORK_WORDS = fixed.at - ADA_WORK
        ada_col = [fixed.take(2, 16), fixed.take(4, 16), fixed.take(4, 16)]
        norm_a = fixed.take(5, 16)
        gate_1 = fixed.take(D)
        gate_mix = [fixed.take(2, D), fixed.take(1, D)]
        gate_ffn = [fixed.take(512), fixed.take(256)]
        ssq = fixed.take(4)
        meansq = fixed.take(4)
        rstd = fixed.take(4)
        neg_half = fixed.take(32)
        small = fixed.take(112)
        lam_b = fixed.take(4)
        ARENA1 = fixed.at
        ARENA1_WORDS = WORDS - ARENA1

        chunks = []

        def cols(w, a, n):
            return w[:, a:a + n].rearrange("(k p) f -> p k f", p=P)

        def rows(w, a, n):
            return w[a:a + n, :].rearrange("(k p) f -> p k f", p=P)

        def chunk(name, src):
            chunks.append((name, src))

        w_in = A["w_in"]
        for i in range(4):
            chunk(f"ada0.{i}", cols(A["w_ada"], 512 * i, 512))
        chunk("u", cols(w_in, 0, 512))
        chunk("dt", cols(w_in, 5120, 48))
        chunk("zf", cols(w_in, 512, 512))
        chunk("w_four", rows(A["w_fourier"], 0, 512))
        for i in range(4, 6):
            chunk(f"ada0.{i}", cols(A["w_ada"], 512 * i, 512))
        for i in range(5):
            chunk(f"conv{i}", cols(w_in, 2560 + 512 * i, 512))
        for i in range(3):
            chunk(f"zs{i}", cols(w_in, 1024 + 512 * i, 512))
        for i in range(20):
            chunk(f"ada{i // 12 + 1}.{i % 12}", cols(A["ada_w"][i // 12], 512 * (i % 12), 512))
        for i in range(4):
            chunk(f"w_out{i}", rows(A["w_out"], 512 * i, 512))
            if i == 1:
                chunk("ada2.8", cols(A["ada_w"][1], 512 * 8, 512))
        for i in range(21, 24):
            chunk(f"ada{i // 12 + 1}.{i % 12}", cols(A["ada_w"][i // 12], 512 * (i % 12), 512))
        for i in range(6):
            chunk(f"even{i}", cols(A["even_w_in"][0], 512 * i, 512))
        for i in range(2):
            chunk(f"even_out{i}", rows(A["even_w_out"][0], 512 * i, 512))
        N_PRE0 = len(chunks)
        odd = A["odd_w_in"][0]
        odd_chunks = []
        odd_chunks.append(("odd_cq", cols(odd, 0, 416)))
        odd_chunks.append(("odd_rqk", cols(odd, 416, 512)))
        odd_chunks.append(("odd_rv", cols(odd, 928, 512)))
        odd_chunks.append(("odd_rg", cols(odd, 1440, 512)))
        odd_chunks.append(("w_ukv", rows(A["mla_w_ukv"][0], 0, 128)))
        odd_chunks.append(("w_uq", rows(A["mla_w_uq"][0], 0, 256)))
        for i in range(2):
            odd_chunks.append((f"odd_out{i}", rows(A["odd_w_out"][0], 512 * i, 512)))
        chunks += odd_chunks
        place, fill_no = {}, {}
        filled = [sem(f"slot{i}_filled") for i in range(6)]
        fills = [0] * 6
        turn = 0
        for n, (name, _) in enumerate(chunks[:N_PRE0]):
            s = turn % 3
            turn += 1
            fills[s] += 1
            place[name], fill_no[name] = s, fills[s]
        moe_slot = [[0] * 6, [0] * 6]
        moe_fill = [[0] * 6, [0] * 6]

        def moe_places(l):
            first = turn % 3
            for j in range(6):
                s = (first + j) % 3 + (3 if j >= 3 else 0)
                moe_slot[l][j] = s
                moe_fill[l][j] = fills[s]
            for s in range(6):
                fills[s] += EXPERTS

        moe_places(0)
        for name, _ in chunks[N_PRE0:]:
            s = turn % 3
            turn += 1
            fills[s] += 1
            place[name], fill_no[name] = s, fills[s]
        moe_places(1)

        def slot(s, k, n):
            return mem[:, RING0 + s * SLOT:RING0 + s * SLOT + k * n].rearrange("p (k f) -> p k f", f=n)

        def chunk_view(name):
            src = dict(chunks)[name]
            return slot(place[name], src.shape[1], src.shape[2])

        mm_done = sem("mm_done")
        took_sem = {"dve": sem("dve_took"), "act": sem("act_took")}
        consts_in = sem("consts_in")
        x_in, ctx_in, bias_in = sem("x_in"), sem("ctx_in"), sem("bias_in")
        ctx2_in = sem("ctx2_in")
        arena_in = {n: sem(f"{n}_in") for n in ("dft", "rope", "na_bias", "odd_tables", "router0", "router1", "gain1", "gain2")}
        silu_pad = sem("silu_pad")
        silu_done = sem("silu_done")
        sums_done = sem("sums_done")
        ms_done = sem("ms_done")
        rstd_done = sem("rstd_done")
        xn_done = sem("xn_done")
        pool_zero = sem("pool_zero")
        dt_abs, dt_log, a_ready, a_exp = sem("dt_abs"), sem("dt_log"), sem("a_ready"), sem("a_exp")
        ctx_arg, ctx_exp, ctx_w = sem("ctx_arg"), sem("ctx_exp"), sem("ctx_w")
        x_ecum, xw_done = sem("x_ecum"), sem("xw_done")
        y_skip, ssd_z, ssd_sq = sem("y_skip"), sem("ssd_z"), sem("ssd_sq")
        conv_done, act_conv = sem("conv_done"), sem("act_conv")
        decay_out, m_ready, gated_done = sem("decay_out"), sem("m_ready"), sem("gated_done")
        out_stored, out_ready = sem("out_stored"), sem("out_ready")
        neg_max, comb_done = sem("neg_max"), sem("comb_done")
        na_neg, na_p = sem("na_neg"), sem("na_p")
        m_neg = sem("m_neg")
        lam_sum, lam_exp = sem("lam_sum"), sem("lam_exp")
        q_ready, att_done = sem("q_ready"), sem("att_done")
        rt_exp = sem("rt_exp")
        aff_done, topk_done, d_done = sem("aff_done"), sem("topk_done"), sem("d_done")
        lg_abs, lg_ln, lg_done = sem("lg_abs"), sem("lg_ln"), sem("lg_done")
        ret_arg, ret_tab, ret_qdec, rkw_done, rq_done = (sem(n) for n in ("ret_arg", "ret_tab", "ret_qdec", "rkw_done", "rq_done"))
        moe_bufs_zero = sem("moe_bufs_zero")
        pair = lambda n: [sem(n + "0"), sem(n + "1")]
        dstage, xe_staged, moe_used, silu_ready = pair("dstage"), pair("xe_staged"), pair("moe_used"), pair("silu_ready")
        hid_ready, hidT_mm, hidT_ready, y_ready = pair("hid_ready"), pair("hidT_mm"), pair("hidT_ready"), pair("y_ready")
        dT_mm, dgT_ready, scat_mm, acc_done = pair("dT_mm"), pair("dgT_ready"), pair("scat_mm"), pair("acc_done")

        N_CONST_DMAS = 3
        tiles = {}

        class Tile:
            pass

        class Banks:

            def __init__(self, pe):
                self.pe, self.count, self.next = pe, 0, 0
                self.ordinal = {"dve": 0, "act": 0}
                self.last = [None] * 8
                self.open_banks = set()

            def open(self, name, by):
                while self.next % 8 in self.open_banks:
                    self.next += 1
                b = self.next % 8
                self.next += 1
                prev = self.last[b]
                if prev is not None:
                    self.pe.wait_ge(took_sem[prev.by], prev.ordinal)
                t = Tile()
                t.name, t.by, t.b, t.ps = name, by, b, bank[b]
                self.open_banks.add(b)
                return t

            def scratch(self):
                while self.next % 8 in self.open_banks:
                    self.next += 1
                prev = self.last[self.next % 8]
                if prev is not None:
                    self.pe.wait_ge(took_sem[prev.by], prev.ordinal)
                return bank[self.next % 8][:, :]

            def close(self, t, ins):
                ins.then_inc(mm_done, 1)
                self.count += 1
                self.ordinal[t.by] += 1
                t.no, t.ordinal = self.count, self.ordinal[t.by]
                self.last[t.b] = t
                self.open_banks.discard(t.b)
                assert t.name not in tiles
                tiles[t.name] = t

        taken = {"dve": 0, "act": 0}

        def arrive(eng, name):
            eng.wait_ge(mm_done, tiles[name].no)
            return tiles[name].ps

        def took(name, ins):
            t = tiles[name]
            taken[t.by] += 1
            assert taken[t.by] == t.ordinal, (name, taken[t.by], t.ordinal)
            ins.then_inc(took_sem[t.by], 1)

        def wait_took(eng, name):
            eng.wait_ge(took_sem[tiles[name].by], tiles[name].ordinal)

        chunk_freed = {}

        NORM_TILES = [4, 2, 4, 4, 4, 2, 2]
        NORM_SUM = [sum(NORM_TILES[:i + 1]) for i in range(7)]

        ADA_AT_HEAD = {}
        for h in range(HEADS):
            if h % 4 != 3:
                ADA_AT_HEAD[h] = 6 + len(ADA_AT_HEAD)
        ADA_LEFT = 6 + len(ADA_AT_HEAD)

        def ada_kind(k):
            s, i = ADA[k]
            v, half = i // 2, i % 2
            if s == 0:
                return ("col", v, half) if v < 2 else ("gate1", 0, half)
            return {0: ("col", 0, half), 1: ("col", 1, half), 2: ("mix", 0, half),
                    3: ("col", 2, half), 4: ("col", 3, half), 5: ("ffn", 0, half)}[v]

        a1 = Region(ARENA1, ARENA1_WORDS)
        mixT = a1.take(16, SEQ)
        uT, zfT, mixedT = mixT[:, 4:8, :], mixT[:, 8:12, :], mixT[:, 12:16, :]
        cumT = a1.take(2, SEQ)
        dt_z, dt_a, dt_v, a_dt = (a1.take(4, 48) for _ in range(4))
        cum_col = a1.take(4, 48)
        x_dec = a1.take(2, 48)
        w_ctx = a1.take(2, 48)
        exp_alog = a1.take(48)
        y_t = [a1.take(GW) for _ in range(2)]
        r = Region(XRES + 2048, 2048)
        y_acc = [r.take(GW) for _ in range(2)]
        off_t = [y_t, [r.take(GW) for _ in range(2)]]
        sq_junk = r.take(GW)
        gain_1 = Region(ARENA2 + 4096, D).take(D)
        a2 = Region(ARENA2, 3 * SLOT)
        xs_tok = a2.take(4, D_SSD)
        conv0 = a2.at
        xpad = [a2.take(6, 66) for _ in range(2)]
        cpad = [a2.take(258) for _ in range(2)]
        conv_acc = [a2.take(512) for _ in range(2)]
        conv_out = [a2.take(512) for _ in range(2)]
        dft_a = a2.take(2, 4, 256)
        a2b = Region(conv0, 6144)
        cb = a2b.take(GROUPS, 2, 384)
        h_init = a2b.take(2, D_SSD)
        dft_tab, dft_at = CONSTS[1]
        dft = Region(ARENA2, 1280).take(dft_tab.shape[1])
        DFT = lambda n: dft[:, dft_at[n][0]:dft_at[n][0] + dft_at[n][1]]
        dft_cos = DFT("dft_cos").rearrange("p (a b) -> p a b", b=SEQ)
        dft_nsin = DFT("dft_nsin").rearrange("p (a b) -> p a b", b=SEQ)
        r = Region(XN, 4096)
        zs = r.take(2, D_SSD)
        c_fm = r.take(GROUPS, SEQ)
        r = Region(XRES + 2048, 2048)
        b_tok = r.take(2, 512)
        b_fm = r.take(GROUPS, SEQ)
        xw = [mixT[:, 4:16, :].rearrange("p a b -> p (a b)").rearrange("p (q c) -> p q c", c=D_SSD),
              Region(HT, 4096).take(2, D_SSD)]
        r = Region(HT, 4096)
        dec_arg = [r.take(2, 384) for _ in range(2)]
        dec_exp = [r.take(2, 384) for _ in range(2)]
        m_mat = [r.take(2, SEQ) for _ in range(2)]
        res_t = [Region(ARENA1 + 512 * i, 512).take(512) for i in range(4)]
        r = Region(ARENA2, 3 * SLOT)
        qz = [r.take(4, TOK) for _ in range(2)]
        k_fm = r.take(4, TOK)
        v_tok = r.take(4, 512)
        nqz = [r.take(4, TOK) for _ in range(2)]
        r = Region(ARENA1, ARENA1_WORDS)
        nk_fm = r.take(4, TOK)
        nv_tok = r.take(4, 512)
        keep = r.at
        rope_tab, rope_at = CONSTS[2]
        rope = r.take(rope_tab.shape[1])
        ROPE = lambda n: rope[:, rope_at[n][0]:rope_at[n][0] + rope_at[n][1]]
        rope_raw = [r.take(TOK) for _ in range(2)]
        rope_t = [r.take(SEQ) for _ in range(2)]
        r = Region(keep, ARENA1 + ARENA1_WORDS - keep)
        probs = [[r.take(512) for _ in range(2)] for _ in range(2)]
        na_p_buf = [Region(ADA_WORK + 512 * i, 512).take(512) for i in (1, 2, 3)]
        sq_t = r.take(512)
        r = Region(XN, 4096)
        na_bias = r.take(8, 384)
        att_T2 = [r.take(4, P) for _ in range(2)]
        att = Region(HT, 4096).take(4, D)
        attT = Region(moe_slot[0][5] * SLOT, SLOT).take(KT, TOK)
        UNITS = [unit for u in range(16) for unit in (("d", u), ("n", 2 * u), ("n", 2 * u + 1))]
        per_tile = len(UNITS) // 4
        AHEAD = 4
        r = Region(ARENA1, ARENA1_WORDS)
        xe_hi = r.take(4, 1024)
        d_tok = r.take(4, 512)
        hid = r.take(512)
        xe_lo = Region(HT, 4096).take(4, 1024)
        r = Region(XN, 4096)
        y_sb = r.take(D)
        silu_h = r.take(512)
        hidT = r.take(512)
        dgT = r.take(512)
        dstg = r.take(4, P)
        xe_stg = r.take(1024)
        r = Region(ADA_WORK, ADA_WORK_WORDS)
        router_sb = r.take(KT, 32)
        aff = r.take(4, EXPERTS)
        aff_work = r.take(SEQ)
        sel_e = r.take(SEQ)
        top8 = [r.take(8) for _ in range(4)]
        slot_t = r.take(4, EXPERTS)
        rt_mx = r.take(4, 1)
        lgT = r.take(TOK)
        rt_t = r.take(4, EXPERTS)
        rt_sum = r.take(4, 1)
        r = Region(ARENA2, 3 * SLOT)
        mk = r.take(8, TOK)
        mq = r.take(8, SEQ)
        mv_tok = r.take(4, 512)
        rv_tok = r.take(4, 512)
        rg_tok = r.take(2, 512)
        ret_state = r.take(4, SEQ)
        r = Region(ARENA1, ARENA1_WORDS)
        ret_d = r.take(4, 512)
        odd_tab, odd_at = CONSTS[3]
        odd_c = r.take(odd_tab.shape[1])
        ODD = lambda n: odd_c[:, odd_at[n][0]:odd_at[n][0] + odd_at[n][1]]
        rk_tok = r.take(2, SEQ)
        probs1 = [r.take(512) for _ in range(2)]
        probs1.append(ada_row[0])
        r = Region(XRES + 2048, 2048)
        rqz = r.take(4, SEQ)
        rk_fm = r.take(2, SEQ)
        ret_s2 = [r.take(2, SEQ)]
        r = Region(XN, 4096)
        c_lat = r.take(4, 384)
        cqT = r.take(2, SEQ)
        ckvT = r.take(TOK)
        kr_raw = r.take(TOK)
        q_raw = [r.take(512), probs1[1]]
        q_rot = [probs1[0], probs1[2]]
        ret_s2.append(r.take(2, SEQ))
        r = Region(XN, 4096)
        att1 = r.take(2, D)
        r.take(512)
        att_T21 = [r.take(4, P) for _ in range(2)]
        r = Region(HT, 4096)
        rqf = r.take(4, SEQ)
        rqb = r.take(4, SEQ)
        rvw_all = r.take(4, 2, SEQ)
        ret_sq = Region(r.at - 2048, 1024).take(2, 512)
        BT = (4, 5, 6, 7, 0, 1, 2, 3)
        attT1 = Region(HT, 4096).take(KT, SEQ)
        kr_copied = sem("kr_copied")
        res_done = sem("res_done")
        gates_done = sem("gates_done")
        router_pad = sem("router_pad")
        d_squared = sem("d_squared")
        gain0_done, na_masked = sem("gain0_done"), sem("na_masked")
        part_used = sem("part_used")

        POW = ["norm0", *(f"norm1.{j}" for j in range(2)), "norm2", "diff_a", "diff_b", *(f"norm3.{j}" for j in range(4)), "norm4", "lat", "ret",
               *(f"norm5.{j}" for j in range(2)), "norm6"]
        NORM_A = {0: 0, 2: 1, 3: 2, 4: 3, 5: 4}
        NORM_B = {0: (0, 0), 2: (1, 0), 3: (1, 2), 4: (2, 0), 5: (2, 2)}
        ssq8, ms8, rstd8 = small[:, 0:8], small[:, 8:16], small[:, 16:24]
        a_neg, a_mx, a_sum, a_rec = small[:, 0:6], small[:, 6:12], small[:, 12:18], small[:, 18:24]
        n_neg, n_mx, n_sum, n_rec = small[:, 24:28], small[:, 28:32], small[:, 32:48], small[:, 48:64]
        d_ss, d_ms = small[:, 64:80], small[:, 80:96]
        m_ng, m_mx, m_sum, m_rec = small[:, 8:11], small[:, 11:14], small[:, 40:56], small[:, 96:112]

        def xe_rows(l, kt, s):
            S = 64 if l == 0 else 32
            rows = (xe_lo if kt < 4 else xe_hi)[:, kt % 4, 0:EXPERTS * S].rearrange("p (e s) -> p e s", s=S)
            return rows[:, :, CAP * s:CAP * s + CAP]

        block = ctx.enter_context(nc.Block())

        @block.tensor
        def _(pe):
            B = Banks(pe)

            def use(name):
                pe.wait_ge(filled[place[name]], 16 * fill_no[name])
                return chunk_view(name)

            def done_with(name):
                chunk_freed[name] = (mm_done, B.count)

            def mm(o, lhsT, rhs, start, stop):
                return nc.tensor.matmul(o, lhsT, rhs, start=start, stop=stop, skip_group_check=True)

            def warm(n):
                o = B.scratch()
                for _ in range(n):
                    nc.tensor.matmul(o, ident, cbuf[:, 0:512], start=True, stop=True, skip_group_check=True)

            def tr(o, i):
                return nc.tensor.transpose(o, i, ident)

            def ada_rows(k):
                s, i = ADA[k]
                w = use(f"ada{s}.{i}")
                t = B.open(f"row{k}", "act" if k in ADA_AT_HEAD.values() else "dve")
                for kt in range(KT):
                    g = kt % 4
                    as_rows = ada_kind(k)[0] != "col"
                    last = mm(t.ps[32 * g:32 * g + 32, :], silu_c[min(s, 1)][:, kt, :], w[:, kt, :], kt < 4, kt >= 4 and not (as_rows and g == 0))
                if as_rows:
                    pick = C("ada_pick").rearrange("p (a b) -> p a b", b=2)
                    last = mm(t.ps[0:2, :], pick[:, ROW_STEPS.index(k), :], ada_bias, False, True)
                B.close(t, last)
                done_with(f"ada{s}.{i}")

            def ada_outs(k):
                kind, v, half = ada_kind(k)
                wait_took(pe, f"row{k}")
                row = ada_row[k % 2]
                l = ADA[k][0] - 1
                if kind == "col":
                    t = B.open(f"col{k}", "dve")
                    for j in range(4):
                        last = mm(t.ps[:, 2 * j:2 * j + 2], row[:, P * j:P * j + P], C("sum2"), True, True)
                    B.close(t, last)
                elif kind == "ffn":
                    t = B.open(f"col{k}", "dve")
                    if l == 0:
                        last = mm(t.ps[64 * half:64 * half + 64, :], C("sel_xc"), row, True, True)
                    else:
                        for q in range(2):
                            g = 2 * half + q
                            last = mm(t.ps[32 * g:32 * g + 32, 0:256], C("sel_x")[:, 0:32], row[:, 256 * q:256 * q + 256], True, True)
                    B.close(t, last)
                else:
                    for j, sel in enumerate(("sel_x", "sel_c")[:2 if (kind == "mix" and l == 0) else 1]):
                        t = B.open(f"col{k}" + "c" * j, "dve")
                        B.close(t, mm(t.ps[:, :], C(sel), row, True, True))

            def norm_T(n):
                T = NORM_TILES[n]
                if n in (3, 4, 5):
                    warm(4)
                pe.wait_ge(xn_done, NORM_SUM[n])
                for kt in range(KT):
                    t = B.open(f"nT{n}.{kt}", "act" if kt % 2 else "dve")
                    for j in range(T):
                        last = tr(t.ps[:, P * j:P * j + P], xn[:, j, P * kt:P * kt + P])
                    B.close(t, last)
                wait_took(pe, f"nT{n}.6")
                wait_took(pe, f"nT{n}.7")

            def feature_major(t, w, c0, mw, n0, n1, o=None, p0=0):
                o = t.ps[p0:p0 + mw, 0:n1 - n0] if o is None else o
                for kt in range(KT):
                    last = mm(o, w[:, kt, c0:c0 + mw], hT[:, kt, n0:n1], kt == 0, kt == KT - 1)
                return last

            def token_major(o, w, j, c0, nw):
                for kt in range(KT):
                    last = mm(o, hT[:, kt, P * j:P * j + P], w[:, kt, c0:c0 + nw], kt == 0, kt == KT - 1)
                return last

            pe.wait_ge(consts_in, 16 * N_CONST_DMAS)
            pe.wait_ge(bias_in, 16)
            pe.wait_ge(silu_done, 2)
            for k in range(4):
                if k >= 2:
                    warm(6 - 2 * k + 2)
                ada_rows(k)
                if k:
                    ada_outs(k - 1)
            ada_outs(3)
            norm_T(0)
            for name in ("u", "zf"):
                w = use(name)
                for m in range(4):
                    t = B.open(f"{name}{m}", "act")
                    B.close(t, feature_major(t, w, P * m, P, 0, SEQ))
                done_with(name)
                if name == "u":
                    w = use("dt")
                    t = B.open("dt", "dve")
                    for j in range(4):
                        last = token_major(t.ps[:, 48 * j:48 * j + 48], w, j, 0, 48)
                    B.close(t, last)
                    done_with("dt")
            pe.wait_ge(arena_in["dft"], 16)
            wait_took(pe, "u3")
            for j in range(2):
                for h in range(2):
                    t = B.open(f"fa{j}{h}", "dve")
                    for q in range(2):
                        last = mm(t.ps[:, 256 * q:256 * q + 256], uT[:, 2 * h + q, P * j:P * j + P], DFT("dft_ch"), True, True)
                    B.close(t, last)
            wait_took(pe, "fa11")
            for h in range(2):
                t = B.open(f"fm{h}", "dve")
                for q in range(2):
                    n = 0
                    for j in range(2):
                        for part, tab in ((0, dft_cos), (1, dft_nsin)):
                            last = mm(t.ps[:, 256 * q:256 * q + 256], dft_a[:, j, 2 * h + q, P * part:P * part + P], tab[:, j, :], n == 0, n == 3)
                            n += 1
                B.close(t, last)
            w = use("w_four")
            wait_took(pe, "fm1")
            wait_took(pe, "zf3")
            for m in range(4):
                t = B.open(f"four{m}", "dve")
                for kt in range(4):
                    last = mm(t.ps[:, 0:SEQ], w[:, kt, P * m:P * m + P], mixedT[:, kt, :], kt == 0, kt == 3)
                B.close(t, last)
            done_with("w_four")

            ada_rows(4)
            ada_rows(5)
            ada_outs(4)
            ada_outs(5)

            def conv_proj(j):
                w = use(f"conv{j // 4}")
                t = B.open(f"conv{j}", "act")
                B.close(t, feature_major(t, w, P * (j % 4), P, 0, TOK if j < 16 else SEQ))
                if j % 4 == 3:
                    done_with(f"conv{j // 4}")

            def conv_T(j):
                if j >= 16:
                    return
                pe.wait_ge(act_conv, j + 1)
                t = B.open(f"ct{j}", "act")
                src = conv_out[j % 2]
                for q in (range(4) if j < 12 else range(2, 4)):
                    last = tr(t.ps[:, P * q:P * q + P], src[:, P * q:P * q + P])
                B.close(t, last)

            pe.wait_ge(a_ready, 1)
            t = B.open("cumT", "dve")
            for d, tab in enumerate((tri_f, tri_b)):
                for q in range(2):
                    last = mm(t.ps[0:24, SEQ * d:SEQ * d + SEQ], a_dt[:, q, 24 * d:24 * d + 24], tab[:, q, :], q == 0, q == 1)
            B.close(t, last)
            t = B.open("cum_col", "dve")
            for j in range(4):
                for d in range(2):
                    up = (d == 0) == (j < 2)
                    tab = tri_f if up else tri_b
                    lt = j % 2
                    qs = [q for q in range(2) if (q <= lt if up else q >= lt)]
                    for q in qs:
                        last = mm(t.ps[:, 48 * j + 24 * d:48 * j + 24 * d + 24], tab[:, q, P * lt:P * lt + P],
                                  a_dt[:, 2 * (j // 2) + q, 24 * d:24 * d + 24], q == qs[0], q == qs[-1])
            B.close(t, last)
            conv_proj(0)
            conv_proj(1)
            for j in range(CONV_TILES):
                if j + 2 < CONV_TILES:
                    conv_proj(j + 2)
                conv_T(j)
            for i in range(3):
                w = use(f"zs{i}")
                for j in range(2):
                    t = B.open(f"zs{i}{j}", "act")
                    B.close(t, token_major(t.ps[:, :], w, j, 0, 512))
                done_with(f"zs{i}")

            pe.wait_ge(act_conv, CONV_TILES)
            for g in range(GROUPS):
                t = B.open(f"cb{g}", "dve")
                for q in range(2):
                    last = mm(t.ps[:, SEQ * q:SEQ * q + SEQ], b_fm[:, g, P * q:P * q + P], c_fm[:, g, :], True, True)
                B.close(t, last)
            wait_took(pe, "ct15")
            for d in range(2):
                pe.wait_ge(xw_done, 2 * (d + 1))
                for g in range(GROUPS):
                    t = B.open(f"hs{d}{g}", "act")
                    for q in range(2):
                        last = mm(t.ps[:, 0:GW], b_tok[:, q, P * g:P * g + P], xw[d][:, q, GW * g:GW * g + GW], q == 0, q == 1)
                    B.close(t, last)
            wait_took(pe, "hs13")
            wait_took(pe, "cumT")

            def head_rows(h):
                t = B.open(f"bc{h}", "dve")
                B.close(t, mm(t.ps[:, :], ident[:, h:h + 1].to_broadcast([P, P]), cumT.rearrange("p a b -> p (a b)"), True, True))

            y_open = {}

            def head_y(h):
                g, c = h // HPG, 64 * (h % HPG)
                if h % HPG == 0:
                    for l in range(2):
                        y_open[l] = B.open(f"y{g}{l}", "dve")
                pe.wait_ge(m_ready, h + 1)
                for l in range(2):
                    for q in range(2):
                        last = mm(y_open[l].ps[:, c:c + 64], m_mat[h % 2][:, q, P * l:P * l + P], xs_tok[:, q, 64 * h:64 * h + 64], q == 0, q == 1)
                    if h % HPG == HPG - 1:
                        B.close(y_open[l], last)
                if h % HPG == HPG - 1:
                    for l in range(2):
                        for d in range(2):
                            t = B.open(f"off{g}{l}{d}", "dve")
                            B.close(t, mm(t.ps[:, 0:GW], c_fm[:, g, P * l:P * l + P], h_init[:, d, GW * g:GW * g + GW], True, True))

            head_rows(0)
            head_rows(1)
            for h in range(HEADS):
                if h + 2 < HEADS:
                    head_rows(h + 2)
                if h in ADA_AT_HEAD:
                    ada_rows(ADA_AT_HEAD[h])
                    if h:
                        ada_outs(ADA_AT_HEAD[h] - 1)
                head_y(h)
            for k in range(ADA_LEFT, 26):
                ada_rows(k)
                ada_outs(k - 1)

            def gated_T(m):
                t = B.open(f"gT{m}", "act" if m % 2 else "dve")
                for l in range(2):
                    last = tr(t.ps[:, P * l:P * l + P], zs[:, l, P * m:P * m + P])
                B.close(t, last)

            for m in range(9):
                pe.wait_ge(gated_done, 2 * (m // 3 + 1))
                gated_T(m)
            wait_took(pe, "four3")

            def project_out(names, src, T, tag):
                ws = [use(name) for name in names]
                for j in range(T):
                    o = [B.open(f"{tag}{j}{n}", "dve") for n in range(2)]
                    for kt in range(4 * len(ws)):
                        for n in range(2):
                            last = mm(o[n].ps[:, :], src[:, kt, P * j:P * j + P], ws[kt // 4][:, kt % 4, 512 * n:512 * n + 512], kt == 0, kt == 4 * len(ws) - 1)
                            if kt == 4 * len(ws) - 1:
                                B.close(o[n], last)
                for name in names:
                    done_with(name)

            def project_block1():
                o = {(j, n): B.open(f"o1_{j}{n}", "dve") for j in range(2) for n in range(2)}

                def products(j, kt, w):
                    for n in range(2):
                        last = mm(o[j, n].ps[:, :], mixT[:, kt, P * j:P * j + P], w[:, kt % 4, 512 * n:512 * n + 512], kt == 0, kt == 15)
                        if kt == 15:
                            B.close(o[j, n], last)
                    return last

                for i in range(4):
                    if i == 2:
                        pe.wait_ge(gated_done, 8)
                        for m in range(9, 12):
                            gated_T(m)
                    w = use(f"w_out{i}")
                    for q in range(4):
                        kt = 4 * i + q
                        if kt >= 4:
                            wait_took(pe, f"gT{kt - 4}")
                        if i < 3:
                            for j in range(2):
                                last = products(j, kt, w)
                    if i == 3:
                        for j in range(2):
                            for q in range(4):
                                products(j, 12 + q, w)
                        done_with("w_out3")
                    else:
                        last.then_inc(part_used, 1)
                        chunk_freed[f"w_out{i}"] = (part_used, i + 1)
                    if i == 1:
                        ada_rows(26)
                        ada_outs(25)

            project_block1()

            for k in range(27, 30):
                ada_rows(k)
                ada_outs(k - 1)
            ada_outs(29)

            norm_T(2)
            pe.wait_ge(arena_in["rope"], 16)

            def rotate(name, m):
                wait_took(pe, f"{name}{m}")
                t = B.open(f"{name}r{m}", "dve")
                B.close(t, mm(t.ps[:, 0:SEQ], ROPE("rope_swap"), rope_raw[m % 2][:, 0:SEQ], True, True))

            QK = [(name, m) for name in "qk" for m in range(4)]
            for i, (name, m) in enumerate(QK):
                if m == 0:
                    w = use(f"even{i // 4}")
                t = B.open(f"{name}{m}", "act")
                B.close(t, feature_major(t, w, P * m, P, 0, TOK))
                if m == 3:
                    done_with(f"even{i // 4}")
                if i:
                    rotate(*QK[i - 1])
            w = use("even2")
            for j in range(4):
                t = B.open(f"v{j}", "act")
                B.close(t, token_major(t.ps[:, :], w, j, 0, 512))
                if j == 0:
                    rotate(*QK[-1])
            done_with("even2")
            for i, name in ((3, "nq"), (4, "nk")):
                w = use(f"even{i}")
                for m in range(4):
                    t = B.open(f"{name}{m}", "act")
                    B.close(t, feature_major(t, w, P * m, P, 0, TOK))
                done_with(f"even{i}")
            w = use("even5")
            for j in range(4):
                t = B.open(f"nv{j}", "act")
                B.close(t, token_major(t.ps[:, :], w, j, 0, 512))
            done_with("even5")
            wait_took(pe, "nv3")
            wait_took(pe, "kr3")

            def d_scores(u):
                j, h = u // 4, u % 4
                n0 = 0 if j < 2 else SEQ
                for c in range(2):
                    t = B.open(f"ds{u}{'ab'[c]}", "act")
                    B.close(t, mm(t.ps[:, n0:TOK], qz[c][:, h, P * j:P * j + P], k_fm[:, h, n0:TOK], True, True))

            def probs_T(tag, u, src, j):
                t = B.open(f"{tag}T{u}", "act")
                for b in range(0 if j < 2 else 2, 4):
                    last = tr(t.ps[:, P * b:P * b + P], src[:, P * b:P * b + P])
                B.close(t, last)

            av_open = {}

            def attend(tag, u, per, width, v, j, h, T2):
                if h == 0:
                    av_open[tag] = B.open(f"{tag}o{j}", "dve")
                t = av_open[tag]
                wait_took(pe, f"{tag}T{u}")
                b0 = 0 if j < 2 else 2
                for b in range(b0, 4):
                    last = mm(t.ps[:, width * h:width * h + width], T2[:, b, :], v[:, b, width * h:width * h + width], b == b0, b == 3)
                if h == per - 1:
                    B.close(t, last)

            def n_scores(u):
                j, h = u // 8, u % 8
                n0 = 0 if j < 2 else SEQ
                t = B.open(f"ns{u}", "dve" if j < 2 else "act")
                B.close(t, mm(t.ps[:, n0:TOK], nqz[h % 2][:, h // 2, P * j:P * j + P], nk_fm[:, h // 2, n0:TOK], True, True))

            def unit_scores(k):
                kind, u = UNITS[k]
                (d_scores if kind == "d" else n_scores)(u)

            def unit_attend(k):
                kind, u = UNITS[k]
                if kind == "d":
                    attend("d", u, 4, P, v_tok, u // 4, u % 4, att_T2[k % 2])
                else:
                    attend("n", u, 8, 64, nv_tok, u // 8, u % 8, att_T2[k % 2])

            for k in range(AHEAD):
                unit_scores(k)
            for k, (kind, u) in enumerate(UNITS):
                if kind == "d":
                    pe.wait_ge(comb_done, u + 1)
                    probs_T("d", u, probs[u % 2][0], u // 4)
                else:
                    if u < 16:
                        pe.wait_ge(na_p, u + 1)
                    else:
                        wait_took(pe, f"ns{u}")
                    probs_T("n", u, na_p_buf[u % 3], u // 8)
                if k + AHEAD < len(UNITS):
                    unit_scores(k + AHEAD)
                if k:
                    unit_attend(k - 1)
            unit_attend(len(UNITS) - 1)
            aT = {}

            def att_T(kt, j0, j1):
                if j0 == 0:
                    aT[kt] = B.open(f"aT{kt}", "dve" if kt < 4 else "act")
                for j in range(j0, j1):
                    last = tr(aT[kt].ps[:, P * j:P * j + P], att[:, j, P * kt:P * kt + P])
                if j1 == 4:
                    B.close(aT[kt], last)

            pe.wait_ge(att_done, 3)
            for kt in range(4):
                att_T(kt, 0, 3)
            pe.wait_ge(att_done, 4)
            for kt in range(4):
                att_T(kt, 3, 4)
            wait_took(pe, "no3")
            for kt in range(4, 8):
                att_T(kt, 0, 4)
            wait_took(pe, "aT3")
            wait_took(pe, "aT7")
            project_out(["even_out0", "even_out1"], attT, 4, "o2_")

            def route(l):
                T = 4 if l == 0 else 2
                norm_T(3 if l == 0 else 5)
                pe.wait_ge(arena_in[f"router{l}"], 16)
                t = B.open(f"rl{l}", "dve")
                for kt in range(KT):
                    g = kt % 4
                    last = mm(t.ps[32 * g:32 * g + 32, 0:P * T], router_sb[:, kt, :], hT[:, kt, 0:P * T], kt < 4, kt >= 4)
                B.close(t, last)
                wait_took(pe, f"rl{l}")
                t = B.open(f"lg{l}", "dve")
                for j in range(T):
                    last = mm(t.ps[:, EXPERTS * j:EXPERTS * j + EXPERTS], lgT[:, P * j:P * j + P], C("sum_e"), True, True)
                B.close(t, last)
                pe.wait_ge(aff_done, l + 1)
                t = B.open(f"affT{l}", "dve")
                for j in range(T):
                    r0 = 32 * (j // 2)
                    last = mm(t.ps[r0:r0 + EXPERTS, P * (j % 2):P * (j % 2) + P], aff[:, j, :], ident, True, True)
                B.close(t, last)
                warm(5)
                pe.wait_ge(topk_done, l + 1)
                t = B.open(f"slotT{l}", "dve")
                for j in range(T):
                    r0 = 32 * (j // 2)
                    n_rows = 16 * T - 16
                    last = mm(t.ps[:, EXPERTS * j:EXPERTS * j + EXPERTS], sel_e[0:n_rows, P * (j % 2):P * (j % 2) + P],
                              ident[0:n_rows, r0:r0 + EXPERTS], True, True)
                B.close(t, last)
                if l == 0:
                    warm(2)
                for s in range(T // 2):
                    pe.wait_ge(d_done, (s + 1 if l == 0 else 3))
                    for kt in range(KT):
                        t = B.open(f"ga{l}.{kt}{s}", "act" if (kt + s) % 2 else "dve")
                        for q in range(2):
                            last = mm(t.ps[:, :], xn[:, 2 * s + q, P * kt:P * kt + P], d_tok[:, 2 * s + q, :], q == 0, q == 1)
                        B.close(t, last)

            def experts(l):
                n_grp = 2 if l == 0 else 4
                S = P // n_grp
                W = FF // n_grp
                J = W // P
                T = 4 if l == 0 else 2
                used, xe = moe_used[l], xe_stg.rearrange("p (g k s) -> p g k s", g=n_grp, k=KT)
                h1, h3, tps, yps, dps = bank[0], bank[1], bank[2], bank[3], bank[4]
                pe.wait_ge(took_sem["dve"], B.ordinal["dve"])
                pe.wait_ge(took_sem["act"], B.ordinal["act"])
                pieces = [slot(moe_slot[l][j], 4, 1024) for j in range(6)]
                hT4 = hidT[:, 0:P * J].rearrange("p (j g s) -> p j g s", j=J, g=n_grp)
                with nc.tensor.Fori(0, EXPERTS // n_grp) as it:
                    for e in range(n_grp):
                        def landed(j):
                            pe.wait_ge(filled[moe_slot[l][j]], it * (16 * n_grp) + 16 * (moe_fill[l][j] + e + 1))
                        pe.wait_ge(xe_staged[l], it * n_grp + (e + 1))
                        for m, ps in ((0, h1), (1, h3)):
                            for half in range(2):
                                landed(2 * m + half)
                                w = pieces[2 * m + half]
                                for q in range(4):
                                    kt = 4 * half + q
                                    for g in range(n_grp):
                                        last = mm(ps[S * g:S * g + S, 0:W], xe[:, e, kt, :], w[:, q, W * g:W * g + W], kt == 0, kt == KT - 1)
                                last.then_inc(used, 1)
                        pe.wait_ge(hid_ready[l], it * n_grp + (e + 1))
                        for j in range(J):
                            last = tr(tps[:, P * j:P * j + P], hid[:, P * j:P * j + P])
                        last.then_inc(hidT_mm[l], 1)
                        pe.wait_ge(hidT_ready[l], it * n_grp + (e + 1))
                        if e:
                            pe.wait_ge(y_ready[l], it * n_grp + e)
                        for half in range(2):
                            landed(4 + half)
                            w = pieces[4 + half]
                            for q in range(4):
                                ft = 4 * half + q
                                for g in range(n_grp):
                                    last = mm(yps[S * g:S * g + S, 0:W], hT4[:, ft % J, ft // J, :], w[:, q, W * g:W * g + W], ft == 0, ft == 7)
                            last.then_inc(used, 1)
                        if e == 0:
                            pe.wait_ge(dstage[l], it + 1)
                            for j in range(T):
                                last = tr(dps[:, P * j:P * j + P], dstg[:, j, :])
                            last.then_inc(dT_mm[l], 1)
                    pe.wait_ge(dgT_ready[l], it + 1)
                    pe.wait_ge(y_ready[l], it * n_grp + n_grp)
                    for i in range(2 * T):
                        if i >= 3:
                            pe.wait_ge(acc_done[l], it * (2 * T) + (i - 2))
                        mm(bank[5 + i % 3][:, :], dgT[:, P * (i // 2):P * (i // 2) + P], y_sb[:, 512 * (i % 2):512 * (i % 2) + 512],
                           True, True).then_inc(scat_mm[l], 1)
                pe.wait_ge(acc_done[l], 2 * T * (EXPERTS // n_grp))

            route(0)
            experts(0)

            norm_T(4)
            w = use("odd_cq")
            for j in range(4):
                t = B.open(f"lat{j}", "dve")
                B.close(t, token_major(t.ps[:, 0:384], w, j, 0, 384) if j < 2 else token_major(t.ps[:, 256:384], w, j, 256, 128))
            t = B.open("krope", "act")
            B.close(t, feature_major(t, w, 384, 32, 0, TOK, p0=64))
            done_with("odd_cq")
            pe.wait_ge(arena_in["odd_tables"], 16)
            w = use("odd_rqk")
            for m in range(2):
                t = B.open(f"rq{m}", "act")
                B.close(t, feature_major(t, w, P * m, P, 0, SEQ))
            for m in range(2):
                t = B.open(f"rk{m}", "act")
                B.close(t, feature_major(t, w, 256 + P * m, P, 0, SEQ))
            for j in range(2):
                t = B.open(f"rkt{j}", "act")
                B.close(t, token_major(t.ps[:, 0:SEQ], w, 2 + j, 256, SEQ))
            done_with("odd_rqk")
            w = use("odd_rv")
            for j in range(4):
                t = B.open(f"rv{j}", "act")
                B.close(t, token_major(t.ps[:, :], w, j, 0, 512))
            done_with("odd_rv")
            w = use("odd_rg")
            for j in range(2):
                t = B.open(f"rg{j}", "act")
                B.close(t, token_major(t.ps[:, :], w, j, 0, 512))
            done_with("odd_rg")
            wait_took(pe, "krope")
            t = B.open("krot", "dve")
            B.close(t, mm(t.ps[64:96, 0:SEQ], ODD("mla_swap")[64:96, 64:96], kr_raw[64:96, 0:SEQ], True, True))
            pe.wait_ge(q_ready, 1)
            for m in range(2):
                t = B.open(f"cqT{m}", "dve")
                for j in range(2):
                    last = tr(t.ps[:, P * j:P * j + P], c_lat[:, j, P * m:P * m + P])
                B.close(t, last)
            t = B.open("ckvT", "dve")
            for j in range(4):
                last = tr(t.ps[:, P * j:P * j + P], c_lat[:, j, 256:384])
            B.close(t, last)
            w = use("w_ukv")
            wait_took(pe, "ckvT")
            for h in range(8):
                t = B.open(f"kn{h}", "act")
                B.close(t, mm(t.ps[0:64, :], w[:, 0, P * h:P * h + 64], ckvT, True, True))
            wv = w[:, 0, :].rearrange("p (h c) -> p h c", c=P)[:, :, 64:128]
            for j in range(4):
                t = B.open(f"mv{j}", "act")
                B.close(t, mm(t.ps[:, :], ckvT[:, P * j:P * j + P], wv, True, True))
            done_with("w_ukv")
            w = use("w_uq")

            def queries(h):
                t = B.open(f"mq{h}", "act")
                for i in range(2):
                    for kt in range(2):
                        last = mm(t.ps[0:96, SEQ * i:SEQ * i + SEQ], w[:, kt, 96 * (h + i):96 * (h + i) + 96], cqT[:, kt, :], kt == 0, kt == 1)
                B.close(t, last)

            queries(0)
            for h in range(0, 8, 2):
                if h < 6:
                    queries(h + 2)
                if h == 4:
                    done_with("w_uq")
                wait_took(pe, f"mq{h}")
                t = B.open(f"mqr{h}", "dve")
                B.close(t, mm(t.ps[0:96, :], ODD("mla_swap")[0:96, 0:96], q_raw[h // 2 % 2][0:96, :], True, True))
            wait_took(pe, "mv3")
            pe.wait_ge(kr_copied, 1)

            def m_scores(u):
                j, h = u // 8, u % 8
                if u < 8 and u % 2 == 0:
                    wait_took(pe, f"mqr{u}")
                t = B.open(f"ms{u}", "act")
                B.close(t, mm(t.ps[:, :], mq[0:96, h, P * j:P * j + P], mk[0:96, h, :], True, True))

            for hp in range(2):
                t = B.open(f"rs{hp}", "act")
                for i in range(2):
                    h = 2 * hp + i
                    for q in range(2):
                        pe.wait_ge(rkw_done, 2 * h + q + 1)
                        last = mm(t.ps[:, SEQ * i:SEQ * i + SEQ], rk_tok[:, q, P * hp:P * hp + P], rvw_all[:, h, q, :], q == 0, q == 1)
                B.close(t, last)
            m_scores(0)
            m_scores(1)
            pe.wait_ge(rq_done, 1)
            wait_took(pe, "rs1")
            ro = [B.open(f"ro{j}", "dve") for j in range(2)]

            def r_scores(h):
                t = B.open(f"rsc{h}", "dve")
                for q in range(2):
                    last = mm(t.ps[:, SEQ * q:SEQ * q + SEQ], rk_fm[:, h // 2, P * q:P * q + P], rqz[:, h, :], True, True)
                B.close(t, last)

            r_scores(0)
            for h in range(4):
                if h + 1 < 4:
                    r_scores(h + 1)
                wait_took(pe, f"rsc{h}")
                for j in range(2):
                    o = ro[j].ps[:, P * h:P * h + P]
                    s3 = ret_s2[h % 2]
                    for q in range(2):
                        mm(o, s3[:, q, P * j:P * j + P], rv_tok[:, q, P * h:P * h + P], q == 0, False)
                    mm(o, rqf[:, h, P * j:P * j + P], ret_state[:, h, 0:P], False, False)
                    last = mm(o, rqb[:, h, P * j:P * j + P], ret_state[:, h, P:2 * P], False, True)
                    if h == 3:
                        B.close(ro[j], last)
            for u in range(16):
                if u + 2 < 16:
                    m_scores(u + 2)
                wait_took(pe, f"ms{u}")
                probs_T("m", u, probs1[u % 3], 0)
                if u:
                    attend("m", u - 1, 8, 64, mv_tok, (u - 1) // 8, (u - 1) % 8, att_T21[(u - 1) % 2])
            attend("m", 15, 8, 64, mv_tok, 1, 7, att_T21[1])
            for kt in BT:
                if kt == 4:
                    pe.wait_ge(att_done, 6)
                if kt == 0:
                    wait_took(pe, "mo1")
                t = B.open(f"bT{kt}", "dve" if kt % 2 else "act")
                for j in range(2):
                    last = tr(t.ps[:, P * j:P * j + P], att1[:, j, P * kt:P * kt + P])
                B.close(t, last)
            wait_took(pe, "bT3")
            wait_took(pe, "bT2")
            project_out(["odd_out0", "odd_out1"], attT1, 2, "o3_")
            route(1)
            experts(1)
        @block.vector
        def _(dve):
            V = nc.vector

            def settle():
                dve.drain()

            def scaled(o, i, s1, s2, op0, op1):
                return V.tensor_scalar(o, i, s1, s2, op0, op1)

            def pow_wait(name):
                dve.wait_ge(rstd_done, POW.index(name) + 1)

            def ada_rows(k):
                ps = arrive(dve, f"row{k}")
                took(f"row{k}", V.tensor_copy(ada_row[k % 2], ps[:, :]))

            def ada_outs(k):
                kind, v, half = ada_kind(k)
                s = ADA[k][0]
                l = s - 1
                ps = arrive(dve, f"col{k}")
                if kind == "col":
                    tiled = lambda a: a.rearrange("p (j i) -> p j i", i=2)
                    took(f"col{k}", V.tensor_tensor(tiled(ada_col[s][:, v, 8 * half:8 * half + 8]), tiled(ps[:, 0:8]),
                                                    G("ada_bias")[:, 4 * COL_STEPS.index(k):4 * COL_STEPS.index(k) + 4].unsqueeze(2).to_broadcast([P, 4, 2]), ALU.add))
                elif kind == "ffn":
                    w = 512 if l == 0 else 256
                    took(f"col{k}", V.tensor_copy(gate_ffn[l][64 * half:64 * half + 64, :], ps[64 * half:64 * half + 64, 0:w]))
                else:
                    dst = gate_1 if s == 0 else gate_mix[l][:, 0, :]
                    took(f"col{k}", V.tensor_copy(dst[:, 512 * half:512 * half + 512], ps[:, :]))
                    if kind == "mix" and l == 0:
                        ps = arrive(dve, f"col{k}c")
                        took(f"col{k}c", V.tensor_copy(gate_mix[l][:, 1, 512 * half:512 * half + 512], ps[:, :]))

            def gains(n):
                s, v = NORM_B[n]
                gain = {0: G("norm_w"), 2: G("norm_mix")[:, 0:8], 3: G("norm_ffn")[:, 0:8], 4: G("norm_mix")[:, 8:16], 5: G("norm_ffn")[:, 8:16]}[n]
                sc = ada_col[s][:, v + 1, :].rearrange("p (k i) -> p k i", i=2)
                o = norm_a[:, NORM_A[n], :].rearrange("p (k i) -> p k i", i=2)
                return V.scalar_tensor_tensor(out=o, in0=sc, scalar=1.0, in1=gain.unsqueeze(2).to_broadcast([P, KT, 2]), op0=ALU.add, op1=ALU.mult)

            def mean_squares(n):
                T = NORM_TILES[n]
                dve.wait_ge(sums_done, NORM_SUM[n])
                scaled(meansq[:, 0:T], ssq[:, 0:T], 1.0 / D, EPS, ALU.mult, ALU.add).then_inc(ms_done, 1)
                pow_wait(f"norm{n}")

            def norm_rows(n):
                mean_squares(n)
                for j in range(2 if n in (2, 4) else NORM_TILES[n]):
                    V.tensor_scalar(xn[:, j, :], xres[:, j, :], rstd[:, j:j + 1], None, ALU.mult).then_inc(xn_done, 1)

            def modulate(n, name, kt, o, T=None):
                ps = arrive(dve, name)
                s, v = NORM_B[n]
                for i in range((NORM_TILES[n] if T is None else T) // 2):
                    last = scaled(o[:, kt, SEQ * i:SEQ * i + SEQ], ps[:, SEQ * i:SEQ * i + SEQ], norm_a[:, NORM_A[n], 2 * kt + i:2 * kt + i + 1],
                                  ada_col[s][:, v, 2 * kt + i:2 * kt + i + 1], ALU.mult, ALU.add)
                took(name, last)

            def norm_T(n):
                for kt in range(0, KT, 2):
                    modulate(n, f"nT{n}.{kt}", kt, hT)

            dve.wait_ge(consts_in, 16 * N_CONST_DMAS)
            lam_p = R("diff_lambda")
            for i in range(2):
                V.tensor_tensor_reduce(y_t[i][:, 0:64], lam_p[:, 128 * i:128 * i + 64], lam_p[:, 128 * i + 64:128 * i + 128], 1.0, 0.0,
                                       ALU.mult, ALU.add, lam_b[:, i:i + 1]).then_inc(lam_sum, 1)
            for k in range(4):
                ada_rows(k)
                if k:
                    ada_outs(k - 1)
                if k == 2:
                    norm_rows(0)
            ada_outs(3)
            settle()
            gains(0).then_inc(gain0_done, 1)
            dve.wait_ge(lam_exp, 1)
            V.tensor_tensor(lam_b[:, 0:1], lam_b[:, 3:4], lam_b[:, 2:3], ALU.subtract)
            settle()
            V.tensor_scalar(lam_b[:, 0:1], lam_b[:, 0:1], -LAM_INIT, None, ALU.add)
            norm_T(0)
            ps = arrive(dve, "dt")
            took("dt", V.tensor_tensor(dt_z, ps[:, 0:192].rearrange("p (a b) -> p a b", b=48), R("dt_bias").unsqueeze(1).to_broadcast([P, 4, 48]), ALU.add))
            settle()
            V.scalar_tensor_tensor(out=dt_a, in0=dt_z, scalar=-1.0, in1=dt_z, op0=ALU.mult, op1=ALU.max).then_inc(dt_abs, 1)
            dve.wait_ge(dt_log, 1)
            V.scalar_tensor_tensor(out=dt_v, in0=dt_z, scalar=0.0, in1=dt_a, op0=ALU.max, op1=ALU.add)
            settle()
            dve.wait_ge(a_exp, 1)
            V.scalar_tensor_tensor(out=a_dt, in0=dt_v, scalar=-1.0, in1=exp_alog.unsqueeze(1).to_broadcast([P, 4, 48]), op0=ALU.mult, op1=ALU.mult).then_inc(a_ready, 1)
            for j in range(2):
                for h in range(2):
                    ps = arrive(dve, f"fa{j}{h}")
                    took(f"fa{j}{h}", V.tensor_copy(dft_a[:, j, 2 * h:2 * h + 2, :], ps.rearrange("p (a b) -> p a b", b=256)))
            for h in range(2):
                ps = arrive(dve, f"fm{h}")
                took(f"fm{h}", V.tensor_copy(mixedT[:, 2 * h:2 * h + 2, :], ps.rearrange("p (a b) -> p a b", b=SEQ)))
            for m in range(4):
                ps = arrive(dve, f"four{m}")
                took(f"four{m}", V.scalar_tensor_tensor(out=mixT[:, m, :], in0=ps[:, 0:SEQ], scalar=G("b_four")[:, m:m + 1], in1=zfT[:, m, :],
                                                        op0=ALU.add, op1=ALU.mult))
            ada_rows(4)
            ada_rows(5)
            ada_outs(4)
            ada_outs(5)
            ps = arrive(dve, "cumT")
            dve.wait_ge(pool_zero, 3)
            took("cumT", V.tensor_copy(cumT[0:24], ps[0:24, :].rearrange("p (a b) -> p a b", b=SEQ)))
            ps = arrive(dve, "cum_col")
            took("cum_col", V.tensor_copy(cum_col, ps[:, 0:192].rearrange("p (a b) -> p a b", b=48)))
            settle()
            V.tensor_tensor(dt_z[:, 0:2, :], cum_col[:, 2:4, :], a_dt[:, 2:4, :], ALU.subtract).then_inc(ctx_arg, 1)
            dve.wait_ge(ctx_exp, 1)
            V.tensor_tensor(w_ctx, dt_z[:, 0:2, :], dt_v[:, 2:4, :], ALU.mult).then_inc(ctx_w, 1)
            for j in range(CONV_TILES):
                wait_took(dve, f"conv{j}")
                if j >= 2:
                    dve.wait_ge(act_conv, j - 1)
                w = G("conv_w")[:, 9 * j:9 * j + 9]
                acc = conv_acc[j % 2]
                xa, ca = acc[:, 0:SEQ].rearrange("p (r c) -> p r c", c=GRID_W), acc[:, SEQ:TOK]
                xp, cp = xpad[j % 2], cpad[j % 2]
                for tap in range(9):
                    dr, dc = tap // 3, tap % 3
                    src = xp[:, dr:dr + ROWS, dc:dc + GRID_W]
                    ctx_tap = 3 + tap if tap < 3 and j < 16 else None
                    if tap == 0:
                        last = V.tensor_scalar(xa, src, w[:, 0:1], None, ALU.mult)
                        if ctx_tap is not None:
                            V.tensor_scalar(ca, cp[:, 0:SEQ], w[:, 3:4], None, ALU.mult)
                    else:
                        settle()
                        if ctx_tap is not None:
                            V.scalar_tensor_tensor(out=ca, in0=cp[:, tap:tap + SEQ], scalar=w[:, 3 + tap:4 + tap], in1=ca, op0=ALU.mult, op1=ALU.add)
                        last = V.scalar_tensor_tensor(out=xa, in0=src, scalar=w[:, tap:tap + 1], in1=xa, op0=ALU.mult, op1=ALU.add)
                last.then_inc(conv_done, 1)
            for g in range(GROUPS):
                ps = arrive(dve, f"cb{g}")
                for q in range(2):
                    lo, hi = (0, SEQ) if q == 0 else (P, SEQ)
                    V.tensor_tensor(cb[:, g, q, 0:hi - lo], ps[:, SEQ * q + lo:SEQ * q + hi], tri_f[:, q, lo:hi], ALU.mult)
                    at = hi - lo
                    lo, hi = (0, P) if q == 0 else (0, SEQ)
                    last = V.tensor_tensor(cb[:, g, q, at:384], ps[:, SEQ * q + lo:SEQ * q + hi], tri_b[:, q, lo:hi], ALU.mult)
                took(f"cb{g}", last)

            def decay_args(h):
                ps = arrive(dve, f"bc{h}")
                d = dec_arg[h % 2]
                f0, f1 = cum_col[:, 0, h:h + 1], cum_col[:, 1, h:h + 1]
                b0, b1 = cum_col[:, 0, 24 + h:25 + h], cum_col[:, 1, 24 + h:25 + h]
                scaled(d[:, 0, 0:256], ps[:, 0:256], f0, 0.0, ALU.subtract, ALU.min)
                scaled(d[:, 0, 256:384], ps[:, 256:384], b0, 0.0, ALU.subtract, ALU.min)
                scaled(d[:, 1, 0:128], ps[:, 128:256], f1, 0.0, ALU.subtract, ALU.min)
                took(f"bc{h}", scaled(d[:, 1, 128:384], ps[:, 256:512], b1, 0.0, ALU.subtract, ALU.min))

            def mixing(h):
                dve.wait_ge(decay_out, h + 1)
                e, m, g = dec_exp[h % 2], m_mat[h % 2], h // HPG
                stt = lambda o, i, s, c: V.scalar_tensor_tensor(out=o, in0=i, scalar=s, in1=c, op0=ALU.mult, op1=ALU.mult)
                stt(m[:, 0, :], e[:, 0, 0:256], dt_v[:, 0, h:h + 1], cb[:, g, 0, 0:256])
                stt(m[:, 1, :], e[:, 1, 128:384], dt_v[:, 1, 24 + h:25 + h], cb[:, g, 1, 128:384])
                stt(e[:, 0, 256:384], e[:, 0, 256:384], dt_v[:, 0, 24 + h:25 + h], cb[:, g, 0, 256:384])
                stt(e[:, 1, 0:128], e[:, 1, 0:128], dt_v[:, 1, h:h + 1], cb[:, g, 1, 0:128])
                settle()
                V.tensor_tensor(m[:, 0, 0:128], m[:, 0, 0:128], e[:, 0, 256:384], ALU.add)
                V.tensor_tensor(m[:, 1, 128:256], m[:, 1, 128:256], e[:, 1, 0:128], ALU.add).then_inc(m_ready, 1)

            by_head = lambda a: a.rearrange("p (h c) -> p h c", c=64)

            def group_out(g):
                if g == 0:
                    dve.wait_ge(x_ecum, 1)
                dve.wait_ge(y_skip, g + 1)
                for l in range(2):
                    ps = arrive(dve, f"y{g}{l}")
                    took(f"y{g}{l}", V.tensor_tensor(y_acc[l], ps[:, 0:GW], y_acc[l], ALU.add))
                for l in range(2):
                    for d in range(2):
                        ps = arrive(dve, f"off{g}{l}{d}")
                        took(f"off{g}{l}{d}", V.tensor_tensor(by_head(off_t[l][d]), by_head(ps[:, 0:GW]),
                             x_dec[:, l, 24 * d + HPG * g:24 * d + HPG * g + HPG].unsqueeze(2).to_broadcast([P, HPG, 64]), ALU.mult))

            decay_args(0)
            decay_args(1)
            for h in range(HEADS):
                mixing(h)
                if h + 2 < HEADS:
                    decay_args(h + 2)
                if h in ADA_AT_HEAD and h:
                    ada_outs(ADA_AT_HEAD[h] - 1)
                if h % HPG == HPG - 1:
                    group_out(h // HPG)
            for k in range(ADA_LEFT, 26):
                ada_rows(k)
                ada_outs(k - 1)
            settle()
            for n in (2, 3, 4):
                gains(n)
            for m in range(0, 12, 2):
                if m == 10:
                    ada_rows(26)
                    ada_outs(25)
                ps = arrive(dve, f"gT{m}")
                took(f"gT{m}", V.tensor_scalar(mixT[:, 4 + m, :], ps[:, 0:SEQ], G("ssd_norm")[:, m:m + 1], None, ALU.mult))

            def residual(tag, T, gate, n=None):
                for i in range(2 * T):
                    j, half = i // 2, i % 2
                    cs = slice(512 * half, 512 * half + 512)
                    ps = arrive(dve, f"{tag}{j}{half}")
                    took(f"{tag}{j}{half}", V.tensor_tensor(res_t[i % 4], ps[:, :], gate(j)[:, cs], ALU.mult))
                    settle()
                    V.tensor_tensor(xres[:, j, cs], xres[:, j, cs], res_t[i % 4], ALU.add).then_inc(res_done, 1)
                    if half and n is not None:
                        dve.wait_ge(sums_done, NORM_SUM[n - 1] + j + 1)
                        scaled(meansq[:, j:j + 1], ssq[:, j:j + 1], 1.0 / D, EPS, ALU.mult, ALU.add).then_inc(ms_done, 1)
                        pow_wait(f"norm{n}.{j}")
                        if n == 1:
                            dve.wait_ge(arena_in["gain1"], 16)
                            V.scalar_tensor_tensor(out=xres[:, j, :], in0=xres[:, j, :], scalar=rstd[:, j:j + 1], in1=gain_1,
                                                   op0=ALU.mult, op1=ALU.mult).then_inc(xn_done, 1)
                        else:
                            V.tensor_scalar(xn[:, j, :], xres[:, j, :], rstd[:, j:j + 1], None, ALU.mult).then_inc(xn_done, 1)

            residual("o1_", 2, lambda j: gate_1, 1)
            for k in range(27, 30):
                ada_rows(k)
                ada_outs(k - 1)
                if k == 28:
                    norm_rows(2)
            ada_outs(29)
            settle()
            gains(5)

            norm_T(2)
            dve.wait_ge(arena_in["rope"], 16)
            dve.wait_ge(pool_zero, 4)
            for i in range(8):
                name, m = "qk"[i // 4], i % 4
                ps = arrive(dve, f"{name}r{m}")
                raw, t = rope_raw[m % 2][:, 0:SEQ], rope_t[m % 2]
                V.tensor_tensor(t, ps[:, 0:SEQ], ROPE("rope_sin"), ALU.mult)
                V.tensor_tensor(raw, raw, ROPE("rope_cos"), ALU.mult)
                settle()
                if name == "q":
                    V.tensor_tensor(qz[0][0:64, m, 0:SEQ], raw[0:64], t[0:64], ALU.add)
                    last = V.tensor_tensor(qz[1][64:128, m, 0:SEQ], raw[64:128], t[64:128], ALU.add)
                else:
                    last = V.tensor_tensor(k_fm[:, m, 0:SEQ], raw, t, ALU.add)
                took(f"{name}r{m}", last)
                settle()

            def d_max(u):
                n0 = 0 if u < 8 else SEQ
                for c in range(2):
                    i = 2 * (u % 2) + c
                    ps = arrive(dve, f"ds{u}{'ab'[c]}")
                    V.tensor_reduce(a_mx[:, i:i + 1], ps[:, n0:TOK], AX, ALU.max)
                    settle()
                    V.tensor_scalar(a_neg[:, i:i + 1], a_mx[:, i:i + 1], -NA_SCALE, None, ALU.mult).then_inc(neg_max, 1)

            def combine(u):
                n0 = 0 if u < 8 else SEQ
                wait_took(dve, f"ds{u}b")
                i = 2 * (u % 2)
                p0, p1 = probs[u % 2][0][:, n0:TOK], probs[u % 2][1][:, n0:TOK]
                V.reciprocal(a_rec[:, i:i + 2], a_sum[:, i:i + 2])
                settle()
                scaled(p1, p1, a_rec[:, i + 1:i + 2], lam_b[:, 0:1], ALU.mult, ALU.mult)
                settle()
                V.scalar_tensor_tensor(out=p0, in0=p0, scalar=a_rec[:, i:i + 1], in1=p1, op0=ALU.mult, op1=ALU.add).then_inc(comb_done, 1)

            def d_out(j):
                ps = arrive(dve, f"do{j}")
                took(f"do{j}", V.tensor_copy(att[:, j, 0:512], ps[:, :]))
                if j == 3:
                    settle()
                    V.tensor_tensor(sq_t, att[:, j, 0:512], att[:, j, 0:512], ALU.mult)
                    settle()
                    V.tensor_reduce(d_ss[:, 12:16], sq_t.rearrange("p (h c) -> p h c", c=P), AX, ALU.add)
                    settle()

            def n_max(u):
                j, h = u // 8, u % 8
                ps = arrive(dve, f"ns{u}")
                i = u % 3
                if j < 2:
                    s = na_p_buf[i]
                    V.scalar_tensor_tensor(out=s[:, 0:SEQ], in0=ps[:, 0:SEQ], scalar=NA_SCALE, in1=na_bias[:, h, P - P * j:P - P * j + SEQ], op0=ALU.mult, op1=ALU.add)
                    took(f"ns{u}", V.tensor_scalar(s[:, SEQ:TOK], ps[:, SEQ:TOK], NA_SCALE, None, ALU.mult))
                    settle()
                    V.tensor_reduce(n_mx[:, i:i + 1], s, AX, ALU.max)
                else:
                    V.tensor_reduce(n_mx[:, i:i + 1], ps[:, SEQ:TOK], AX, ALU.max)
                settle()
                V.tensor_scalar(n_neg[:, i:i + 1], n_mx[:, i:i + 1], -1.0 if j < 2 else -NA_SCALE, None, ALU.mult).then_inc(na_neg, 1)

            def head_norm(name, j, o):
                ps = arrive(dve, name)
                i = 8 * (j % 2)
                V.reciprocal(n_rec[:, i:i + 8], n_sum[:, i:i + 8])
                settle()
                took(name, V.tensor_tensor(by_head(o), by_head(ps[:, :]), n_rec[:, i:i + 8].unsqueeze(2).to_broadcast([P, 8, 64]), ALU.mult))

            def d_roots(j0, j1):
                cs = slice(4 * j0, 4 * j1)
                scaled(d_ms[:, cs], d_ss[:, cs], 1.0 / P, EPS, ALU.mult, ALU.add).then_inc(ms_done, 1)

            def d_norm(j):
                o = att[:, j, 0:512].rearrange("p (h c) -> p h c", c=P)
                V.tensor_tensor(o, o, d_ss[:, 4 * j:4 * j + 4].unsqueeze(2).to_broadcast([P, 4, P]), ALU.mult).then_inc(att_done, 1)

            def unit_max(k):
                kind, u = UNITS[k]
                (d_max if kind == "d" else n_max)(u)

            wait_took(dve, "nv3")
            d_max(0)
            dve.wait_ge(na_masked, 1)
            for k in range(1, AHEAD):
                unit_max(k)
                if k == 1:
                    combine(0)
            for k in range(len(UNITS)):
                j = k // per_tile
                if k % per_tile == per_tile - 1:
                    d_out(j)
                    if j == 3:
                        d_roots(3, 4)
                if k % per_tile == 1 and j:
                    head_norm(f"no{j - 1}", j - 1, att[:, j - 1, 512:1024])
                if k + AHEAD < len(UNITS):
                    unit_max(k + AHEAD)
                if k + 2 < len(UNITS) and UNITS[k + 2][0] == "d":
                    combine(UNITS[k + 2][1])
                if j == 3 and k % per_tile in (4, 6, 8):
                    if k % per_tile == 4:
                        dve.wait_ge(d_squared, 3)
                        d_roots(0, 3)
                        pow_wait("diff_a")
                    d_norm(k % per_tile // 2 - 2)
            pow_wait("diff_b")
            d_norm(3)
            head_norm("no3", 3, att[:, 3, 512:1024])
            for kt in range(4):
                ps = arrive(dve, f"aT{kt}")
                took(f"aT{kt}", scaled(attT[:, kt, :], ps[:, :], G("subln")[:, 0:1], 1.0 - LAM_INIT, ALU.mult, ALU.mult))
            lg, lgt = small[:, 0:8], small[:, 8:16]
            V.scalar_tensor_tensor(out=lgt, in0=R("ret_decay"), scalar=-1.0, in1=R("ret_decay"), op0=ALU.mult, op1=ALU.max).then_inc(lg_abs, 1)
            dve.wait_ge(lg_ln, 1)
            V.scalar_tensor_tensor(out=lg, in0=R("ret_decay"), scalar=0.0, in1=lgt, op0=ALU.min, op1=ALU.subtract).then_inc(lg_done, 1)
            residual("o2_", 4, lambda j: gate_mix[0][:, j // 2, :], 3)

            def route(l):
                n, T = (3, 4) if l == 0 else (5, 2)
                norm_T(n)
                three = lambda a: a[:, 0:T, :]
                ps = arrive(dve, f"rl{l}")
                took(f"rl{l}", V.tensor_copy(lgT[:, 0:P * T], ps[:, 0:P * T]))
                ps = arrive(dve, f"lg{l}")
                lg = ps[:, 0:EXPERTS * T].rearrange("p (a b) -> p a b", b=EXPERTS)
                V.tensor_reduce(rt_mx[:, 0:T, 0], lg, AX, ALU.max)
                settle()
                took(f"lg{l}", V.tensor_tensor(three(rt_t), lg, rt_mx[:, 0:T, :].to_broadcast([P, T, EXPERTS]), ALU.subtract))
                dve.wait_ge(rt_exp, l + 1)
                V.tensor_reduce(rt_sum[:, 0:T, 0], three(aff), AX, ALU.add)
                settle()
                V.reciprocal(rt_mx[:, 0:T, :], rt_sum[:, 0:T, :])
                settle()
                V.tensor_tensor(three(aff), three(aff), rt_mx[:, 0:T, :].to_broadcast([P, T, EXPERTS]), ALU.mult).then_inc(aff_done, 1)
                ps = arrive(dve, f"affT{l}")
                n_rows = 16 * T - 16
                if l == 0:
                    for r0 in (0, 32):
                        last = V.tensor_copy(aff_work[r0:r0 + EXPERTS, :], ps[r0:r0 + EXPERTS, 0:SEQ])
                else:
                    last = V.tensor_copy(aff_work[0:EXPERTS, :], ps[0:EXPERTS, 0:SEQ])
                took(f"affT{l}", last)
                wk, sel = aff_work[0:n_rows, :], sel_e[0:n_rows, :]
                for i in range(CAP // 8):
                    settle()
                    V.max(top8[i][0:n_rows, :], wk)
                    settle()
                    V.match_replace(wk, top8[i][0:n_rows, :], wk, -1.0)
                settle()
                V.tensor_scalar(sel, wk, 0.0, None, ALU.is_lt)
                settle()
                V.tensor_tensor_scan(wk, sel, sel, 0.0, ALU.add, ALU.max)
                settle()
                V.tensor_tensor(sel, sel, wk, ALU.mult).then_inc(topk_done, 1)
                ps = arrive(dve, f"slotT{l}")
                took(f"slotT{l}", V.tensor_copy(three(slot_t), ps[:, 0:EXPERTS * T].rearrange("p (a b) -> p a b", b=EXPERTS)))
                settle()
                grid = [P, EXPERTS, CAP]
                cube = lambda a: a.rearrange("p (e s) -> p e s", s=CAP)
                for j in range(T):
                    last = V.tensor_tensor(cube(d_tok[:, j, :]), C("iota").unsqueeze(1).to_broadcast(grid), slot_t[:, j, :].unsqueeze(2).to_broadcast(grid), ALU.is_equal)
                    if j % 2:
                        last.then_inc(d_done, 1)
                for s in range(T // 2):
                    for kt in range(KT):
                        if (kt + s) % 2 == 0:
                            name = f"ga{l}.{kt}{s}"
                            ps = arrive(dve, name)
                            took(name, gathered(V, l, kt, s, ps))
                settle()
                for s in range(T // 2):
                    wait_took(dve, f"ga{l}.{7 - s}{s}")
                S = CAP * T // 2
                for half, src in ((0, xe_lo), (1, xe_hi)):
                    last = V.tensor_copy(xe_stg.rearrange("p (g k s) -> p g k s", g=P // S, k=KT)[:, 0, 4 * half:4 * half + 4, :], src[:, :, 0:S])
                last.then_inc(xe_staged[l], 1)
                for j in range(T):
                    last = V.tensor_tensor(cube(d_tok[:, j, :]), cube(d_tok[:, j, :]), aff[:, j, :].unsqueeze(2).to_broadcast(grid), ALU.mult)
                last.then_inc(gates_done, 1)

            def gathered(V, l, kt, s, ps):
                n = 3 if l == 0 else 5
                sh, v = NORM_B[n]
                return scaled(xe_rows(l, kt, s), ps.rearrange("p (e s) -> p e s", s=CAP), norm_a[:, NORM_A[n], 2 * kt + s:2 * kt + s + 1],
                              ada_col[sh][:, v, 2 * kt + s:2 * kt + s + 1], ALU.mult, ALU.add)

            def experts(l):
                n_grp = 2 if l == 0 else 4
                S, W, T = P // n_grp, FF // n_grp, 4 if l == 0 else 2
                with nc.vector.Fori(0, EXPERTS // n_grp) as it:
                    for e in range(n_grp):
                        dve.wait_ge(silu_ready[l], it * n_grp + (e + 1))
                        dve.wait_ge(moe_used[l], it * (6 * n_grp) + (6 * e + 4))
                        V.tensor_tensor(hid[:, 0:W], silu_h[:, 0:W], bank[1][:, 0:W], ALU.mult).then_inc(hid_ready[l], 1)
                        dve.wait_ge(moe_used[l], it * (6 * n_grp) + (6 * e + 6))
                        for g in range(n_grp):
                            last = V.tensor_tensor(y_sb[S * e:S * e + S, W * g:W * g + W], bank[3][S * g:S * g + S, 0:W],
                                                   gate_ffn[l][S * g:S * g + S, :], ALU.mult)
                        last.then_inc(y_ready[l], 1)
                    for i in range(2 * T):
                        dve.wait_ge(scat_mm[l], it * (2 * T) + (i + 1))
                        x = xres[:, i // 2, 512 * (i % 2):512 * (i % 2) + 512]
                        V.tensor_tensor(x, x, bank[5 + i % 3][:, :], ALU.add).then_inc(acc_done[l], 1)

            route(0)
            experts(0)

            settle()
            norm_rows(4)
            norm_T(4)
            lat_ss, lat_ms = small[:, 64:72], small[:, 80:88]
            for j in range(4):
                ps = arrive(dve, f"lat{j}")
                c0 = 0 if j < 2 else 256
                took(f"lat{j}", V.tensor_copy(c_lat[:, j, c0:384], ps[:, c0:384]))
                settle()
                if j < 2:
                    V.tensor_tensor_reduce(probs1[0][:, 0:256], c_lat[:, j, 0:256], c_lat[:, j, 0:256], 1.0, 0.0, ALU.mult, ALU.add, lat_ss[:, j:j + 1])
                V.tensor_tensor_reduce(probs1[1][:, 0:128], c_lat[:, j, 256:384], c_lat[:, j, 256:384], 1.0, 0.0, ALU.mult, ALU.add, lat_ss[:, 2 + j:3 + j])
                settle()
            scaled(lat_ms[:, 0:2], lat_ss[:, 0:2], 1.0 / 256, EPS, ALU.mult, ALU.add)
            scaled(lat_ms[:, 2:6], lat_ss[:, 2:6], 1.0 / 128, EPS, ALU.mult, ALU.add).then_inc(ms_done, 1)
            pow_wait("lat")
            for j in range(2):
                V.tensor_scalar(c_lat[:, j, 0:256], c_lat[:, j, 0:256], lat_ss[:, j:j + 1], None, ALU.mult)
            for j in range(4):
                last = V.tensor_scalar(c_lat[:, j, 256:384], c_lat[:, j, 256:384], lat_ss[:, 2 + j:3 + j], None, ALU.mult)
            last.then_inc(q_ready, 1)
            dve.wait_ge(arena_in["odd_tables"], 16)
            for h in range(4):
                V.tensor_scalar(ret_d[:, h, :], ODD("ret_bwd"), lg[:, 4 + h:5 + h], None, ALU.mult)
                settle()
                V.scalar_tensor_tensor(out=ret_d[:, h, :], in0=ODD("ret_fwd"), scalar=lg[:, h:h + 1], in1=ret_d[:, h, :], op0=ALU.mult, op1=ALU.add).then_inc(ret_arg, 1)
            ps = arrive(dve, "krot")
            t = probs1[0][64:96, 0:SEQ]
            kx = kr_raw[64:96, 0:SEQ]
            V.tensor_tensor(t, ps[64:96, 0:SEQ], ODD("mla_sin")[64:96], ALU.mult)
            V.tensor_tensor(kx, kx, ODD("mla_cos")[64:96], ALU.mult)
            settle()
            took("krot", V.tensor_tensor(kx, kx, t, ALU.add))
            for m in range(2):
                ps = arrive(dve, f"cqT{m}")
                took(f"cqT{m}", V.tensor_scalar(cqT[:, m, :], ps[:, 0:SEQ], G("q_norm")[:, m:m + 1], None, ALU.mult))
            ps = arrive(dve, "ckvT")
            took("ckvT", V.tensor_scalar(ckvT, ps[:, :], G("kv_norm")[:, 0:1], None, ALU.mult))
            def m_max(u):
                i = u % 3
                ps = arrive(dve, f"ms{u}")
                V.tensor_reduce(m_mx[:, i:i + 1], ps[:, :], AX, ALU.max)
                settle()
                V.tensor_scalar(m_ng[:, i:i + 1], m_mx[:, i:i + 1], -MLA_SCALE, None, ALU.mult).then_inc(m_neg, 1)

            def m_norm(name, j):
                ps = arrive(dve, name)
                V.reciprocal(m_rec[:, 8 * j:8 * j + 8], m_sum[:, 8 * j:8 * j + 8])
                settle()
                took(name, V.tensor_tensor(by_head(att1[:, j, 0:512]), by_head(ps[:, :]), m_rec[:, 8 * j:8 * j + 8].unsqueeze(2).to_broadcast([P, 8, 64]), ALU.mult))

            def retention_inputs():
                dve.wait_ge(ret_qdec, 8)
                ages = small[:, 24:40].rearrange("p (h d q) -> p h d q", d=2, q=2)
                wait_took(dve, "rv3")
                dve.wait_ge(mm_done, tiles["rg1"].no)
                for h in range(4):
                    for q in range(2):
                        for d in range(2):
                            last = scaled(rvw_all[:, h, q, P * d:P * d + P], rv_tok[:, 2 + q, P * h:P * h + P], ages[:, h, d, q:q + 1], 0.125, ALU.mult, ALU.mult)
                        last.then_inc(rkw_done, 1)
                for h in range(4):
                    V.tensor_tensor(rqf[:, h, :], rqf[:, h, :], rqz[:, h, :], ALU.mult)
                    last = V.tensor_tensor(rqb[:, h, :], rqb[:, h, :], rqz[:, h, :], ALU.mult)
                last.then_inc(rq_done, 1)

            retention_inputs()
            two = lambda a: a.rearrange("p (h c) -> p h c", c=SEQ)
            for h in range(0, 8, 2):
                ps = arrive(dve, f"mqr{h}")
                tab = lambda n: ODD(n)[0:96].unsqueeze(1).to_broadcast([96, 2, SEQ])
                t, raw = q_rot[h // 2 % 2][0:96], q_raw[h // 2 % 2][0:96]
                V.tensor_tensor(two(t), two(ps[0:96, :]), tab("mla_sin"), ALU.mult)
                V.tensor_tensor(two(raw), two(raw), tab("mla_cos"), ALU.mult)
                settle()
                took(f"mqr{h}", V.tensor_tensor(mq[0:96, h:h + 2, :], two(raw), two(t), ALU.add))
            m_max(0)
            m_max(1)
            dve.wait_ge(ret_tab, 4)
            for h in range(4):
                ps = arrive(dve, f"rsc{h}")
                took(f"rsc{h}", V.scalar_tensor_tensor(out=ret_s2[h % 2].rearrange("p a b -> p (a b)"), in0=ps[:, :], scalar=0.125, in1=ret_d[:, h, :], op0=ALU.mult, op1=ALU.mult))
            for j in range(2):
                ps = arrive(dve, f"ro{j}")
                took(f"ro{j}", V.tensor_copy(att1[:, j, 512:1024], ps[:, :]))

            def retention_norm(step):
                settle()
                for j in range(2):
                    o = att1[:, j, 512:1024]
                    by_h = lambda a: a.rearrange("p (h c) -> p h c", c=P)
                    if step == 0:
                        V.tensor_tensor(ret_sq[:, j, :], o, o, ALU.mult)
                    elif step == 1:
                        V.tensor_reduce(lat_ss[:, 4 * j:4 * j + 4], by_h(ret_sq[:, j, :]), AX, ALU.add)
                    elif step == 3:
                        V.tensor_tensor(by_h(o), by_h(o), lat_ss[:, 4 * j:4 * j + 4].unsqueeze(2).to_broadcast([P, 4, P]), ALU.mult)
                    elif step == 4:
                        V.tensor_tensor(o, o, rg_tok[:, j, :], ALU.mult).then_inc(att_done, 1)
                if step == 2:
                    scaled(lat_ms, lat_ss, 1.0 / P, EPS, ALU.mult, ALU.add).then_inc(ms_done, 1)

            for u in range(16):
                if u + 2 < 16:
                    if u >= 1:
                        wait_took(dve, f"ms{u - 1}")
                    if u == 9:
                        m_norm("mo0", 0)
                    m_max(u + 2)
                if u in (1, 2, 3, 5, 6):
                    if u == 5:
                        pow_wait("ret")
                        wait_took(dve, "rg1")
                    retention_norm((1, 2, 3, 5, 6).index(u))
            m_norm("mo1", 1)
            for kt in BT[1::2]:
                ps = arrive(dve, f"bT{kt}")
                took(f"bT{kt}", V.tensor_copy(attT1[:, kt, :], ps[:, 0:SEQ]))
            residual("o3_", 2, lambda j: gate_mix[1][:, 0, :], 5)
            route(1)
            experts(1)
            settle()
            mean_squares(6)
            dve.wait_ge(arena_in["gain2"], 16)
            for j in range(2):
                V.scalar_tensor_tensor(out=xres[:, j, :], in0=xres[:, j, :], scalar=rstd[:, j:j + 1], in1=gate_1, op0=ALU.mult, op1=ALU.mult).then_inc(out_ready, 1)

        @block.scalar
        def _(act):
            S = nc.scalar

            def copy(o, i):
                return S.activation(o, i, ACT.Copy)

            def settle():
                act.drain()

            act.wait_ge(consts_in, 16 * N_CONST_DMAS)
            act.wait_ge(silu_pad, 2)
            for s, name in enumerate(("cvec1", "cvec2")):
                S.activation(silu_c[s][:, :, 0:2], G(name).rearrange("p (k i) -> p k i", i=2), ACT.Silu).then_inc(silu_done, 1)
            S.activation(exp_alog, R("a_log"), ACT.Exp).then_inc(a_exp, 1)
            act.wait_ge(lam_sum, 2)
            S.activation(lam_b[:, 2:4], lam_b[:, 0:2], ACT.Exp).then_inc(lam_exp, 1)

            def squares(n, done=None, before=0):
                for j in (2, 3, 0, 1) if n == 2 else range(NORM_TILES[n]):
                    if n == 2 and j < 2:
                        act.wait_ge(xn_done, NORM_SUM[0] + j + 1)
                    if done is not None:
                        act.wait_ge(done, before + 2 * j + 2)
                    junk = j
                    if n in (4, 6):
                        junk = 1 + j % 2 * 2
                        if j >= 2:
                            settle()
                    S.activation(xn[:, junk, :], xres[:, j, :], ACT.Square, accum_out=ssq[:, j:j + 1]).then_inc(sums_done, 1)

            def other_rows(n):
                act.wait_ge(rstd_done, POW.index(f"norm{n}") + 1)
                for j in range(2, 4):
                    S.activation(xn[:, j, :], xres[:, j, :], ACT.Identity, scale=rstd[:, j:j + 1]).then_inc(xn_done, 1)

            def norm_T(n):
                sh, v = NORM_B[n]
                for kt in range(1, KT, 2):
                    ps = arrive(act, f"nT{n}.{kt}")
                    for i in range(NORM_TILES[n] // 2):
                        last = S.activation(hT[:, kt, SEQ * i:SEQ * i + SEQ], ps[:, SEQ * i:SEQ * i + SEQ], ACT.Identity,
                                            scale=norm_a[:, NORM_A[n], 2 * kt + i:2 * kt + i + 1], bias=ada_col[sh][:, v, 2 * kt + i:2 * kt + i + 1])
                    took(f"nT{n}.{kt}", last)

            def take(name, o, i, func=ACT.Copy):
                took(name, S.activation(o, i, func))

            act.wait_ge(x_in, 16)
            act.wait_ge(ctx_in, 16)
            squares(0)
            act.wait_ge(gain0_done, 1)
            norm_T(0)
            for m in range(4):
                take(f"u{m}", uT[:, m, :], arrive(act, f"u{m}")[:, 0:SEQ])
            act.wait_ge(dt_abs, 1)
            S.activation(dt_a, dt_a, ACT.Exp, scale=-1.0)
            settle()
            S.activation(dt_a, dt_a, ACT.Ln, bias=1.0).then_inc(dt_log, 1)
            for m in range(4):
                take(f"zf{m}", zfT[:, m, :], arrive(act, f"zf{m}")[:, 0:SEQ], ACT.Silu)

            wait_took(act, "cum_col")
            S.activation(x_dec, cum_col[:, 0:2, :], ACT.Exp).then_inc(x_ecum, 1)
            act.wait_ge(ctx_arg, 1)
            S.activation(dt_z[:, 0:2, :], dt_z[:, 0:2, :], ACT.Exp).then_inc(ctx_exp, 1)
            act.wait_ge(pool_zero, 2)

            def pad(j):
                ps = arrive(act, f"conv{j}")
                if j >= 2:
                    act.wait_ge(conv_done, j - 1)
                last = copy(xpad[j % 2][:, 1:1 + ROWS, 1:1 + GRID_W], ps[:, 0:SEQ].rearrange("p (r c) -> p r c", c=GRID_W))
                if j < 16:
                    last = copy(cpad[j % 2][:, 1:1 + SEQ], ps[:, SEQ:TOK])
                took(f"conv{j}", last)

            pad(0)
            pad(1)
            for j in range(CONV_TILES):
                act.wait_ge(conv_done, j + 1)
                acc, b = conv_acc[j % 2], G("conv_b")[:, j:j + 1]
                if 2 <= j < 18:
                    act.wait_ge(mm_done, tiles[f"ct{j - 2}"].no)
                if j < 12:
                    S.activation(conv_out[j % 2], acc, ACT.Silu, bias=b).then_inc(act_conv, 1)
                elif j < 16:
                    S.activation(b_fm[:, j - 12, :], acc[:, 0:SEQ], ACT.Silu, bias=b)
                    S.activation(conv_out[j % 2][:, SEQ:TOK], acc[:, SEQ:TOK], ACT.Silu, bias=b).then_inc(act_conv, 1)
                else:
                    S.activation(c_fm[:, j - 16, :], acc[:, 0:SEQ], ACT.Silu, bias=b).then_inc(act_conv, 1)
                if j + 2 < CONV_TILES:
                    pad(j + 2)
                if j < 16:
                    ps = arrive(act, f"ct{j}").rearrange("p (t c) -> p t c", c=P)
                    if j < 12:
                        take(f"ct{j}", xs_tok[:, :, P * j:P * j + P], ps)
                    else:
                        take(f"ct{j}", b_tok[:, :, P * (j - 12):P * (j - 12) + P], ps[:, 2:4, :])
            for i in range(3):
                for j in range(2):
                    take(f"zs{i}{j}", zs[:, j, 512 * i:512 * i + 512], arrive(act, f"zs{i}{j}")[:, :], ACT.Silu)
            for d in range(2):
                for g in range(GROUPS):
                    take(f"hs{d}{g}", h_init[:, d, GW * g:GW * g + GW], arrive(act, f"hs{d}{g}")[:, 0:GW])

            def gated_squares(g):
                act.wait_ge(ssd_z, g + 1)
                for l in range(2):
                    settle()
                    S.activation(sq_junk, zs[:, l, GW * g:GW * g + GW], ACT.Square, accum_out=ssq8[:, 4 * l + g:4 * l + g + 1]).then_inc(ssd_sq, 1)

            for h in range(HEADS):
                wait_took(act, f"bc{h}")
                S.activation(dec_exp[h % 2], dec_arg[h % 2], ACT.Exp).then_inc(decay_out, 1)
                if h in ADA_AT_HEAD:
                    k = ADA_AT_HEAD[h]
                    take(f"row{k}", ada_row[k % 2], arrive(act, f"row{k}")[:, :])
                if h >= HPG and h % HPG == 2:
                    gated_squares(h // HPG - 1)
            gated_squares(GROUPS - 1)
            for m in range(1, 12, 2):
                ps = arrive(act, f"gT{m}")
                took(f"gT{m}", S.activation(mixT[:, 4 + m, :], ps[:, 0:SEQ], ACT.Copy, scale=G("ssd_norm")[:, m:m + 1]))
            squares(1, res_done)

            act.wait_ge(ctx2_in, 16)
            squares(2)
            other_rows(2)
            norm_T(2)
            act.wait_ge(pool_zero, 4)
            for i in range(8):
                name, m = "qk"[i // 4], i % 4
                ps = arrive(act, f"{name}{m}")
                if i >= 2:
                    prev = "qk"[(i - 2) // 4] + f"r{(i - 2) % 4}"
                    wait_took(act, prev)
                if name == "q":
                    copy(qz[0][0:64, m, SEQ:TOK], ps[0:64, SEQ:TOK])
                    copy(qz[1][64:128, m, SEQ:TOK], ps[64:128, SEQ:TOK])
                else:
                    copy(k_fm[:, m, SEQ:TOK], ps[:, SEQ:TOK])
                take(f"{name}{m}", rope_raw[m % 2][:, 0:SEQ], ps[:, 0:SEQ])
            for j in range(4):
                take(f"v{j}", v_tok[:, j, :], arrive(act, f"v{j}")[:, :])
            for m in range(4):
                ps = arrive(act, f"nq{m}")
                copy(nqz[0][0:64, m, :], ps[0:64, :])
                take(f"nq{m}", nqz[1][64:128, m, :], ps[64:128, :])
            for m in range(4):
                take(f"nk{m}", nk_fm[:, m, :], arrive(act, f"nk{m}")[:, :])
            for j in range(4):
                take(f"nv{j}", nv_tok[:, j, :], arrive(act, f"nv{j}")[:, :])
            wait_took(act, "kr3")

            def d_exp(u):
                n0 = 0 if u < 8 else SEQ
                for c in range(2):
                    i = 2 * (u % 2) + c
                    name = f"ds{u}{'ab'[c]}"
                    act.wait_ge(neg_max, 2 * u + c + 1)
                    ps = tiles[name].ps
                    took(name, S.activation(probs[u % 2][c][:, n0:TOK], ps[:, n0:TOK], ACT.Exp, bias=a_neg[:, i:i + 1], scale=NA_SCALE, accum_out=a_sum[:, i:i + 1]))

            def probs_T(tag, u, T2, x):
                ps = arrive(act, f"{tag}T{u}").rearrange("p (b q) -> p b q", q=P)
                b0 = 0 if x else 2
                take(f"{tag}T{u}", T2[:, b0:4, :], ps[:, b0:4, :])

            def n_exp(u):
                j, h, i = u // 8, u % 8, u % 3
                act.wait_ge(na_neg, u + 1)
                s, total = na_p_buf[i], n_sum[:, 8 * (j % 2) + h:8 * (j % 2) + h + 1]
                if j < 2:
                    S.activation(s, s, ACT.Exp, bias=n_neg[:, i:i + 1], accum_out=total).then_inc(na_p, 1)
                else:
                    ps = tiles[f"ns{u}"].ps
                    took(f"ns{u}", S.activation(s[:, SEQ:TOK], ps[:, SEQ:TOK], ACT.Exp, bias=n_neg[:, i:i + 1], scale=NA_SCALE, accum_out=total))

            def unit_exp(k):
                kind, u = UNITS[k]
                (d_exp if kind == "d" else n_exp)(u)

            for k in range(AHEAD):
                unit_exp(k)
            for k, (kind, u) in enumerate(UNITS):
                probs_T(kind, u, att_T2[k % 2], k < len(UNITS) // 2)
                if k + AHEAD < len(UNITS):
                    unit_exp(k + AHEAD)
                j = k // per_tile - 1
                if k % per_tile == 0 and j >= 0:
                    wait_took(act, f"do{j}")
                    for h in range(4):
                        last = S.activation(sq_t[:, P * h:P * h + P], att[:, j, P * h:P * h + P], ACT.Square, accum_out=d_ss[:, 4 * j + h:4 * j + h + 1])
                    last.then_inc(d_squared, 1)
            for kt in range(4, 8):
                take(f"aT{kt}", attT[:, kt, :], arrive(act, f"aT{kt}")[:, :])

            act.wait_ge(lg_abs, 1)
            lg, lgt = small[:, 0:8], small[:, 8:16]
            S.activation(lgt, lgt, ACT.Exp, scale=-1.0)
            settle()
            S.activation(lgt, lgt, ACT.Ln, bias=1.0).then_inc(lg_ln, 1)

            def route(l):
                n, T = (3, 4) if l == 0 else (5, 2)
                squares(n, res_done, 4 if l == 0 else 12)
                norm_T(n)
                wait_took(act, f"lg{l}")
                S.activation(aff[:, 0:T, :], rt_t[:, 0:T, :], ACT.Exp).then_inc(rt_exp, 1)
                sh, v = NORM_B[n]
                for s in range(T // 2):
                    for kt in range(KT):
                        if (kt + s) % 2:
                            name = f"ga{l}.{kt}{s}"
                            ps = arrive(act, name)
                            took(name, S.activation(xe_rows(l, kt, s), ps.rearrange("p (e s) -> p e s", s=CAP), ACT.Identity,
                                                    scale=norm_a[:, NORM_A[n], 2 * kt + s:2 * kt + s + 1], bias=ada_col[sh][:, v, 2 * kt + s:2 * kt + s + 1]))

            def experts(l):
                n_grp = 2 if l == 0 else 4
                W, T = FF // n_grp, 4 if l == 0 else 2
                with nc.scalar.Fori(0, EXPERTS // n_grp) as it:
                    for e in range(n_grp):
                        act.wait_ge(moe_used[l], it * (6 * n_grp) + (6 * e + 2))
                        S.activation(silu_h[:, 0:W], bank[0][:, 0:W], ACT.Silu).then_inc(silu_ready[l], 1)
                        act.wait_ge(hidT_mm[l], it * n_grp + (e + 1))
                        copy(hidT[:, 0:W], bank[2][:, 0:W]).then_inc(hidT_ready[l], 1)
                        if e == 0:
                            act.wait_ge(dT_mm[l], it + 1)
                            copy(dgT[:, 0:P * T], bank[4][:, 0:P * T]).then_inc(dgT_ready[l], 1)

            route(0)
            experts(0)

            squares(4, acc_done[0], 2 * 4 * (EXPERTS // 2 - 1))
            other_rows(4)
            norm_T(4)
            take("krope", kr_raw[64:96, :], arrive(act, "krope")[64:96, :])
            act.wait_ge(pool_zero, 5)
            for m in range(2):
                ps = arrive(act, f"rq{m}")
                copy(rqz[0:64, 2 * m, :], ps[0:64, 0:SEQ])
                take(f"rq{m}", rqz[64:128, 2 * m + 1, :], ps[64:128, 0:SEQ])
            for m in range(2):
                take(f"rk{m}", rk_fm[:, m, :], arrive(act, f"rk{m}")[:, 0:SEQ])
            for j in range(2):
                take(f"rkt{j}", rk_tok[:, j, :], arrive(act, f"rkt{j}")[:, 0:SEQ])
            for j in range(4):
                take(f"rv{j}", rv_tok[:, j, :], arrive(act, f"rv{j}")[:, :])
            for j in range(2):
                take(f"rg{j}", rg_tok[:, j, :], arrive(act, f"rg{j}")[:, :], ACT.Silu)
            act.wait_ge(lg_done, 1)
            act.wait_ge(arena_in["odd_tables"], 16)
            ret_q = ODD("ret_q").rearrange("p (d i) -> p d i", i=SEQ)
            age = C("ret_age").rearrange("p (d q) -> p d q", q=2)
            ages = small[:, 24:40].rearrange("p (h d q) -> p h d q", d=2, q=2)
            for h in range(4):
                for d, o in ((0, rqf), (1, rqb)):
                    rate = lg[:, 4 * d + h:4 * d + h + 1]
                    S.activation(ages[:, h, d, :], age[:, d, :], ACT.Exp, scale=rate)
                    S.activation(o[:, h, :], ret_q[:, d, :], ACT.Exp, scale=rate).then_inc(ret_qdec, 1)
            for h in range(4):
                act.wait_ge(ret_arg, h + 1)
                S.activation(ret_d[:, h, :], ret_d[:, h, :], ACT.Exp).then_inc(ret_tab, 1)
            for h in range(8):
                take(f"kn{h}", mk[0:64, h, :], arrive(act, f"kn{h}")[0:64, :])
            for j in range(4):
                take(f"mv{j}", mv_tok[:, j, :], arrive(act, f"mv{j}")[:, :])
            for h in range(0, 8, 2):
                ps = arrive(act, f"mq{h}")
                if h >= 4:
                    wait_took(act, f"mqr{h - 4}")
                take(f"mq{h}", q_raw[h // 2 % 2][0:96, :], ps[0:96, :])

            def m_exp(u):
                j, h, i = u // 8, u % 8, u % 3
                act.wait_ge(m_neg, u + 1)
                ps = tiles[f"ms{u}"].ps
                if u < 3:
                    wait_took(act, "mqr6")
                took(f"ms{u}", S.activation(probs1[i], ps[:, :], ACT.Exp, bias=m_ng[:, i:i + 1], scale=MLA_SCALE, accum_out=m_sum[:, u:u + 1]))

            for hp in range(2):
                take(f"rs{hp}", ret_state[:, 2 * hp:2 * hp + 2, :], arrive(act, f"rs{hp}").rearrange("p (h c) -> p h c", c=SEQ))
            m_exp(0)
            m_exp(1)
            for u in range(16):
                if u + 2 < 16:
                    m_exp(u + 2)
                probs_T("m", u, att_T21[u % 2], True)
            for kt in BT[0::2]:
                take(f"bT{kt}", attT1[:, kt, :], arrive(act, f"bT{kt}")[:, 0:SEQ])
            route(1)
            experts(1)
            squares(6, acc_done[1], 2 * 2 * (EXPERTS // 4 - 1))

        @block.gpsimd
        def _(pool):
            Q = nc.gpsimd

            def roots(name, o, i):
                pool.wait_ge(ms_done, POW.index(name) + 1)
                n = i.shape[1]
                Q.tensor_tensor(o, i, neg_half[:, 0:n], ALU.pow).then_inc(rstd_done, 1)

            def norm_roots(n):
                roots(f"norm{n}", rstd[:, 0:NORM_TILES[n]], meansq[:, 0:NORM_TILES[n]])

            def tile_roots(n):
                for j in range(NORM_TILES[n]):
                    roots(f"norm{n}.{j}", rstd[:, j:j + 1], meansq[:, j:j + 1])

            Q.memset(neg_half, -0.5)
            Q.memset(ada_bias, 0.0).then_inc(pool_zero, 1)
            for s in range(2):
                Q.memset(silu_c[s], 0.0).then_inc(silu_pad, 1)
            Q.memset(mem[:, conv0:conv0 + 2 * (396 + 258)], 0.0).then_inc(pool_zero, 1)
            Q.memset(cumT, 0.0).then_inc(pool_zero, 1)
            norm_roots(0)
            pool.dma_start(dft, A["dft_tab"]).then_inc(arena_in["dft"], 16)
            pool.wait_ge(ctx_w, 1)
            wait_took(pool, "ct15")
            wait_took(pool, "four3")
            for d in range(2):
                if d:
                    pool.wait_ge(mm_done, tiles["zs21"].no)
                for q in range(2):
                    Q.tensor_tensor(xw[d][:, q, :].rearrange("p (h c) -> p h c", c=64), xs_tok[:, 2 + q, :].rearrange("p (h c) -> p h c", c=64),
                                    w_ctx[:, q, 24 * d:24 * d + 24].unsqueeze(2).to_broadcast([P, HEADS, 64]), ALU.mult).then_inc(xw_done, 1)
            pool.wait_ge(mm_done, tiles["hs13"].no)
            pool.wait_ge(consts_in, 16 * N_CONST_DMAS)
            for g in range(GROUPS):
                z = [zs[:, l, GW * g:GW * g + GW] for l in range(2)]
                for l in range(2):
                    last = Q.tensor_tensor(y_acc[l].rearrange("p (h c) -> p h c", c=64), xs_tok[:, l, GW * g:GW * g + GW].rearrange("p (h c) -> p h c", c=64),
                                           R("d_skip")[:, HPG * g:HPG * g + HPG].unsqueeze(2).to_broadcast([P, HPG, 64]), ALU.mult)
                last.then_inc(y_skip, 1)
                wait_took(pool, f"off{g}11")
                for d in range(2):
                    for l in range(2):
                        Q.tensor_tensor(y_acc[l], y_acc[l], off_t[l][d], ALU.add)
                    pool.drain()
                for l in range(2):
                    last = Q.tensor_tensor(z[l], y_acc[l], z[l], ALU.mult)
                last.then_inc(ssd_z, 1)
                pool.wait_ge(ssd_sq, 2 * g + 2)
                by_tile = lambda a: a.rearrange("p (l g) -> p l g", g=GROUPS)[:, :, g]
                Q.tensor_scalar(by_tile(ms8), by_tile(ssq8), 1.0 / GW, EPS, ALU.mult, ALU.add)
                pool.drain()
                Q.tensor_tensor(by_tile(rstd8), by_tile(ms8), neg_half[:, 0:2], ALU.pow)
                pool.drain()
                for l in range(2):
                    Q.tensor_scalar(z[l], z[l], rstd8[:, 4 * l + g:4 * l + g + 1], None, ALU.mult).then_inc(gated_done, 1)
            pool.dma_start(gain_1, A["final_norm_w"].unsqueeze(0).to_broadcast([P, D])).then_inc(arena_in["gain1"], 16)
            pool.dma_start(xres[:, 2:4, :], A["ctx_2"][0].rearrange("(t p) d -> p t d", p=P)).then_inc(ctx2_in, 16)
            pool.dma_start(rope, A["rope_tab"]).then_inc(arena_in["rope"], 16)
            for b in (*qz, *nqz):
                last = Q.memset(b, 0.0)
            last.then_inc(pool_zero, 1)
            tile_roots(1)
            pool.wait_ge(res_done, 4)
            pool.dma_start(gate_1, A["final_norm_2"].unsqueeze(0).to_broadcast([P, D])).then_inc(arena_in["gain2"], 16)
            def load_router(l):
                pool.dma_start(router_sb[:, :, 0:EXPERTS], A["moe_router"][l].rearrange("(k p) e -> p k e", p=P)).then_inc(arena_in[f"router{l}"], 16)

            norm_roots(2)
            pool.wait_ge(mm_done, tiles["row29"].no)
            Q.memset(router_sb, 0.0).then_inc(router_pad, 1)
            pool.wait_ge(router_pad, 1)
            load_router(0)
            pool.wait_ge(mm_done, tiles["nT2.7"].no)
            pool.dma_start(na_bias.rearrange("p h n -> p (h n)"), A["na_bias"]).then_inc(arena_in["na_bias"], 16)
            pool.wait_ge(arena_in["na_bias"], 16)
            nb = na_bias.rearrange("p h (m c) -> p (h m) c", c=GRID_W)
            Q.tensor_tensor(nb, nb, C("na_mask").unsqueeze(1).to_broadcast([P, 48, GRID_W]), ALU.add).then_inc(na_masked, 1)
            roots("diff_a", d_ss[:, 0:12], d_ms[:, 0:12])
            roots("diff_b", d_ss[:, 12:16], d_ms[:, 12:16])

            def experts(l):
                T, n_grp = (4, 2) if l == 0 else (2, 4)
                S = P // n_grp
                steps = EXPERTS // n_grp
                xe = xe_stg.rearrange("p (g k s) -> p g k s", g=n_grp, k=KT)
                last_gather = [f"ga{l}.7{s}" for s in range(T // 2)] + [f"ga{l}.6{s}" for s in range(T // 2)]
                for name in last_gather:
                    wait_took(pool, name)
                if l == 0:
                    Q.memset(dstg, 0.0).then_inc(moe_bufs_zero, 1)
                    pool.wait_ge(moe_bufs_zero, 1)

                def stage_rows(e, at):
                    for half, src in ((0, xe_lo), (1, xe_hi)):
                        last = Q.tensor_copy(xe[:, e, 4 * half:4 * half + 4, :], src[:, :, at])
                    last.then_inc(xe_staged[l], 1)

                def stage_gates(at):
                    if l == 0:
                        d4 = dstg.rearrange("p t (g s) -> p t g s", g=n_grp)
                        for s in range(2):
                            last = Q.tensor_copy(d4[:, 2 * s:2 * s + 2, :, CAP * s:CAP * s + CAP],
                                                 d_tok[:, 2 * s:2 * s + 2, at].rearrange("p t (g s) -> p t g s", s=CAP))
                    else:
                        last = Q.tensor_copy(dstg[:, 0:2, :], d_tok[:, 0:2, at])
                    last.then_inc(dstage[l], 1)

                pool.wait_ge(xe_staged[l], 1)
                for e in range(1, n_grp):
                    stage_rows(e, slice(S * e, S * e + S))
                pool.wait_ge(gates_done, l + 1)
                stage_gates(slice(0, n_grp * CAP))
                with nc.gpsimd.Fori(0, steps - 1) as it:
                    for e in range(n_grp):
                        pool.wait_ge(moe_used[l], it * (6 * n_grp) + (6 * e + 4))
                        stage_rows(e, bass.ds(it * P + (P + S * e), S))
                        if e == 0:
                            pool.wait_ge(dT_mm[l], it + 1)
                            stage_gates(bass.ds(it * (n_grp * CAP) + n_grp * CAP, n_grp * CAP))

            tile_roots(3)
            pool.wait_ge(mm_done, tiles["rl0"].no)
            load_router(1)
            experts(0)
            pool.wait_ge(acc_done[0], 2 * 4 * (EXPERTS // 2))
            pool.dma_start(odd_c, A["odd_tab"]).then_inc(arena_in["odd_tables"], 16)
            norm_roots(4)
            pool.wait_ge(xn_done, NORM_SUM[4])
            Q.memset(rqz, 0.0).then_inc(pool_zero, 1)
            roots("lat", small[:, 64:70], small[:, 80:86])
            wait_took(pool, "krot")
            Q.tensor_copy(mk[64:96, :, :], kr_raw[64:96, :].unsqueeze(1).to_broadcast([32, 8, TOK])).then_inc(kr_copied, 1)
            roots("ret", small[:, 64:72], small[:, 80:88])
            tile_roots(5)
            experts(1)
            norm_roots(6)

        @block.sync
        def _(sp):
            def load_x(name, t0, s):
                sp.dma_start(xres[:, t0:t0 + 2, :], A[name][0].rearrange("(t p) d -> p t d", p=P)).then_inc(s, 16)

            sp.dma_start(cbuf, A["const_tab"]).then_inc(consts_in, 16)
            sp.dma_start(par, A["par"]).then_inc(consts_in, 16)
            sp.dma_start(rowp, A["rowp"].unsqueeze(0).to_broadcast([P, N_ROWP])).then_inc(consts_in, 16)
            sp.wait_ge(pool_zero, 1)
            sp.dma_start(ada_bias[0:len(ROW_STEPS), :], A["ada_bias"]).then_inc(bias_in, 16)
            order = [n for n, _ in chunks]
            last_in_slot = [None] * 6

            def load(name):
                s = place[name]
                prev = last_in_slot[s]
                if prev is not None:
                    sem_, v = prev
                    sp.wait_ge(sem_, v)
                src = dict(chunks)[name]
                sp.dma_start(slot(s, src.shape[1], src.shape[2]), src).then_inc(filled[s], 16)
                last_in_slot[s] = chunk_freed[name]

            def load_experts(l):
                w = (A["moe_w1"][l], A["moe_w3"][l], A["moe_w2"][l])

                def piece(j, e):
                    s = moe_slot[l][j]
                    src = w[j // 2][e, 512 * (j % 2):512 * (j % 2) + 512, :].rearrange("(k p) f -> p k f", p=P) if isinstance(e, int) else \
                        w[j // 2][bass.ds(e, 1), 512 * (j % 2):512 * (j % 2) + 512, :].rearrange("o (k p) f -> p (o k) f", p=P)
                    sp.dma_start(slot(s, 4, 1024), src).then_inc(filled[s], 16)

                for j in (0, 3, 4, 1, 2, 5):
                    s = moe_slot[l][j]
                    if j < 3:
                        sem_, v = last_in_slot[s]
                        sp.wait_ge(sem_, v)
                    elif j < 5:
                        sp.wait_ge(mm_done, tiles["aT0" if l == 0 else "bT0"].no)
                    else:
                        sp.wait_ge(mm_done, tiles["o2_31" if l == 0 else "bT0"].no)
                    piece(j, 0)
                with nc.sync.Fori(1, EXPERTS) as e:
                    for j in range(6):
                        sp.wait_ge(moe_used[l], e * 6 + (j - 5))
                        piece(j, e)
                for j in range(6):
                    last_in_slot[moe_slot[l][j]] = (moe_used[l], 6 * (EXPERTS - 1) + j + 1)

            for name in order[:2]:
                load(name)
            load_x("x", 0, x_in)
            load_x("ctx", 2, ctx_in)
            for name in order[2:N_PRE0]:
                load(name)
            load_experts(0)
            for name in order[N_PRE0:]:
                load(name)
            load_experts(1)
            for j in range(2):
                sp.wait_ge(out_ready, j + 1)
                sp.dma_start(out[0, P * j:P * j + P, :], xres[:, j, :]).then_inc(out_stored, 16)
            sp.wait_ge(out_stored, 32)


WEIGHTS = ["x", "ctx", "ctx_2", "w_ada", "w_in", "w_fourier", "w_out", "ada_w", "even_w_in", "even_w_out", "moe_w1", "moe_w3", "moe_w2",
           "moe_router", "odd_w_in", "odd_w_out", "mla_w_uq", "mla_w_ukv", "final_norm_w", "final_norm_2"]


def laid_out(i):
    f = {k: np.asarray(v) for k, v in i.items()}
    col = lambda a: np.ascontiguousarray(a.reshape(-1, P).T)
    pair = lambda a, b: np.stack([col(a), col(b)], 2).reshape(P, 16)
    ada_b = np.concatenate([f["b_ada"].reshape(6, 512), f["ada_b_2"].reshape(24, 512)], 0)
    parts = {
        "cvec1": pair(f["c"][0], f["c_ctx"]), "cvec2": pair(f["c_2"][0], f["c_ctx_2"]), "norm_w": col(f["norm_w"][0]),
        "conv_w": f["conv_w"][0].reshape(9, CONV_TILES, P).transpose(2, 1, 0).reshape(P, 180), "conv_b": col(f["conv_b"][0]),
        "ssd_norm": col(f["ssd_norm_w"][0]), "b_four": col(f["b_fourier"][0]), "norm_mix": col(f["norm_mix_2"].reshape(-1)),
        "norm_ffn": col(f["norm_ffn_2"].reshape(-1)), "subln": col(f["diff_subln_2"][0]), "q_norm": col(f["mla_q_norm_2"][0]),
        "kv_norm": col(f["mla_kv_norm_2"][0]), "ada_bias": col(ada_b[COL_STEPS]),
    }
    o = {"par": np.concatenate([parts[n] for n in PAR], 1)}
    rows_ = {"dt_bias": f["dt_bias"], "a_log": f["a_log"], "d_skip": f["d_skip"], "diff_lambda": f["diff_lambda_2"], "ret_decay": f["ret_decay_logit_2"]}
    o["rowp"] = np.concatenate([rows_[n].reshape(-1) for n in ROWP])
    o["ada_bias"] = ada_b[ROW_STEPS]
    par_, c, m, k = np.meshgrid(np.arange(2), np.arange(GRID_W), np.arange(6), np.arange(GRID_W), indexing="ij")
    dr, dc = m + 5 - par_, k - c + 15
    ok = (dc >= 0) & (dc < 31)
    padded = np.pad(f["na_rpb_2"][0], ((0, 0), (0, 0), (0, 1)))
    o["na_bias"] = np.ascontiguousarray(padded[:, dr, np.where(ok, dc, 31)].transpose(1, 2, 0, 3, 4).reshape(P, 8 * 384))
    names = {"ada_w": "ada_w_2", "even_w_in": "even_w_in_2", "even_w_out": "even_w_out_2", "moe_w1": "moe_w1_2", "moe_w3": "moe_w3_2",
             "moe_w2": "moe_w2_2", "moe_router": "moe_router_2", "odd_w_in": "odd_w_in_2", "odd_w_out": "odd_w_out_2",
             "mla_w_uq": "mla_w_uq_2", "mla_w_ukv": "mla_w_ukv_2"}
    for n in WEIGHTS:
        a = f[names.get(n, n)]
        o[n] = np.ascontiguousarray(a[0] if n in ("w_ada", "w_in", "w_fourier", "w_out") else a)
    for n, (tab, _) in zip(("const_tab", "dft_tab", "rope_tab", "odd_tab"), CONSTS):
        o[n] = tab
    return o


def kernel(**inputs):
    import concourse.bacc as bacc
    from concourse.bass_utils import run_bass_kernel_spmd

    arrays = {f"in_{n}": a for n, a in laid_out(inputs).items()}
    nc = bacc.Bacc("TRN2", target_bir_lowering=False, num_devices=1)
    A = {n[3:]: nc.dram_tensor(n, a.shape, mybir.dt.from_np(a.dtype), kind="ExternalInput").ap() for n, a in arrays.items()}
    out = nc.dram_tensor("out", (1, SEQ, D), F32, kind="ExternalOutput").ap()
    build(nc, A, out)
    return run_bass_kernel_spmd(nc, [arrays], core_ids=[0]).results[0]["out"]
```
